# Optimizing a Trainium2 kernel written in Bass

```python
import math
import jax, jax.numpy as jnp
from jax import lax
import numpy as np

D_MODEL = 1024
BATCH = 1
SEQ = 256
DEPTH = 4

CHUNK = 64
QBLOCK = 128
ROPE_THETA = 10000.0
NORM_EPS = 1e-6
N_MIXERS = 3

A_HEADS = 8
A_QK_DIM = 64
A_V_DIM = 2 * A_QK_DIM
A_WIDTH = A_HEADS * A_V_DIM
A_QK_WIDTH = A_HEADS * 2 * A_QK_DIM
A_IN = 2 * A_QK_WIDTH + A_WIDTH + A_WIDTH

B_WIDTH = D_MODEL
B_CONV = 31
B_IN = 3 * B_WIDTH

C_HEADS = 8
C_NOPE = 128
C_ROPE = 64
C_QK = C_NOPE + C_ROPE
C_V = 128
C_Q_LORA = 256
C_KV_LORA = 128
C_WIDTH = C_HEADS * C_V
C_IN = C_Q_LORA + C_KV_LORA + C_ROPE + C_WIDTH

N_A = (DEPTH + 2) // 3
N_B = (DEPTH + 1) // 3
N_C = DEPTH // 3


def _rms_norm(x, g):
    xf = x.astype(jnp.float32)
    y = xf * lax.rsqrt(jnp.mean(xf * xf, axis=-1, keepdims=True) + NORM_EPS)
    return (y * g.astype(jnp.float32)).astype(x.dtype)

def _layer_norm(x, g, b):
    xf = x.astype(jnp.float32)
    mu = jnp.mean(xf, axis=-1, keepdims=True)
    xc = xf - mu
    y = xc * lax.rsqrt(jnp.mean(xc * xc, axis=-1, keepdims=True) + NORM_EPS)
    return (y * g.astype(jnp.float32) + b.astype(jnp.float32)).astype(x.dtype)

def _rope_cos_sin(seq, dim):
    inv = 1.0 / (ROPE_THETA ** (jnp.arange(0, dim, 2, dtype=jnp.float32) / dim))
    ang = jnp.arange(seq, dtype=jnp.float32)[:, None] * inv[None, :]
    return jnp.cos(ang), jnp.sin(ang)

def _apply_rope(x, cos, sin):
    xf = x.astype(jnp.float32)
    x1, x2 = jnp.split(xf, 2, axis=-1)
    return jnp.concatenate([x1 * cos - x2 * sin, x2 * cos + x1 * sin], axis=-1).astype(x.dtype)

def _chunk_causal_softmax(s, q_start):
    qb, kl = s.shape[-2], s.shape[-1]
    q_chunk = (q_start + jnp.arange(qb)) // CHUNK
    k_chunk = jnp.arange(kl) // CHUNK
    allowed = k_chunk[None, :] <= q_chunk[:, None]
    return jax.nn.softmax(jnp.where(allowed, s, -jnp.inf), axis=-1)

def _diff_attention(h, w_in, q_g, k_g, lq1, lk1, lq2, lk2, sub_g, w_out, lambda_init):
    bsz, seq, _ = h.shape
    proj = h @ w_in
    q, k, v, gate = jnp.split(proj, [A_QK_WIDTH, 2 * A_QK_WIDTH, 2 * A_QK_WIDTH + A_WIDTH], axis=-1)
    q = q.reshape(bsz, seq, A_HEADS, 2, A_QK_DIM)
    k = k.reshape(bsz, seq, A_HEADS, 2, A_QK_DIM)
    v = v.reshape(bsz, seq, A_HEADS, A_V_DIM).transpose(0, 2, 1, 3).astype(jnp.float32)
    cos, sin = _rope_cos_sin(seq, A_QK_DIM)
    cos, sin = cos[:, None, None, :], sin[:, None, None, :]
    q = _apply_rope(_rms_norm(q, q_g), cos, sin).transpose(0, 2, 3, 1, 4).astype(jnp.float32)
    k = _apply_rope(_rms_norm(k, k_g), cos, sin).transpose(0, 2, 3, 1, 4).astype(jnp.float32)
    f32 = jnp.float32
    lam = (jnp.exp(jnp.sum(lq1.astype(f32) * lk1.astype(f32)))
           - jnp.exp(jnp.sum(lq2.astype(f32) * lk2.astype(f32))) + lambda_init)
    scale = A_QK_DIM ** -0.5
    outs = []
    for s0 in range(0, seq, QBLOCK):
        e = s0 + QBLOCK
        s = jnp.einsum('bhmqd,bhmkd->bhmqk', q[:, :, :, s0:e], k[:, :, :, :e]) * scale
        p = _chunk_causal_softmax(s, s0)
        wts = p[:, :, 0] - lam * p[:, :, 1]
        outs.append(jnp.einsum('bhqk,bhkd->bhqd', wts, v[:, :, :e]))
    o = jnp.concatenate(outs, axis=2)
    o = _rms_norm(o, sub_g) * (1.0 - lambda_init)
    o = o.transpose(0, 2, 1, 3).reshape(bsz, seq, A_WIDTH).astype(h.dtype)
    return (o * jax.nn.silu(gate)) @ w_out

def _conformer_conv(h, w_in, b_in, conv_w, conv_b, ln_g, ln_b, w_out):
    proj = h @ w_in + b_in
    a, b, gate = jnp.split(proj, 3, axis=-1)
    u = a * jax.nn.sigmoid(b)
    u = lax.conv_general_dilated(
        u, conv_w[:, None, :].astype(u.dtype), window_strides=(1,),
        padding=[(B_CONV - 1, 0)], dimension_numbers=('NWC', 'WIO', 'NWC'),
        feature_group_count=B_WIDTH) + conv_b
    u = jax.nn.silu(_layer_norm(u, ln_g, ln_b))
    return (u * jax.nn.silu(gate)) @ w_out

def _mla(h, w_in, cq_g, w_uq, ckv_g, w_ukv, q_g, k_g, w_out):
    bsz, seq, _ = h.shape
    proj = h @ w_in
    c_q, c_kv, k_rope, gate = jnp.split(
        proj, [C_Q_LORA, C_Q_LORA + C_KV_LORA, C_Q_LORA + C_KV_LORA + C_ROPE], axis=-1)
    q = (_rms_norm(c_q, cq_g) @ w_uq).reshape(bsz, seq, C_HEADS, C_QK)
    kv = (_rms_norm(c_kv, ckv_g) @ w_ukv).reshape(bsz, seq, C_HEADS, C_NOPE + C_V)
    q_nope, q_rope = jnp.split(q, [C_NOPE], axis=-1)
    k_nope, v = jnp.split(kv, [C_NOPE], axis=-1)
    cos, sin = _rope_cos_sin(seq, C_ROPE)
    q_nope = _rms_norm(q_nope, q_g[:C_NOPE])
    q_rope = _apply_rope(_rms_norm(q_rope, q_g[C_NOPE:]), cos[:, None, :], sin[:, None, :])
    k_nope = _rms_norm(k_nope, k_g[:C_NOPE])
    k_rope = _apply_rope(_rms_norm(k_rope, k_g[C_NOPE:]), cos, sin).astype(jnp.float32)
    qn = q_nope.transpose(0, 2, 1, 3).astype(jnp.float32)
    qr = q_rope.transpose(0, 2, 1, 3).astype(jnp.float32)
    kn = k_nope.transpose(0, 2, 1, 3).astype(jnp.float32)
    vv = v.transpose(0, 2, 1, 3).astype(jnp.float32)
    scale = C_QK ** -0.5
    outs = []
    for s0 in range(0, seq, QBLOCK):
        e = s0 + QBLOCK
        s = (jnp.einsum('bhqd,bhkd->bhqk', qn[:, :, s0:e], kn[:, :, :e])
             + jnp.einsum('bhqr,bkr->bhqk', qr[:, :, s0:e], k_rope[:, :e])) * scale
        p = _chunk_causal_softmax(s, s0)
        outs.append(jnp.einsum('bhqk,bhkd->bhqd', p, vv[:, :, :e]))
    o = jnp.concatenate(outs, axis=2).transpose(0, 2, 1, 3).reshape(bsz, seq, C_WIDTH).astype(h.dtype)
    return (o * jax.nn.silu(gate)) @ w_out

def first_inputs(seed: int = 0) -> dict:
    key = jax.random.key(seed)
    keys = iter(jax.random.split(key, 40))

    def nrm(shape, scale):
        return jax.random.normal(next(keys), shape, dtype=jnp.float32) * scale

    def gain(shape):
        return 1.0 + nrm(shape, 0.02)

    out_scale = 0.5
    return {
        'x': nrm((BATCH, SEQ, D_MODEL), 1.0),
        'a_norm_g': gain((N_A, D_MODEL)),
        'a_w_in': nrm((N_A, D_MODEL, A_IN), D_MODEL ** -0.5),
        'a_q_norm_g': gain((N_A, A_QK_DIM)),
        'a_k_norm_g': gain((N_A, A_QK_DIM)),
        'a_lam_q1': nrm((N_A, A_QK_DIM), 0.1),
        'a_lam_k1': nrm((N_A, A_QK_DIM), 0.1),
        'a_lam_q2': nrm((N_A, A_QK_DIM), 0.1),
        'a_lam_k2': nrm((N_A, A_QK_DIM), 0.1),
        'a_sub_norm_g': gain((N_A, A_V_DIM)),
        'a_w_out': nrm((N_A, A_WIDTH, D_MODEL), out_scale * A_WIDTH ** -0.5),
        'b_norm_g': gain((N_B, D_MODEL)),
        'b_w_in': nrm((N_B, D_MODEL, B_IN), D_MODEL ** -0.5),
        'b_b_in': nrm((N_B, B_IN), 0.01),
        'b_conv_w': nrm((N_B, B_CONV, B_WIDTH), B_CONV ** -0.5),
        'b_conv_b': nrm((N_B, B_WIDTH), 0.01),
        'b_ln_g': gain((N_B, B_WIDTH)),
        'b_ln_b': nrm((N_B, B_WIDTH), 0.01),
        'b_w_out': nrm((N_B, B_WIDTH, D_MODEL), out_scale * B_WIDTH ** -0.5),
        'c_norm_g': gain((N_C, D_MODEL)),
        'c_w_in': nrm((N_C, D_MODEL, C_IN), D_MODEL ** -0.5),
        'c_cq_norm_g': gain((N_C, C_Q_LORA)),
        'c_w_uq': nrm((N_C, C_Q_LORA, C_HEADS * C_QK), C_Q_LORA ** -0.5),
        'c_ckv_norm_g': gain((N_C, C_KV_LORA)),
        'c_w_ukv': nrm((N_C, C_KV_LORA, C_HEADS * (C_NOPE + C_V)), C_KV_LORA ** -0.5),
        'c_q_norm_g': gain((N_C, C_QK)),
        'c_k_norm_g': gain((N_C, C_QK)),
        'c_w_out': nrm((N_C, C_WIDTH, D_MODEL), out_scale * C_WIDTH ** -0.5),
    }

def first_block(x, a_norm_g, a_w_in, a_q_norm_g, a_k_norm_g, a_lam_q1, a_lam_k1, a_lam_q2,
              a_lam_k2, a_sub_norm_g, a_w_out, b_norm_g, b_w_in, b_b_in, b_conv_w, b_conv_b,
              b_ln_g, b_ln_b, b_w_out, c_norm_g, c_w_in, c_cq_norm_g, c_w_uq, c_ckv_norm_g,
              c_w_ukv, c_q_norm_g, c_k_norm_g, c_w_out):
    for i in range(DEPTH):
        kind, j = i % N_MIXERS, i // N_MIXERS
        if kind == 0:
            lambda_init = 0.8 - 0.6 * math.exp(-0.3 * i)
            h = _rms_norm(x, a_norm_g[j])
            x = x + _diff_attention(h, a_w_in[j], a_q_norm_g[j], a_k_norm_g[j], a_lam_q1[j],
                                    a_lam_k1[j], a_lam_q2[j], a_lam_k2[j], a_sub_norm_g[j],
                                    a_w_out[j], lambda_init)
        elif kind == 1:
            h = _rms_norm(x, b_norm_g[j])
            x = x + _conformer_conv(h, b_w_in[j], b_b_in[j], b_conv_w[j], b_conv_b[j],
                                    b_ln_g[j], b_ln_b[j], b_w_out[j])
        else:
            h = _rms_norm(x, c_norm_g[j])
            x = x + _mla(h, c_w_in[j], c_cq_norm_g[j], c_w_uq[j], c_ckv_norm_g[j], c_w_ukv[j],
                         c_q_norm_g[j], c_k_norm_g[j], c_w_out[j])
    return x


DEPTH_2 = 2

N_EVEN = (DEPTH_2 + 1) // 2
N_ODD = DEPTH_2 // 2

N_Q_HEADS = 8
N_KV_HEADS = 2
HEAD_DIM = 64
Q_GROUP = N_Q_HEADS // N_KV_HEADS
WINDOW = 128
ATTN_BLOCK = 128
ALIBI_MAX = 8.0
CONV_WIDTH_B = D_MODEL // 2
CONV_GROUPS_B = 8
CONV_K_B = 3
Q_DIM = N_Q_HEADS * HEAD_DIM
KV_DIM = N_KV_HEADS * HEAD_DIM
EVEN_IN = Q_DIM + 2 * KV_DIM + 3 * CONV_WIDTH_B
EVEN_MIX = Q_DIM + CONV_WIDTH_B
EVEN_SPLITS = (Q_DIM, Q_DIM + KV_DIM, Q_DIM + 2 * KV_DIM, Q_DIM + 2 * KV_DIM + CONV_WIDTH_B, Q_DIM + 2 * KV_DIM + 2 * CONV_WIDTH_B)
LRU_WIDTH = D_MODEL
LRU_HEADS = 8
LRU_HEAD_DIM = LRU_WIDTH // LRU_HEADS
CONV_K_C = 4
LRU_C = 8.0
D_FF = (D_MODEL * 7) // 2
N_EXPERTS = 8
TOP_K = 2
MOE_BLOCK = 128
NEG_INF = -1e30


def rms_norm(x, g):
    xf = x.astype(jnp.float32)
    y = xf * lax.rsqrt(jnp.mean(xf * xf, axis=-1, keepdims=True) + NORM_EPS)
    return (y * g.astype(jnp.float32)).astype(x.dtype)

def causal_depthwise_conv(x, w):
    K = w.shape[0]
    S = x.shape[1]
    xp = jnp.pad(x, ((0, 0), (K - 1, 0), (0, 0)))
    return sum(xp[:, k:k + S] * w[k] for k in range(K))

def alibi_slopes():
    h = jnp.arange(1, N_Q_HEADS + 1, dtype=jnp.float32)
    return jnp.exp2(-ALIBI_MAX * h / N_Q_HEADS)

def sliding_window_attention(q, k, v, sinks):
    B, S = q.shape[0], q.shape[1]
    L = ATTN_BLOCK
    nb = S // L
    qb = q.reshape(B, nb, L, N_KV_HEADS, Q_GROUP, HEAD_DIM)

    def band(t):
        cur = t.reshape(B, nb, L, N_KV_HEADS, HEAD_DIM)
        prev = jnp.pad(cur, ((0, 0), (1, 0), (0, 0), (0, 0), (0, 0)))[:, :-1]
        return jnp.concatenate([prev, cur], axis=2)

    kb, vb = band(k), band(v)
    scores = jnp.einsum('bnqkgd,bnskd->bnkgqs', qb, kb, preferred_element_type=jnp.float32) * (HEAD_DIM ** -0.5)
    qi = jnp.arange(L)[:, None]
    sj = jnp.arange(2 * L)[None, :]
    diff = L + qi - sj
    s_abs = (jnp.arange(nb)[:, None] - 1) * L + jnp.arange(2 * L)[None, :]
    valid = (diff >= 0)[None] & (diff < WINDOW)[None] & (s_abs >= 0)[:, None, :]
    slopes = alibi_slopes().reshape(N_KV_HEADS, Q_GROUP)
    bias = -slopes[:, :, None, None] * diff.astype(jnp.float32)
    scores = jnp.where(valid[None, :, None, None], scores + bias, NEG_INF)
    sink = jnp.broadcast_to(sinks.astype(jnp.float32).reshape(N_KV_HEADS, Q_GROUP)[None, None, :, :, None, None], scores.shape[:-1] + (1,))
    probs = jax.nn.softmax(jnp.concatenate([scores, sink], axis=-1), axis=-1)[..., :-1]
    out = jnp.einsum('bnkgqs,bnskd->bnqkgd', probs.astype(v.dtype), vb)
    return out.reshape(B, S, Q_DIM)

def attn_conv_mixer(h, w_in, q_gain, k_gain, sinks, conv_w, w_out):
    B, S, _ = h.shape
    q, k, v, gate_b, gate_c, u = jnp.split(h @ w_in, EVEN_SPLITS, axis=-1)
    q = rms_norm(q.reshape(B, S, N_Q_HEADS, HEAD_DIM), q_gain)
    k = rms_norm(k.reshape(B, S, N_KV_HEADS, HEAD_DIM), k_gain)
    v = v.reshape(B, S, N_KV_HEADS, HEAD_DIM)
    attn = sliding_window_attention(q, k, v, sinks)
    conv = gate_b * causal_depthwise_conv(gate_c * u, conv_w)
    return jnp.concatenate([attn, conv], axis=-1) @ w_out

def recurrent_mixer(h, w_in, conv_w, conv_b, ga_w, ga_b, gx_w, gx_b, lam, w_out):
    B, S, _ = h.shape
    y_branch, x_branch = jnp.split(h @ w_in, 2, axis=-1)
    y_branch = jax.nn.gelu(y_branch)
    xc = causal_depthwise_conv(x_branch, conv_w) + conv_b
    xh = xc.reshape(B, S, LRU_HEADS, LRU_HEAD_DIM)
    r = jax.nn.sigmoid(jnp.einsum('bshi,hij->bshj', xh, ga_w).reshape(B, S, LRU_WIDTH) + ga_b)
    i = jax.nn.sigmoid(jnp.einsum('bshi,hij->bshj', xh, gx_w).reshape(B, S, LRU_WIDTH) + gx_b)
    log_a = -LRU_C * r.astype(jnp.float32) * jax.nn.softplus(-lam.astype(jnp.float32))
    a = jnp.exp(log_a)
    mult = jnp.sqrt(jnp.maximum(-jnp.expm1(2.0 * log_a), 0.0))
    mult = jnp.where(jnp.arange(S)[None, :, None] == 0, 1.0, mult)
    b = mult * (i * xc).astype(jnp.float32)

    def combine(c1, c2):
        a1, b1 = c1
        a2, b2 = c2
        return a1 * a2, a2 * b1 + b2

    _, hs = lax.associative_scan(combine, (a, b), axis=1)
    return (y_branch * hs.astype(h.dtype)) @ w_out

def swiglu(h, w_gate, w_up, w_down):
    return (jax.nn.silu(h @ w_gate) * (h @ w_up)) @ w_down

def moe_swiglu(h, w_router, w_gate, w_up, w_down):
    B, S, D = h.shape
    T = B * S
    xf = h.reshape(T, D)
    logits = (xf @ w_router).astype(jnp.float32)
    top_logits, top_idx = lax.top_k(logits, TOP_K)
    gates = jax.nn.softmax(top_logits, axis=-1)
    n_assign = T * TOP_K
    e_flat = top_idx.reshape(-1).astype(jnp.int32)
    tok_flat = jnp.repeat(jnp.arange(T, dtype=jnp.int32), TOP_K)
    g_flat = gates.reshape(-1)
    order = jnp.argsort(e_flat)
    e_sorted = e_flat[order]
    counts = jnp.zeros((N_EXPERTS,), jnp.int32).at[e_flat].add(1)
    padded = (counts + MOE_BLOCK - 1) // MOE_BLOCK * MOE_BLOCK
    pad_end = jnp.cumsum(padded)
    pad_start = pad_end - padded
    start = jnp.cumsum(counts) - counts
    dest = pad_start[e_sorted] + jnp.arange(n_assign, dtype=jnp.int32) - start[e_sorted]
    n_rows = n_assign + N_EXPERTS * MOE_BLOCK
    n_blocks = n_rows // MOE_BLOCK
    row_tok = jnp.zeros((n_rows,), jnp.int32).at[dest].set(tok_flat[order])
    row_gate = jnp.zeros((n_rows,), jnp.float32).at[dest].set(g_flat[order])
    blk_start = jnp.arange(n_blocks, dtype=jnp.int32) * MOE_BLOCK
    blk_expert = jnp.minimum(jnp.searchsorted(pad_end, blk_start, side='right'), N_EXPERTS - 1)

    def expert_block(args):
        tok, e = args
        xb = xf[tok]
        hb = jax.nn.silu(xb @ w_gate[e]) * (xb @ w_up[e])
        return hb @ w_down[e]

    yb = lax.map(expert_block, (row_tok.reshape(n_blocks, MOE_BLOCK), blk_expert))
    y = yb.reshape(n_rows, D).astype(jnp.float32) * row_gate[:, None]
    out = jnp.zeros((T, D), jnp.float32).at[row_tok].add(y)
    return out.astype(h.dtype).reshape(B, S, D)

def second_inputs(seed: int = 0) -> dict:
    key = jax.random.key(seed)
    ks = iter(jax.random.split(key, 32))
    f32 = jnp.float32
    res_scale = (2 * DEPTH_2) ** -0.5

    def nrm(shape, scale):
        return jax.random.normal(next(ks), shape, f32) * scale

    x = nrm((BATCH, SEQ, D_MODEL), 1.0)
    norm_mix = 1.0 + nrm((DEPTH_2, D_MODEL), 0.02)
    norm_ffn = 1.0 + nrm((DEPTH_2, D_MODEL), 0.02)
    hy_w_in = nrm((N_EVEN, D_MODEL, EVEN_IN), D_MODEL ** -0.5)
    hy_q_gain = 1.0 + nrm((N_EVEN, HEAD_DIM), 0.02)
    hy_k_gain = 1.0 + nrm((N_EVEN, HEAD_DIM), 0.02)
    hy_sinks = nrm((N_EVEN, N_Q_HEADS), 0.5)
    hy_conv_w = nrm((N_EVEN, CONV_K_B, CONV_WIDTH_B), CONV_K_B ** -0.5)
    hy_w_out = nrm((N_EVEN, EVEN_MIX, D_MODEL), EVEN_MIX ** -0.5 * res_scale)
    rg_w_in = nrm((N_ODD, D_MODEL, 2 * LRU_WIDTH), D_MODEL ** -0.5)
    rg_conv_w = nrm((N_ODD, CONV_K_C, LRU_WIDTH), CONV_K_C ** -0.5)
    rg_conv_b = nrm((N_ODD, LRU_WIDTH), 0.01)
    rg_gate_a_w = nrm((N_ODD, LRU_HEADS, LRU_HEAD_DIM, LRU_HEAD_DIM), LRU_HEAD_DIM ** -0.5)
    rg_gate_a_b = nrm((N_ODD, LRU_WIDTH), 0.01)
    rg_gate_x_w = nrm((N_ODD, LRU_HEADS, LRU_HEAD_DIM, LRU_HEAD_DIM), LRU_HEAD_DIM ** -0.5)
    rg_gate_x_b = nrm((N_ODD, LRU_WIDTH), 0.01)
    a_pow_c = jax.random.uniform(next(ks), (N_ODD, LRU_WIDTH), f32, minval=0.9, maxval=0.999)
    a0 = a_pow_c ** (1.0 / LRU_C)
    rg_lambda = jnp.log(a0) - jnp.log1p(-a0)
    rg_w_out = nrm((N_ODD, LRU_WIDTH, D_MODEL), LRU_WIDTH ** -0.5 * res_scale)
    ffn_w_gate = nrm((N_EVEN, D_MODEL, D_FF), D_MODEL ** -0.5)
    ffn_w_up = nrm((N_EVEN, D_MODEL, D_FF), D_MODEL ** -0.5)
    ffn_w_down = nrm((N_EVEN, D_FF, D_MODEL), D_FF ** -0.5 * res_scale)
    moe_router = nrm((N_ODD, D_MODEL, N_EXPERTS), D_MODEL ** -0.5)
    moe_w_gate = nrm((N_ODD, N_EXPERTS, D_MODEL, D_FF), D_MODEL ** -0.5)
    moe_w_up = nrm((N_ODD, N_EXPERTS, D_MODEL, D_FF), D_MODEL ** -0.5)
    moe_w_down = nrm((N_ODD, N_EXPERTS, D_FF, D_MODEL), D_FF ** -0.5 * res_scale)
    return {'x': x, 'norm_mix': norm_mix, 'norm_ffn': norm_ffn,
            'hy_w_in': hy_w_in, 'hy_q_gain': hy_q_gain, 'hy_k_gain': hy_k_gain, 'hy_sinks': hy_sinks,
            'hy_conv_w': hy_conv_w, 'hy_w_out': hy_w_out,
            'rg_w_in': rg_w_in, 'rg_conv_w': rg_conv_w, 'rg_conv_b': rg_conv_b,
            'rg_gate_a_w': rg_gate_a_w, 'rg_gate_a_b': rg_gate_a_b, 'rg_gate_x_w': rg_gate_x_w,
            'rg_gate_x_b': rg_gate_x_b, 'rg_lambda': rg_lambda, 'rg_w_out': rg_w_out,
            'ffn_w_gate': ffn_w_gate, 'ffn_w_up': ffn_w_up, 'ffn_w_down': ffn_w_down,
            'moe_router': moe_router, 'moe_w_gate': moe_w_gate, 'moe_w_up': moe_w_up, 'moe_w_down': moe_w_down}

def second_block(x, norm_mix, norm_ffn, hy_w_in, hy_q_gain, hy_k_gain, hy_sinks, hy_conv_w, hy_w_out,
              rg_w_in, rg_conv_w, rg_conv_b, rg_gate_a_w, rg_gate_a_b, rg_gate_x_w, rg_gate_x_b, rg_lambda, rg_w_out,
              ffn_w_gate, ffn_w_up, ffn_w_down, moe_router, moe_w_gate, moe_w_up, moe_w_down):
    for layer in range(DEPTH_2):
        j = layer // 2
        h = rms_norm(x, norm_mix[layer])
        if layer % 2 == 0:
            x = x + attn_conv_mixer(h, hy_w_in[j], hy_q_gain[j], hy_k_gain[j], hy_sinks[j], hy_conv_w[j], hy_w_out[j])
            h = rms_norm(x, norm_ffn[layer])
            x = x + swiglu(h, ffn_w_gate[j], ffn_w_up[j], ffn_w_down[j])
        else:
            x = x + recurrent_mixer(h, rg_w_in[j], rg_conv_w[j], rg_conv_b[j], rg_gate_a_w[j], rg_gate_a_b[j],
                                    rg_gate_x_w[j], rg_gate_x_b[j], rg_lambda[j], rg_w_out[j])
            h = rms_norm(x, norm_ffn[layer])
            x = x + moe_swiglu(h, moe_router[j], moe_w_gate[j], moe_w_up[j], moe_w_down[j])
    return x


def setup_inputs(seed=0):
    out = dict(first_inputs(seed))
    for name, value in second_inputs(seed + 1).items():
        if name != "x":
            out[name + "_2"] = value
    return out


def reference(
    x, a_norm_g, a_w_in, a_q_norm_g, a_k_norm_g, a_lam_q1, a_lam_k1, a_lam_q2, a_lam_k2,
    a_sub_norm_g, a_w_out, b_norm_g, b_w_in, b_b_in, b_conv_w, b_conv_b, b_ln_g, b_ln_b,
    b_w_out, c_norm_g, c_w_in, c_cq_norm_g, c_w_uq, c_ckv_norm_g, c_w_ukv, c_q_norm_g,
    c_k_norm_g, c_w_out, norm_mix_2, norm_ffn_2, hy_w_in_2, hy_q_gain_2, hy_k_gain_2,
    hy_sinks_2, hy_conv_w_2, hy_w_out_2, rg_w_in_2, rg_conv_w_2, rg_conv_b_2, rg_gate_a_w_2,
    rg_gate_a_b_2, rg_gate_x_w_2, rg_gate_x_b_2, rg_lambda_2, rg_w_out_2, ffn_w_gate_2,
    ffn_w_up_2, ffn_w_down_2, moe_router_2, moe_w_gate_2, moe_w_up_2, moe_w_down_2,
):
    x = first_block(
        x, a_norm_g, a_w_in, a_q_norm_g, a_k_norm_g, a_lam_q1, a_lam_k1, a_lam_q2, a_lam_k2,
        a_sub_norm_g, a_w_out, b_norm_g, b_w_in, b_b_in, b_conv_w, b_conv_b, b_ln_g, b_ln_b,
        b_w_out, c_norm_g, c_w_in, c_cq_norm_g, c_w_uq, c_ckv_norm_g, c_w_ukv, c_q_norm_g,
        c_k_norm_g, c_w_out,
    )
    return second_block(
        x, norm_mix_2, norm_ffn_2, hy_w_in_2, hy_q_gain_2, hy_k_gain_2, hy_sinks_2, hy_conv_w_2,
        hy_w_out_2, rg_w_in_2, rg_conv_w_2, rg_conv_b_2, rg_gate_a_w_2, rg_gate_a_b_2,
        rg_gate_x_w_2, rg_gate_x_b_2, rg_lambda_2, rg_w_out_2, ffn_w_gate_2, ffn_w_up_2,
        ffn_w_down_2, moe_router_2, moe_w_gate_2, moe_w_up_2, moe_w_down_2,
    )


_drawn_inputs = setup_inputs


def setup_inputs(seed=0):
    import zlib

    import numpy as np

    out = dict(_drawn_inputs(seed))
    spreads = {}
    factors = {'a_norm_g': 3.728,
     'a_q_norm_g': 4.632,
     'a_k_norm_g': 5.767,
     'a_sub_norm_g': 5.764,
     'b_norm_g': 5.924,
     'b_b_in': 8.0,
     'b_conv_b': 8.0,
     'b_ln_g': 8.0,
     'b_ln_b': 8.0,
     'c_norm_g': 5.523,
     'c_cq_norm_g': 8.0,
     'c_ckv_norm_g': 8.0,
     'c_q_norm_g': 8.0,
     'c_k_norm_g': 7.915,
     'norm_mix_2': 3.826,
     'norm_ffn_2': 21.504,
     'hy_q_gain_2': 64.0,
     'hy_k_gain_2': 64.0,
     'hy_sinks_2': 43.152,
     'rg_conv_b_2': 30.162,
     'rg_gate_a_b_2': 64.0,
     'rg_gate_x_b_2': 64.0}
    for name, (base, spread) in spreads.items():
        noise = np.random.default_rng([zlib.crc32(name.encode()), seed]).standard_normal(out[name].shape)
        drawn = base * np.exp(spread * noise) if base else spread * noise
        out[name] = __import__('jax').numpy.asarray(drawn.astype(out[name].dtype))
    for name, factor in factors.items():
        out[name] = (out[name] * factor).astype(out[name].dtype)
    return out
```

```python
from contextlib import ExitStack

import numpy as np

import concourse.bass as bass
from concourse import mybir

ALU = mybir.AluOpType
ACT = mybir.ActivationFunctionType
F32 = mybir.dt.float32
I32 = mybir.dt.int32
U32 = mybir.dt.uint32
AX = mybir.AxisListType.X

P = 128
SEQ = 256
TILES = SEQ // P
D = 1024
KC = D // P
EPS = 1e-6
MASKED = -1e30

A_HEADS, A_QK, A_V = 8, 64, 128
A_LAMBDA_INIT = (0.8 - 0.6 * float(np.exp(-0.3 * 0)), 0.8 - 0.6 * float(np.exp(-0.3 * 3)))
CHUNK = 64
CONV_TAPS = 31
C_HEADS, C_NOPE, C_ROPE, C_V = 8, 128, 64, 128
C_QK = C_NOPE + C_ROPE
C_Q_LORA, C_KV_LORA = 256, 128
C_HEAD_IN = C_Q_LORA + C_KV_LORA + C_ROPE
H_HEADS, H_KV_HEADS, H_DIM = 8, 2, 64
H_WINDOW = 128
H_CONV = 512
H_TAPS = 3
R_HEADS = 8
R_TAPS = 4
R_C = 8.0
D_FF = 3584
FF_STEP = 512
FF_STEPS = D_FF // FF_STEP
N_EXPERTS = 8

UNIT = KC * 512
RING = 7
UNITS_PER_EXPERT = 3 * FF_STEPS
ITEMS = 16
GROUP = 4

VECTOR_ROWS = {}
_row = 0
for _name, _rows, _width in (
    ("a_norm_g", 2, D), ("b_norm_g", 1, D), ("c_norm_g", 1, D), ("norm_mix_2", 2, D), ("norm_ffn_2", 2, D),
    ("b_b_in", 3, D), ("b_conv_b", 1, D), ("b_ln_g", 1, D), ("b_ln_b", 1, D),
    ("c_cq_norm_g", 1, C_Q_LORA), ("c_ckv_norm_g", 1, C_KV_LORA),
    ("rg_conv_b_2", 1, D), ("rg_gate_a_b_2", 1, D), ("rg_gate_x_b_2", 1, D), ("rg_lambda_2", 1, D),
    ("rg_conv_w_2", R_TAPS, D), ("hy_conv_w_2", H_TAPS, H_CONV), ("b_conv_w", CONV_TAPS, D),
):
    VECTOR_ROWS[_name] = (_row, _rows, _width)
    _row += _rows
N_ROWS = 64
assert _row <= N_ROWS

SPREAD = {}
_col = 0
for _name, _cols in (
    ("a_q_norm_g", 2 * A_QK), ("a_k_norm_g", 2 * A_QK), ("a_sub_norm_g", 2 * A_V),
    ("c_q_norm_g", C_QK), ("c_k_norm_g", C_QK), ("hy_q_gain_2", H_DIM), ("hy_k_gain_2", H_DIM), ("hy_sinks_2", H_HEADS),
    ("a_lam_q1", 2 * A_QK), ("a_lam_k1", 2 * A_QK), ("a_lam_q2", 2 * A_QK), ("a_lam_k2", 2 * A_QK),
):
    SPREAD[_name] = (_col, _cols)
    _col += _cols
N_SPREAD = SPREAD["a_lam_q1"][0]


def constants():
    half = A_QK // 2
    inverse = (1.0 / (np.float32(10000.0) ** (np.arange(0, A_QK, 2, dtype=np.float32) / np.float32(A_QK)))).astype(np.float32)
    angle = np.arange(SEQ, dtype=np.float32)[:, None] * inverse[None, :]
    cos, sin = np.cos(angle).astype(np.float32), np.sin(angle).astype(np.float32)

    def by_tile(a):
        return a.reshape(TILES, P, 2 * half).transpose(1, 0, 2).reshape(P, TILES * 2 * half)

    q = np.arange(P, dtype=np.float32)[:, None]
    back = P + q - np.arange(2 * P, dtype=np.float32)[None, :]
    parts = {
        "ident": np.eye(P, dtype=np.float32),
        "cos": by_tile(np.concatenate([cos, cos], axis=1)),
        "sin": by_tile(np.concatenate([-sin, sin], axis=1)),
        "back": np.where((back >= 0) & (back < H_WINDOW), back, np.float32(1e33)),
        "before": np.triu(np.ones((P, P), np.float32), 1),
        "ones": np.ones((P, P), np.float32),
        "mean": np.full((P, P), 1.0 / D, np.float32),
        "count": np.broadcast_to(np.arange(P, dtype=np.float32), (P, P)),
        "neghalf": np.full((P, 16), -0.5, np.float32),
    }
    at, col = {}, 0
    for name, a in parts.items():
        at[name] = (col, a.shape[1])
        col += a.shape[1]
    return np.ascontiguousarray(np.concatenate(list(parts.values()), axis=1).astype(np.float32)), at


class Banks:

    SHORT, LONG = 0, 4

    def __init__(self):
        self.turns = {0: 0, 4: 0}
        self.at = {}

    def plan(self, name, ring=0):
        n = self.turns[ring]
        self.turns[ring] += 1
        self.at[name] = (ring + n % 4, n // 4)


class Steps:

    def __init__(self, eng, sem):
        self.eng, self.sem, self.done = eng, sem, 0

    def link(self, instruction):
        self.done = self.done + 1
        instruction.then_inc(self.sem, 1)
        self.eng.wait_ge(self.sem, self.done)


def attention_order(layer):
    order = []
    for s in range(ITEMS + 5):
        if s < ITEMS:
            order.append(("scores", s))
        if 0 <= s - 2 < ITEMS:
            order.append(("weights", s - 2))
        if 0 <= s - 3 < ITEMS:
            order.append(("values", s - 3))
        g = (s - 8) // GROUP
        if s >= 8 and (s - 8) % GROUP == 0:
            order.append(("output", g))
    return order


def a_order():
    order = []
    for i in range(16):
        order.append(("product", i))
        if 3 <= i < 11:
            order.append(("turn", i - 3))
    return order


def c_order():
    order = [("low", 0), ("low", 1), ("gate", 0), ("gate", 1), ("lowturn", 0), ("gate", 2), ("lowturn", 1), ("gate", 3)]
    for i in range(9):
        if i < 8:
            order += [("q", i), ("kv", i)]
        if i >= 1:
            order += [("qturn", i - 1), ("kturn", i - 1)]
    return order


def h_order():
    return [
        ("q", 0), ("q", 1), ("kv", 0), ("kv", 1), ("shift", 0), ("value", 0), ("qturn", 0), ("kturn", 0),
        ("gate", 0), ("shift", 1), ("qturn", 1), ("kturn", 1), ("value", 1), ("gate", 1),
    ]


def r_order():
    return (
        [("x", p) for p in range(4)] + [("y", 0), ("y", 1)] + [("gates", h) for h in range(R_HEADS)] + [("y", 2), ("y", 3)]
    )


def ffn_order():
    order = []
    for j in range(FF_STEPS + 1):
        if j < FF_STEPS:
            order += [("gate", j, 0), ("up", j, 0), ("gate", j, 1), ("up", j, 1)]
        if j >= 1:
            order += [("turn", j - 1, 0), ("turn", j - 1, 1), ("down", j - 1, None)]
    return order


def moe_order():
    order = [("gather", 0), ("gather", 1), ("unplace", 0)]
    for j in range(FF_STEPS + 1):
        if j < FF_STEPS:
            order += [("gate", j), ("up", j)]
        if j >= 1:
            order += [("turn", j - 1), ("down", j - 1)]
    return order + [("scatter", i) for i in range(4)]


MOE_SHORT = sum(kind != "down" for kind, _ in moe_order())
assert MOE_SHORT % 4 == 0


def plan_banks():
    banks = Banks()

    def norm(n):
        for i in range(4):
            banks.plan(("norm", n, i))

    def attention(layer):
        for kind, i in attention_order(layer):
            if kind == "values":
                if i % GROUP == 0:
                    banks.plan((layer, "values", i // GROUP), Banks.LONG)
            else:
                banks.plan((layer, kind, i))

    def out(layer):
        for i in range(4):
            banks.plan((layer, "out", i), Banks.LONG)

    def a_layer(j):
        for kind, i in a_order():
            banks.plan((f"a{j}", kind, i))
        attention(f"a{j}")
        out(f"a{j}")

    banks.plan("vectors")
    norm(0)
    a_layer(0)
    norm(1)
    for i in range(12):
        banks.plan(("b", "product", i))
    banks.plan(("b", "sum"), Banks.LONG)
    banks.plan(("b", "squares"), Banks.LONG)
    out("b")
    norm(2)
    for kind, i in c_order():
        banks.plan(("c", kind, i))
    attention("c")
    out("c")
    norm(3)
    a_layer(1)
    norm(4)
    for kind, i in h_order():
        banks.plan(("h", kind, i))
    attention("h")
    out("h")
    norm(5)
    for kind, j, t in ffn_order():
        if kind != "down":
            banks.plan(("ffn", kind, j, t))
    out("ffn")
    norm(6)
    for kind, i in r_order():
        banks.plan(("r", kind, i))
    out("r")
    norm(7)
    banks.plan("logits")
    banks.plan("places")
    for kind, j in moe_order():
        if kind != "down":
            banks.plan(("moe", kind, j))
    for half in range(2):
        banks.plan(("moe", "expert", half), Banks.LONG)
    return banks


class Buffers:
    pass


class Core:

    def __init__(self, nc, ctx, w, consts, const_at, out):
        self.nc, self.w, self.consts, self.out = nc, w, consts, out
        self.banks = plan_banks()
        self.engine_steps = {}

        def sb(name, shape, dtype=F32):
            return ctx.enter_context(nc.sbuf_tensor(name, shape, dtype))

        def sem(name):
            return ctx.enter_context(nc.semaphore(name))

        self.psum = ctx.enter_context(nc.psum_tensor("psum", [P, 8, 512], F32))
        self.ring = sb("ring", [P, RING, UNIT])
        self.x = sb("x", [P, TILES, D])
        self.h = sb("h", [P, TILES, D])
        self.hT = sb("hT", [P, KC, SEQ])
        self.yT = sb("yT", [P, KC, SEQ])
        self.const = sb("const", [P, consts.shape[1]])
        self.spread = sb("spread", [P, N_SPREAD])
        self.vecs = sb("vecs", [P, KC, N_ROWS])
        self.arena = sb("arena", [P, 12800])
        self.small = sb("small", [P, 640])
        self.work = sb("work", [P, 16], I32)
        self.router = sb("router", [P, KC, N_EXPERTS])
        self.best = sb("best", [P, TILES, 8], U32)
        self.carved = 0

        def const(name):
            col, n = const_at[name]
            return self.const[:, col:col + n]

        self.ident, self.before, self.ones, self.mean = const("ident"), const("before"), const("ones"), const("mean")
        self.cos = const("cos").rearrange("p (t d) -> p t d", t=TILES)
        self.sin = const("sin").rearrange("p (t d) -> p t d", t=TILES)
        self.back, self.count, self.neghalf = const("back"), const("count"), const("neghalf")

        at = 0

        def small(n):
            nonlocal at
            at += n
            return self.small[:, at - n:at]

        self.ms, self.rstd = small(2), small(2)
        self.neglam = small(2)
        self.lam_sums, self.lam_exps = small(4), small(4)
        self.subgain = small(2 * A_V)
        self.decay, self.negdecay = small(KC), small(KC)
        self.soft = [small(KC) for _ in range(6)]
        self.group_ms, self.group_rstd = small(4 * 8), small(4 * 8)
        self.top, self.lowest, self.sums, self.inverse = small(4), small(4), small(4), small(4)
        self.pair_scale = small(4)
        self.sink_exp = small(4)
        self.out_ms, self.out_rstd = small(2 * GROUP), small(2 * GROUP)
        self.logits = small(TILES * 8)
        self.sorted = small(TILES * 8)
        self.first = small(TILES * 2)
        self.gap, self.both = small(TILES), small(TILES)
        self.share = small(TILES * 2)
        self.chosen = small(TILES * N_EXPERTS).rearrange("p (t e) -> p t e", t=TILES)
        self.weight = small(TILES * N_EXPERTS).rearrange("p (t e) -> p t e", t=TILES)
        self.place = small(2 * TILES * N_EXPERTS).rearrange("p (s t e) -> p s t e", s=2, t=TILES)
        self.over = small(5 * 8)
        assert at <= 640

        self.x_landed = sem("x_landed")
        self.const_landed = sem("const_landed")
        self.rows_landed = sem("rows_landed")
        self.spread_landed = sem("spread_landed")
        self.router_landed = sem("router_landed")
        self.stored = sem("stored")
        self.landed = [sem(f"unit_landed_{i}") for i in range(RING)]
        self.filled = [sem(f"filled_{i}") for i in range(8)]
        self.freed = [sem(f"freed_{i}") for i in range(8)]
        self.down_done = sem("down_done")
        self.own = {e: sem(f"{e}_own") for e in ("act", "dve", "pool")}
        self.rows_cleared = sem("rows_cleared")
        self.tables_ready = sem("tables_ready")
        self.lam_exps_ready = sem("lam_exps_ready")
        self.soft_ready = sem("soft_ready")
        self.softexp_ready = sem("softexp_ready")
        self.ms_ready = sem("ms_ready")
        self.rstd_ready = sem("rstd_ready")
        self.h_ready = sem("h_ready")
        self.group_squares = sem("group_squares")
        self.group_ms_ready = sem("group_ms_ready")
        self.group_rstd_ready = sem("group_rstd_ready")
        self.staged = sem("staged")
        self.cleared = sem("cleared")
        self.lowest_ready = sem("lowest_ready")
        self.weights_ready = sem("weights_ready")
        self.out_squares = sem("out_squares")
        self.out_ms_ready = sem("out_ms_ready")
        self.out_rstd_ready = sem("out_rstd_ready")
        self.gates_ready = sem("gates_ready")
        self.c_low_staged = sem("c_low_staged")
        self.c_q_staged = sem("c_q_staged")
        self.c_k_staged = sem("c_k_staged")
        self.c_v_ready = sem("c_v_ready")
        self.c_roots_used = sem("c_roots_used")
        self.b_gate_ready = sem("b_gate_ready")
        self.b_pair_done = sem("b_pair_done")
        self.conv_ready = sem("conv_ready")
        self.b_mean_gone = sem("b_mean_gone")
        self.b_squares_ready = sem("b_squares_ready")
        self.b_var_ready = sem("b_var_ready")
        self.b_root_ready = sem("b_root_ready")
        self.b_normed = sem("b_normed")
        self.b_silu_ready = sem("b_silu_ready")
        self.b_mixed = sem("b_mixed")
        self.h_q_staged = sem("h_q_staged")
        self.h_k_staged = sem("h_k_staged")
        self.r_conv_ready = sem("r_conv_ready")
        self.r_decay_ready = sem("r_decay_ready")
        self.r_decays = sem("r_decays")
        self.r_root_in = sem("r_root_in")
        self.r_root_ready = sem("r_root_ready")
        self.r_mixed = sem("r_mixed")
        self.routed = sem("routed")
        self.placed = sem("placed")
        self.gap_ready = sem("gap_ready")
        self.share_ready = sem("share_ready")
        self.work_ready = sem("work_ready")

    def reset_arena(self):
        self.carved = 0

    def carve(self, *shape):
        n = int(np.prod(shape))
        a = self.arena[:, self.carved:self.carved + n]
        self.carved += n
        assert self.carved <= 12800
        if len(shape) == 2:
            return a.rearrange("p (a b) -> p a b", a=shape[0])
        if len(shape) == 3:
            return a.rearrange("p (a b c) -> p a b c", a=shape[0], b=shape[1])
        return a

    def bank(self, name):
        return self.psum[:, self.banks.at[name][0], :]

    def take(self, pe, name, more=0):
        b, use = self.banks.at[name]
        if use > 0:
            pe.wait_ge(self.freed[b], use + more)

    def fill(self, matmul, name):
        matmul.then_inc(self.filled[self.banks.at[name][0]], 1)

    def wait_filled(self, eng, name, more=0):
        b, use = self.banks.at[name]
        eng.wait_ge(self.filled[b], use + 1 + more)

    def release(self, instruction, name):
        instruction.then_inc(self.freed[self.banks.at[name][0]], 1)

    def wait_released(self, eng, name, more=0):
        b, use = self.banks.at[name]
        eng.wait_ge(self.freed[b], use + 1 + more)

    def wait_unit(self, eng, u):
        eng.wait_ge(self.landed[u % RING], 16 * (u // RING + 1))

    def unit(self, u, kc=KC):
        return self.ring[:, u % RING, :].rearrange("p (c n) -> p c n", c=kc)

    def column(self, name, c, row=0):
        r = VECTOR_ROWS[name][0] + row
        return self.vecs[:, c, r:r + 1]

    def wide(self, name, start=0, n=None):
        col, m = SPREAD[name]
        if col >= N_SPREAD:
            return self.hT[:, 0:2, :].rearrange("p c t -> p (c t)")[:, col - N_SPREAD + start:col - N_SPREAD + start + (m - start if n is None else n)]
        return self.spread[:, col + start:col + start + (m - start if n is None else n)]


def over_groups(a, groups):
    return a.unsqueeze(1).broadcast_to([P, groups, a.shape[1]])


def over_columns(a, n):
    return a.unsqueeze(2).broadcast_to([P, a.shape[1], n])



def weight_units(k):
    w, units = k.w, []

    def columns(a, first, n, last_use):
        units.append((a[:, first:first + n].rearrange("(c p) n -> p c n", p=P), (a.shape[0] // P, n), last_use))

    for layer, j in (("a0", 0), ("b", 0), ("c", 0), ("a1", 1), ("h", 0), ("ffn", 0), ("r", 0)):
        if layer[0] == "a":
            for u in range(8):
                columns(w["a_w_in"][j], 512 * u, 512, (layer, "product", 2 * u + 1))
            out = w["a_w_out"][j]
        if layer == "b":
            for half in range(2):
                for kind in range(3):
                    columns(w["b_w_in"][0], D * kind + 512 * half, 512, (layer, "product", 6 * half + 3 + kind))
            out = w["b_w_out"][0]
        if layer == "c":
            columns(w["c_w_in"][0], 0, C_HEAD_IN, (layer, "low", 1))
            columns(w["c_w_in"][0], C_HEAD_IN, 512, (layer, "gate", 1))
            columns(w["c_w_in"][0], C_HEAD_IN + 512, 512, (layer, "gate", 3))
            columns(w["c_w_uq"][0], 0, C_HEADS * C_QK, (layer, "q", 7))
            columns(w["c_w_ukv"][0], 0, C_HEADS * (C_NOPE + C_V), (layer, "kv", 7))
            out = w["c_w_out"][0]
        if layer == "h":
            a = w["hy_w_in_2"][0]
            columns(a, 0, 512, (layer, "q", 1))
            columns(a, 512, 256, (layer, "kv", 1))
            columns(a, 1280, 512, (layer, "shift", 1))
            columns(a, 1792, 512, (layer, "value", 1))
            columns(a, 768, 512, (layer, "gate", 1))
            out = w["hy_w_out_2"][0]
        if layer == "r":
            a = w["rg_w_in_2"][0]
            columns(a, D, 512, (layer, "x", 1))
            columns(a, D + 512, 512, (layer, "x", 3))
            columns(a, 0, 512, (layer, "y", 1))
            units.append(("gates", None, (layer, "gates", R_HEADS - 1)))
            columns(a, 512, 512, (layer, "y", 3))
            out = w["rg_w_out_2"][0]
        if layer == "ffn":
            for j in range(FF_STEPS):
                columns(w["ffn_w_gate_2"][0], FF_STEP * j, FF_STEP, (layer, "gate", j, 1))
                columns(w["ffn_w_up_2"][0], FF_STEP * j, FF_STEP, (layer, "up", j, 1))
                rows = w["ffn_w_down_2"][0][FF_STEP * j:FF_STEP * (j + 1), :]
                units.append((rows.rearrange("(c p) n -> p c n", p=P), (FF_STEP // P, D), j + 1 if j < FF_STEPS - 1 else (layer, "out", 3)))
            continue
        for n in range(2):
            columns(out, 512 * n, 512, (layer, "out", 2 * n + 1))
    return units


def first_units():
    return {"a0": 0, "b": 10, "c": 18, "a1": 25, "h": 35, "ffn": 42, "r": 63}


def sync_weights(k, sp):
    units = weight_units(k)
    assert len(units) == 70 and len(units) % RING == 0
    for u, (src, shape, _) in enumerate(units):
        if u >= RING:
            sync_unit_used(k, sp, units[u - RING][2])
        if isinstance(src, str):
            dst = k.ring[:, u % RING, 0:2 * R_HEADS * P].rearrange("p (g h n) -> p g h n", g=2, h=R_HEADS)
            sp.dma_start(dst[:, 0], k.w["rg_gate_a_w_2"][0].rearrange("h p n -> p h n")).then_inc(k.landed[u % RING], 16)
            sp.dma_start(dst[:, 1], k.w["rg_gate_x_w_2"][0].rearrange("h p n -> p h n")).then_inc(k.gates_ready, 16)
            continue
        dst = k.ring[:, u % RING, 0:shape[0] * shape[1]].rearrange("p (c n) -> p c n", c=shape[0])
        sp.dma_start(dst, src).then_inc(k.landed[u % RING], 16)


def sync_unit_used(k, sp, last_use):
    if isinstance(last_use, int):
        sp.wait_ge(k.down_done, last_use)
    else:
        k.wait_filled(sp, last_use)



def setup_loads(k, act):
    for t in range(TILES):
        act.dma_start(k.x[:, t, :], k.w["x"][0].rearrange("(t p) d -> p t d", p=P)[:, t, :]).then_inc(k.x_landed, 16)
    act.dma_start(k.const[:, :], k.consts).then_inc(k.const_landed, 16)
    act.wait_ge(k.rows_cleared, 1)
    rows = k.yT[:, :, :].rearrange("p c n -> p (c n)")
    for name, (row, n, width) in VECTOR_ROWS.items():
        a = k.w[name]
        src = a[0] if name in ("rg_conv_w_2", "hy_conv_w_2", "b_conv_w") else a
        if name == "b_b_in":
            src = a[0].rearrange("(a d) -> a d", a=3)
        act.dma_start(rows[row:row + n, 0:width], src).then_inc(k.rows_landed, 16)
    for name, (col, n) in SPREAD.items():
        a = k.w[name].rearrange("a n -> (a n)").unsqueeze(0)
        act.dma_start(k.wide(name), a.broadcast_to([P, n])).then_inc(k.spread_landed, 16)


    act.dma_start(k.router[:, :, :], k.w["moe_router_2"][0].rearrange("(c p) e -> p c e", p=P)).then_inc(k.router_landed, 16)


def setup_tensor(k, pe):
    pe.wait_ge(k.const_landed, 16)
    pe.wait_ge(k.rows_landed, 16 * len(VECTOR_ROWS))
    rows = k.yT[:, :, :].rearrange("p c n -> p (c n)")
    k.take(pe, "vectors")
    for c in range(KC):
        last = pe.transpose(k.bank("vectors")[:, N_ROWS * c:N_ROWS * (c + 1)], rows[0:N_ROWS, P * c:P * (c + 1)],
                            k.ident[0:N_ROWS, 0:N_ROWS])
    k.fill(last, "vectors")


def rope_tables(k, v, steps, tables, gain, tile_tables=True):
    half = A_QK // 2
    for t in range(TILES):
        cos, sin = tables[:, 2 * t, :], tables[:, 2 * t + 1, :]
        v.tensor_tensor(cos, k.cos[:, t, :], gain, ALU.mult).then_inc(k.tables_ready, 1)
        v.tensor_tensor(sin[:, 0:half], k.sin[:, t, 0:half], gain[:, half:], ALU.mult).then_inc(k.tables_ready, 1)
        v.tensor_tensor(sin[:, half:], k.sin[:, t, half:], gain[:, 0:half], ALU.mult).then_inc(k.tables_ready, 1)


def setup_vector(k, v):
    steps = k.engine_steps["dve"]
    v.memset(k.yT[:, :, :], 0.0).then_inc(k.rows_cleared, 1)
    k.wait_filled(v, "vectors")
    k.release(v.tensor_copy(k.vecs[:, :, :].rearrange("p c r -> p (c r)"), k.bank("vectors")[:, 0:KC * N_ROWS]), "vectors")
    k.wait_released(v, "vectors")
    v.wait_ge(k.const_landed, 16)
    v.wait_ge(k.spread_landed, 16 * len(SPREAD))
    junk = k.arena[:, 0:A_QK]
    for j in range(2):
        for m, (q, kk) in enumerate((("a_lam_q1", "a_lam_k1"), ("a_lam_q2", "a_lam_k2"))):
            steps.link(v.tensor_tensor_reduce(junk, k.wide(q, A_QK * j, A_QK), k.wide(kk, A_QK * j, A_QK), 1.0, 0.0,
                                              ALU.mult, ALU.add, k.lam_sums[:, 2 * j + m:2 * j + m + 1]))
    lam = k.vecs[:, :, VECTOR_ROWS["rg_lambda_2"][0]]
    neg, mag, s, s2, acc, pos = k.soft
    steps.link(v.tensor_scalar(neg, lam, -1.0, None, ALU.mult))
    steps.link(v.tensor_tensor(mag, neg, lam, ALU.min))
    v.tensor_scalar(pos, neg, 0.0, None, ALU.max).then_inc(k.soft_ready, 1)
    v.wait_ge(k.softexp_ready, 1)
    steps.link(v.tensor_scalar(s2, mag, 2.0, None, ALU.add))
    steps.link(v.reciprocal(s2, s2))
    steps.link(v.tensor_tensor(s, mag, s2, ALU.mult))
    steps.link(v.tensor_tensor(s2, s, s, ALU.mult))
    steps.link(v.tensor_scalar(acc, s2, 1.0 / 17, 1.0 / 15, ALU.mult, ALU.add))
    for n in (13, 11, 9, 7, 5, 3, 1):
        steps.link(v.tensor_tensor(acc, acc, s2, ALU.mult))
        steps.link(v.tensor_scalar(acc, acc, 1.0 / n, None, ALU.add))
    steps.link(v.tensor_tensor(acc, acc, s, ALU.mult))
    v.wait_ge(k.soft_ready, 1)
    steps.link(v.scalar_tensor_tensor(acc, acc, 2.0, pos, ALU.mult, ALU.add))
    steps.link(v.tensor_scalar(k.decay, acc, R_C, None, ALU.mult))
    v.wait_ge(k.lam_exps_ready, 1)
    for j in range(2):
        e = k.lam_exps[:, 2 * j:2 * j + 2]
        steps.link(v.tensor_tensor(k.neglam[:, j:j + 1], e[:, 1:2], e[:, 0:1], ALU.subtract))
        steps.link(v.tensor_scalar(k.neglam[:, j:j + 1], k.neglam[:, j:j + 1], -A_LAMBDA_INIT[j], None, ALU.add))
        steps.link(v.tensor_scalar(k.subgain[:, A_V * j:A_V * (j + 1)], k.wide("a_sub_norm_g", A_V * j, A_V),
                                   1.0 - A_LAMBDA_INIT[j], None, ALU.mult))


def setup_scalar(k, act):
    act.wait_ge(k.soft_ready, 1)
    act.activation(k.soft[1], k.soft[1], ACT.Exp).then_inc(k.softexp_ready, 1)
    act.activation(k.lam_exps, k.lam_sums, ACT.Exp).then_inc(k.lam_exps_ready, 1)



NORM_GAIN = [("a_norm_g", 0), ("b_norm_g", 0), ("c_norm_g", 0), ("a_norm_g", 1), ("norm_mix_2", 0), ("norm_ffn_2", 0),
             ("norm_mix_2", 1), ("norm_ffn_2", 1)]


def norm_scalar(k, act, n, x_from):
    for name in x_from:
        k.wait_released(act, name)
    if n == 0:
        act.wait_ge(k.x_landed, 16 * TILES)
    act.activation(k.h[:, 0, :], k.x[:, 0, :], ACT.Square, scale=float(D) ** -0.5, accum_out=k.ms[:, 0:1]).then_inc(k.ms_ready, 1)
    act.wait_ge(k.rstd_ready, n + 1)
    act.wait_ge(k.ms_ready, 2 * n + 2)
    act.activation(k.h[:, 0, :], k.x[:, 0, :], ACT.Copy, scale=k.rstd[:, 0:1]).then_inc(k.h_ready, 1)
    norm_evacuate(k, act, n, (1, 3))


def norm_vector(k, v, n, x_from):
    for name in x_from:
        k.wait_released(v, name)
    if n == 0:
        v.wait_ge(k.x_landed, 16 * TILES)
    v.tensor_tensor_reduce(k.h[:, 1, :], k.x[:, 1, :], k.x[:, 1, :], 1.0 / D, 0.0, ALU.mult, ALU.add, k.ms[:, 1:2])\
     .then_inc(k.ms_ready, 1)
    v.wait_ge(k.rstd_ready, n + 1)
    v.tensor_scalar(k.h[:, 1, :], k.x[:, 1, :], k.rstd[:, 1:2], None, ALU.mult).then_inc(k.h_ready, 1)
    norm_evacuate(k, v, n, (0, 2))


def norm_evacuate(k, eng, n, turns):
    name, row = NORM_GAIN[n]
    for i in turns:
        k.wait_filled(eng, ("norm", n, i))
        for c in (2 * i, 2 * i + 1):
            src = k.bank(("norm", n, i))[:, SEQ * (c % 2):SEQ * (c % 2 + 1)]
            if eng is k.nc.scalar:
                last = eng.activation(k.hT[:, c, :], src, ACT.Copy, scale=k.column(name, c, row))
            else:
                last = eng.tensor_scalar(k.hT[:, c, :], src, k.column(name, c, row), None, ALU.mult)
        k.release(last, ("norm", n, i))


def norm_pool(k, pool, n):
    pool.wait_ge(k.ms_ready, 2 * n + 2)
    inverse_root(k, pool, k.ms, k.rstd, k.rstd_ready)


def inverse_root(k, pool, ms, rstd, ready):
    n = ms.shape[1]
    k.engine_steps["pool"].link(pool.tensor_scalar(rstd, ms, EPS, None, ALU.add))
    pool.tensor_tensor(rstd, rstd, k.neghalf[:, 0:n], ALU.pow).then_inc(ready, 1)


def norm_tensor(k, pe, n):
    if n == 0:
        pe.wait_ge(k.const_landed, 16)
    pe.wait_ge(k.h_ready, 2 * n + 2)
    for i in range(4):
        k.take(pe, ("norm", n, i))
        for c in (2 * i, 2 * i + 1):
            for t in range(TILES):
                first = SEQ * (c % 2) + P * t
                last = pe.transpose(k.bank(("norm", n, i))[:, first:first + P], k.h[:, t, P * c:P * (c + 1)], k.ident)
        k.fill(last, ("norm", n, i))
    for i in range(4):
        k.wait_released(pe, ("norm", n, i))



def product(k, pe, name, u, lhs, t, kc, n, first=0, width=512):
    k.wait_unit(pe, u)
    k.take(pe, name)
    w = k.ring[:, u % RING, 0:kc * width].rearrange("p (c n) -> p c n", c=kc)
    for c in range(kc):
        last = pe.matmul(k.bank(name)[:, 0:n], lhs[:, c, P * t:P * (t + 1)], w[:, c, first:first + n],
                         start=(c == 0), stop=(c == kc - 1))
    k.fill(last, name)


def channel_product(k, pe, name, u, first):
    k.wait_unit(pe, u)
    k.take(pe, name)
    for half in range(2):
        for c in range(KC):
            last = pe.matmul(k.bank(name)[:, SEQ * half:SEQ * (half + 1)],
                             k.unit(u)[:, c, first + P * half:first + P * (half + 1)], k.hT[:, c, :],
                             start=(c == 0), stop=(c == KC - 1))
    k.fill(last, name)


def out_tensor(k, pe, layer, u):
    for n in range(2):
        for t in range(TILES):
            product(k, pe, (layer, "out", 2 * n + t), u + n, k.yT, t, KC, 512)


def out_vector(k, v, layer):
    for n in range(2):
        for t in range(TILES):
            add_to_x(k, v, (layer, "out", 2 * n + t), t, n)


def add_to_x(k, v, name, t, n):
    k.wait_filled(v, name)
    part = k.x[:, t, 512 * n:512 * (n + 1)]
    k.release(v.tensor_tensor(part, part, k.bank(name), ALU.add), name)


def out_names(layer):
    return [(layer, "out", i) for i in range(4)]



ATTENTIONS = {"a0": 0, "c": 1, "a1": 2, "h": 3}
SCORE_SCALE = {"a": A_QK ** -0.5, "c": C_QK ** -0.5, "h": H_DIM ** -0.5}
VALUE_DIM = {"a": A_V, "c": C_V, "h": H_DIM}


def item(i):
    return i // 8, i % 8


def keys_of(t):
    return P * (t + 1)


def attention_buffers(k):
    a = k.h[:, :, :].rearrange("p t d -> p (t d)")
    probs = a[:, 0:1024].rearrange("p (s n) -> p s n", s=2)
    weights = a[:, 1024:1536].rearrange("p (s n) -> p s n", s=2)
    turned = a[:, 1536:2048].rearrange("p (s n) -> p s n", s=2)
    return probs, weights, turned


def attention_tensor(k, pe, layer, b, u_out):
    probs, weights, turned = attention_buffers(k)
    base, kind = ITEMS * ATTENTIONS[layer], layer[0]
    dim = VALUE_DIM[kind]
    for step, i in attention_order(layer):
        t, head = item(i)
        tile = slice(P * t, P * (t + 1))
        e = keys_of(t)
        if step == "scores":
            name = (layer, step, i)
            k.take(pe, name)
            bank = k.bank(name)
            if kind == "a":
                for m in range(2):
                    last = pe.matmul(bank[:, SEQ * m:SEQ * m + e], b.qT[:, m, head, tile], b.kT[:, head, 0:e], start=True, stop=True)
            if kind == "c":
                pe.matmul(bank[:, 0:e], b.qT[:, head, tile], b.kT[:, head, 0:e], start=True, stop=False)
                last = pe.matmul(bank[:, 0:e], b.qropeT[:, head // 2, tile], b.kropeT[:, head % 2, 0:e], start=False, stop=True)
            if kind == "h":
                last = pe.matmul(bank[:, 0:e], b.qT[:, head % 4, tile], b.kT[:, head // 4, 0:e], start=True, stop=True)
            k.fill(last, name)
        if step == "weights":
            name = (layer, step, i)
            pe.wait_ge(k.weights_ready, base + i + 1)
            k.take(pe, name)
            for c in range(t + 1):
                last = pe.transpose(k.bank(name)[:, P * c:P * (c + 1)], weights[:, i % 2, P * c:P * (c + 1)], k.ident)
            k.fill(last, name)
        if step == "values":
            name = (layer, step, i // GROUP)
            if i % GROUP == 0:
                k.take(pe, name)
            k.wait_released(pe, (layer, "weights", i))
            if kind == "h":
                cols = slice(H_DIM * (head // 4), H_DIM * (head // 4 + 1))
            else:
                cols = slice(dim * head, dim * (head + 1))
            place = dim * (i % GROUP)
            for c in range(t + 1):
                last = pe.matmul(k.bank(name)[:, place:place + dim], turned[:, i % 2, P * c:P * (c + 1)], b.v[:, c, cols],
                                 start=(c == 0), stop=(c == t))
            if i % GROUP == GROUP - 1:
                k.fill(last, name)
        if step == "output":
            name = (layer, step, i)
            pe.wait_ge(k.staged, b.staged0 + i + 1)
            k.take(pe, name)
            for c in range(GROUP * dim // P):
                last = pe.transpose(k.bank(name)[:, P * c:P * (c + 1)], b.y[:, i % 2, P * c:P * (c + 1)], k.ident)
            k.fill(last, name)
    for g in range(ITEMS // GROUP):
        k.wait_released(pe, (layer, "output", g))
    out_tensor(k, pe, layer, u_out)


def attention_scalar(k, act, layer, b):
    probs, weights, turned = attention_buffers(k)
    base, kind = ITEMS * ATTENTIONS[layer], layer[0]
    scale = SCORE_SCALE[kind]
    for s in range(ITEMS + 5):
        if s < ITEMS:
            t, head = item(s)
            e = keys_of(t)
            act.wait_ge(k.lowest_ready, base + s + 1)
            low = k.lowest.rearrange("p (s m) -> p s m", s=2)[:, s % 2, :]
            sums = k.sums.rearrange("p (s m) -> p s m", s=2)[:, s % 2, :]
            name = (layer, "scores", s)
            if kind == "h":
                act.activation(k.sink_exp[:, s % 2:s % 2 + 1], k.wide("hy_sinks_2", head, 1), ACT.Exp, bias=low[:, 0:1])
                k.release(act.activation(probs[:, s % 2, 0:e], b.s[:, s % 2, 0:e], ACT.Exp, bias=low[:, 0:1],
                                         accum_out=sums[:, 0:1]), name)
            else:
                maps = 2 if kind == "a" else 1
                for m in range(maps):
                    last = act.activation(probs[:, s % 2, SEQ * m:SEQ * m + e], k.bank(name)[:, SEQ * m:SEQ * m + e], ACT.Exp,
                                          bias=low[:, m:m + 1], scale=scale, accum_out=sums[:, m:m + 1])
                k.release(last, name)
        if 0 <= s - 2 < ITEMS:
            i = s - 2
            e = keys_of(item(i)[0])
            k.wait_filled(act, (layer, "weights", i))
            k.release(act.activation(turned[:, i % 2, 0:e], k.bank((layer, "weights", i))[:, 0:e], ACT.Copy), (layer, "weights", i))
        g = (s - 6) // GROUP
        if kind == "a" and s >= 6 and (s - 6) % GROUP == 0 and g < 4:
            k.wait_filled(act, (layer, "values", g))
            act.activation(b.squares, k.bank((layer, "values", g)), ACT.Square, scale=float(A_V) ** -0.5).then_inc(k.out_squares, 1)
        g = (s - 8) // GROUP
        if s >= 8 and (s - 8) % GROUP == 0:
            t, half = g // 2, g % 2
            n = GROUP * VALUE_DIM[kind] // P
            k.wait_filled(act, (layer, "output", g))
            src = k.bank((layer, "output", g))[:, 0:P * n].rearrange("p (c q) -> p c q", c=n)
            k.release(act.activation(k.yT[:, n * half:n * (half + 1), P * t:P * (t + 1)], src, ACT.Copy), (layer, "output", g))


def attention_vector(k, v, layer, b):
    steps = k.engine_steps["dve"]
    probs, weights, turned = attention_buffers(k)
    base, kind = ITEMS * ATTENTIONS[layer], layer[0]
    scale = SCORE_SCALE[kind]
    maps = 2 if kind == "a" else 1
    for s in range(ITEMS + 5):
        if s < ITEMS:
            t, head = item(s)
            e = keys_of(t)
            name = (layer, "scores", s)
            k.wait_filled(v, name)
            bank = k.bank(name)
            top = k.top.rearrange("p (s m) -> p s m", s=2)[:, s % 2, 0:maps]
            low = k.lowest.rearrange("p (s m) -> p s m", s=2)[:, s % 2, 0:maps]
            if kind == "h":
                slope = 2.0 ** -(head + 1)
                both = bank[:, 0:e]
                steps.link(v.tensor_scalar(b.s[:, s % 2, 0:e], both, scale, None, ALU.mult))
                steps.link(v.scalar_tensor_tensor(b.s[:, s % 2, 0:e], k.back[:, SEQ - e:SEQ], -slope, b.s[:, s % 2, 0:e],
                                                  ALU.mult, ALU.add))
                steps.link(v.tensor_reduce(top, b.s[:, s % 2, 0:e], AX, ALU.max))
                steps.link(v.tensor_tensor(top, top, k.wide("hy_sinks_2", head, 1), ALU.max))
                v.tensor_scalar(low, top, -1.0, None, ALU.mult).then_inc(k.lowest_ready, 1)
            else:
                bank3 = bank.rearrange("p (m n) -> p m n", m=2)
                steps.link(v.memset(bank3[0:CHUNK, 0:maps, e - CHUNK:e], MASKED))
                steps.link(v.tensor_reduce(top, bank3[:, 0:maps, 0:e], AX, ALU.max))
                v.tensor_scalar(low, top, -scale, None, ALU.mult).then_inc(k.lowest_ready, 1)
        i = s - 1
        if 0 <= i < ITEMS:
            t, head = item(i)
            e = keys_of(t)
            slot = i % 2
            sums = k.sums.rearrange("p (s m) -> p s m", s=2)[:, slot, 0:maps]
            inv = k.inverse.rearrange("p (s m) -> p s m", s=2)[:, slot, 0:maps]
            k.wait_released(v, (layer, "scores", i))
            if kind == "h":
                steps.link(v.tensor_tensor(sums, sums, k.sink_exp[:, slot:slot + 1], ALU.add))
            steps.link(v.reciprocal(inv, sums))
            if i >= 2:
                k.wait_filled(v, (layer, "weights", i - 2))
            if kind == "a":
                j = int(layer[1])
                steps.link(v.tensor_scalar(k.pair_scale[:, slot:slot + 1], inv[:, 1:2], k.neglam[:, j:j + 1], None, ALU.mult))
                steps.link(v.tensor_scalar(b.second[:, 0:e], probs[:, slot, SEQ:SEQ + e], k.pair_scale[:, slot:slot + 1], None, ALU.mult))
                v.scalar_tensor_tensor(weights[:, slot, 0:e], probs[:, slot, 0:e], inv[:, 0:1], b.second[:, 0:e],
                                       ALU.mult, ALU.add).then_inc(k.weights_ready, 1)
            else:
                v.tensor_scalar(weights[:, slot, 0:e], probs[:, slot, 0:e], inv[:, 0:1], None, ALU.mult).then_inc(k.weights_ready, 1)
        g = (s - 6) // GROUP
        if kind == "a" and s >= 6 and (s - 6) % GROUP == 0 and g < 4:
            n = 4 * int(layer[1]) + g
            v.wait_ge(k.out_squares, n + 1)
            v.tensor_reduce(k.out_ms[:, 0:GROUP], b.squares.rearrange("p (h d) -> p h d", h=GROUP), AX, ALU.add)\
             .then_inc(k.out_ms_ready, 1)
        g = (s - 7) // GROUP
        if s >= 7 and (s - 7) % GROUP == 0 and g < 4:
            t, half = g // 2, g % 2
            name = (layer, "values", g)
            k.wait_filled(v, name)
            dim = VALUE_DIM[kind]
            bank = k.bank(name)[:, 0:GROUP * dim]
            y = b.y[:, g % 2, 0:GROUP * dim]
            if g >= 2:
                k.wait_filled(v, (layer, "output", g - 2))
            if kind == "a":
                v.wait_ge(k.out_rstd_ready, 4 * int(layer[1]) + g + 1)
                y3 = y.rearrange("p (h d) -> p h d", h=GROUP)
                k.release(v.tensor_tensor(y3, bank.rearrange("p (h d) -> p h d", h=GROUP),
                                          over_columns(k.out_rstd[:, 0:GROUP], dim), ALU.mult), name)
                k.wait_released(v, name)
                j = int(layer[1])
                steps.link(v.tensor_tensor(y3, y3, over_groups(k.subgain[:, A_V * j:A_V * (j + 1)], GROUP), ALU.mult))
                v.tensor_tensor(y, y, b.gate[:, t, 512 * half:512 * (half + 1)], ALU.mult).then_inc(k.staged, 1)
            if kind == "c":
                k.release(v.tensor_tensor(y, bank, b.gate[:, t, 512 * half:512 * (half + 1)], ALU.mult), name)
                k.wait_released(v, name)
                v.sem_inc(k.staged, 1)
            if kind == "h":
                k.release(v.tensor_copy(y, bank), name)
                k.wait_released(v, name)
                v.sem_inc(k.staged, 1)
    out_vector(k, v, layer)


def attention_pool(k, pool, layer):
    if layer[0] == "a":
        for g in range(4):
            pool.wait_ge(k.out_ms_ready, 4 * int(layer[1]) + g + 1)
            inverse_root(k, pool, k.out_ms[:, 0:GROUP], k.out_rstd[:, 0:GROUP], k.out_rstd_ready)



def a_buffers(k, j):
    k.reset_arena()
    b = Buffers()
    b.qT = k.carve(2 * A_HEADS, SEQ).rearrange("p (m h) t -> p m h t", m=2)
    b.kT = k.carve(A_HEADS, SEQ)
    b.v = k.carve(TILES, A_HEADS * A_V)
    b.gate = k.carve(TILES, A_HEADS * A_V)
    b.raw = k.h[:, 0, 0:512]
    b.direct = k.h[:, 0, 512:1024]
    b.swapped = k.h[:, 1, 0:512]
    b.q = k.carve(2, 512)
    b.squares2 = k.carve(2, 512)
    b.q_tables = k.carve(2 * TILES, A_QK)
    b.k_tables = k.carve(2 * TILES, A_QK)
    b.staged0 = STAGED[f"a{j}"][0]
    b.y, b.squares, b.second = b.q, b.squares2[:, 0, :], b.squares2[:, 1, 0:SEQ]
    return b


STAGED = {"a0": (8, 0), "c": (12, 12), "a1": (16 + 8, 16), "h": (28, 28)}

GROUP_MS = {"a0": 0, "c": 8, "a1": 26, "h": 34}


def a_tensor(k, pe, j, u):
    b, layer = a_buffers(k, j), f"a{j}"
    staged0 = STAGED[layer][1]
    for kind, i in a_order():
        name = (layer, kind, i)
        if kind == "product":
            product(k, pe, name, u + i // 2, k.hT, i % 2, KC, 512)
        else:
            pe.wait_ge(k.staged, staged0 + i + 1)
            k.take(pe, name)
            for c in range(4):
                last = pe.transpose(k.bank(name)[:, P * c:P * (c + 1)], b.q[:, i % 2, P * c:P * (c + 1)], k.ident)
            k.fill(last, name)
    pe.wait_ge(k.cleared, 1 + 2 * j)
    for kind, i in a_order():
        k.wait_released(pe, (layer, kind, i))
    attention_tensor(k, pe, layer, b, u + 8)


def a_scalar(k, act, j):
    b, layer = a_buffers(k, j), f"a{j}"
    act.wait_ge(k.cleared, 1 + 2 * j)
    for kind, i in a_order():
        name = (layer, kind, i)
        bank = k.bank(name)
        u, t = i // 2, i % 2
        if kind == "product":
            if i >= 2 and i < 8:
                act.wait_ge(k.group_ms_ready, GROUP_MS[layer] + i - 1)
            k.wait_filled(act, name)
            if u < 4:
                act.activation(b.squares2[:, i % 2, :], bank, ACT.Square, scale=float(A_QK) ** -0.5).then_inc(k.group_squares, 1)
            elif u < 6:
                k.release(act.activation(b.v[:, t, 512 * (u - 4):512 * (u - 3)], bank, ACT.Copy), name)
            else:
                k.release(act.activation(b.gate[:, t, 512 * (u - 6):512 * (u - 5)], bank, ACT.Silu), name)
        else:
            k.wait_filled(act, name)
            src = bank.rearrange("p (c q) -> p c q", c=4)
            heads, tile = slice(4 * (u % 2), 4 * (u % 2) + 4), slice(P * t, P * (t + 1))
            if u < 2:
                act.activation(b.qT[0:A_QK, 0, heads, tile], src[0:A_QK], ACT.Copy)
                k.release(act.activation(b.qT[A_QK:P, 1, heads, tile], src[A_QK:P], ACT.Copy), name)
            else:
                k.release(act.activation(b.kT[:, heads, tile], src, ACT.Copy), name)
    attention_scalar(k, act, layer, b)


def a_vector(k, v, j):
    b, layer = a_buffers(k, j), f"a{j}"
    steps = k.engine_steps["dve"]
    rope_tables(k, v, steps, b.q_tables, k.wide("a_q_norm_g", A_QK * j, A_QK))
    rope_tables(k, v, steps, b.k_tables, k.wide("a_k_norm_g", A_QK * j, A_QK))
    v.memset(b.qT[:, :, :, :], 0.0).then_inc(k.cleared, 1)
    v.wait_ge(k.tables_ready, TABLES[layer])

    def reduce(i):
        v.wait_ge(k.group_squares, 8 * j + i + 1)
        v.tensor_reduce(k.group_ms[:, 8 * (i % 4):8 * (i % 4 + 1)], b.squares2[:, i % 2, :].rearrange("p (g d) -> p g d", g=8),
                        AX, ALU.add).then_inc(k.group_ms_ready, 1)

    reduce(0)
    for i in range(8):
        if i + 1 < 8:
            reduce(i + 1)
        t = i % 2
        name = (layer, "product", i)
        tables = b.q_tables if i < 4 else b.k_tables
        v.wait_ge(k.group_rstd_ready, GROUP_MS[layer] + i + 1)
        if i >= 2:
            k.wait_filled(v, (layer, "turn", i - 2))
        rotate(k, v, steps, k.bank(name), over_columns(k.group_rstd[:, 8 * (i % 4):8 * (i % 4 + 1)], A_QK), 8,
               tables[:, 2 * t, :], tables[:, 2 * t + 1, :], b, b.q[:, i % 2, :], name)
    attention_vector(k, v, layer, b)


def rotate(k, v, steps, bank, rstd, groups, cos, sin, b, out, name):
    half = A_QK // 2
    n = groups * A_QK

    def grouped(a):
        return a[:, 0:n].rearrange("p (g d) -> p g d", g=groups)

    raw, direct, swapped = grouped(b.raw), grouped(b.direct), grouped(b.swapped)
    k.release(v.tensor_tensor(raw, grouped(bank), rstd, ALU.mult), name)
    k.wait_released(v, name)
    steps.link(v.tensor_tensor(direct, raw, over_groups(cos, groups), ALU.mult))
    steps.link(v.tensor_tensor(swapped[:, :, 0:half], raw[:, :, half:], over_groups(sin[:, 0:half], groups), ALU.mult))
    steps.link(v.tensor_tensor(swapped[:, :, half:], raw[:, :, 0:half], over_groups(sin[:, half:], groups), ALU.mult))
    v.tensor_tensor(grouped(out), direct, swapped, ALU.add).then_inc(k.staged, 1)


TABLES = {"a0": 12, "c": 24, "a1": 36}


def a_pool(k, pool, j):
    for i in range(8):
        n = GROUP_MS[f"a{j}"] + i
        pool.wait_ge(k.group_ms_ready, n + 1)
        inverse_root(k, pool, k.group_ms[:, 8 * (i % 4):8 * (i % 4 + 1)], k.group_rstd[:, 8 * (i % 4):8 * (i % 4 + 1)], k.group_rstd_ready)
    attention_pool(k, pool, f"a{j}")



def b_buffers(k):
    k.reset_arena()
    b = Buffers()
    b.padded = k.carve(KC, CONV_TAPS - 1 + SEQ)
    b.conv = k.carve(KC, SEQ)
    b.gate = k.carve(KC, SEQ)
    b.squares = k.carve(KC, SEQ)
    b.gate_in = k.carve(2, 2 * SEQ)
    b.gate_sigmoid = k.carve(2, 2 * SEQ)
    b.root = k.carve(SEQ)
    b.var = k.carve(SEQ)
    b.rstd = k.h[:, 0, 0:SEQ]
    return b


def b_products():
    return [(6 * half + 3 * pair + kind, kind, 2 * half + pair) for half in range(2) for pair in range(2) for kind in range(3)]


def b_tensor(k, pe, u):
    for i, kind, pair in b_products():
        channel_product(k, pe, ("b", "product", i), u + 3 * (pair // 2) + kind, 2 * P * (pair % 2))
    b = b_buffers(k)
    for name, what, ready in (("sum", b.conv, k.conv_ready), ("squares", b.squares, k.b_squares_ready)):
        k.take(pe, ("b", name))
        for c in range(KC):
            pe.wait_ge(ready, c + 1)
            last = pe.matmul(k.bank(("b", name))[:, 0:SEQ], k.mean, what[:, c, :], start=(c == 0), stop=(c == KC - 1))
        k.fill(last, ("b", name))
    pe.wait_ge(k.b_mixed, KC)
    out_tensor(k, pe, "b", u + 6)


def b_scalar(k, act):
    b = b_buffers(k)
    for i, kind, pair in b_products():
        if kind == 0:
            continue
        name = ("b", "product", i)
        k.wait_filled(act, name)
        if pair >= 2:
            act.wait_ge(k.b_pair_done, pair - 1)
        dst = (b.gate_in if kind == 1 else b.gate_sigmoid)[:, pair % 2, :]
        for half in range(2):
            c = 2 * pair + half
            last = act.activation(dst[:, SEQ * half:SEQ * (half + 1)], k.bank(name)[:, SEQ * half:SEQ * (half + 1)], ACT.Sigmoid,
                                  bias=k.column("b_b_in", c, kind))
        if kind == 1:
            k.release(last, name)
        else:
            last.then_inc(k.b_gate_ready, 1)
    for c in range(KC):
        act.wait_ge(k.b_mean_gone, c + 1)
        act.activation(b.squares[:, c, :], b.conv[:, c, :], ACT.Square).then_inc(k.b_squares_ready, 1)
    act.wait_ge(k.b_var_ready, 1)
    act.activation(b.root, b.var, ACT.Sqrt).then_inc(k.b_root_ready, 1)
    for c in range(KC):
        act.wait_ge(k.b_normed, c + 1)
        act.activation(b.squares[:, c, :], b.conv[:, c, :], ACT.Silu, scale=k.column("b_ln_g", c), bias=k.column("b_ln_b", c))\
           .then_inc(k.b_silu_ready, 1)


def b_vector(k, v):
    b = b_buffers(k)
    steps = k.engine_steps["dve"]
    pad = CONV_TAPS - 1
    steps.link(v.memset(b.padded[:, :, 0:pad], 0.0))
    for pair in range(4):
        a_name, _, g_name = (("b", "product", 6 * (pair // 2) + 3 * (pair % 2) + kind) for kind in range(3))
        k.wait_filled(v, a_name)
        k.wait_released(v, ("b", "product", 6 * (pair // 2) + 3 * (pair % 2) + 1))
        for half in range(2):
            c = 2 * pair + half
            cols = slice(SEQ * half, SEQ * (half + 1))
            last = v.scalar_tensor_tensor(b.padded[:, c, pad:], k.bank(a_name)[:, cols], k.column("b_b_in", c, 0),
                                          b.gate_in[:, pair % 2, cols], ALU.add, ALU.mult)
        k.release(last, a_name)
        v.wait_ge(k.b_gate_ready, pair + 1)
        for half in range(2):
            c = 2 * pair + half
            cols = slice(SEQ * half, SEQ * (half + 1))
            last = v.scalar_tensor_tensor(b.gate[:, c, :], k.bank(g_name)[:, cols], k.column("b_b_in", c, 2),
                                          b.gate_sigmoid[:, pair % 2, cols], ALU.add, ALU.mult)
        k.release(last, g_name)
        k.wait_released(v, g_name)
        v.sem_inc(k.b_pair_done, 1)
        for tap in range(CONV_TAPS):
            for half in range(2):
                c = 2 * pair + half
                window, weight = b.padded[:, c, tap:tap + SEQ], k.column("b_conv_w", c, tap)
                if tap > 0:
                    v.wait_ge(steps.sem, steps.done - 1)
                if tap == 0:
                    last = v.tensor_scalar(b.conv[:, c, :], window, weight, k.column("b_conv_b", c), ALU.mult, ALU.add)
                else:
                    last = v.scalar_tensor_tensor(b.conv[:, c, :], window, weight, b.conv[:, c, :], ALU.mult, ALU.add)
                if tap == CONV_TAPS - 1:
                    last.then_inc(k.conv_ready, 1)
                else:
                    last.then_inc(steps.sem, 1)
                    steps.done += 1
            if tap == CONV_TAPS - 2:
                v.wait_ge(steps.sem, steps.done)
    v.wait_ge(k.conv_ready, KC)
    k.wait_filled(v, ("b", "sum"))
    for c in range(KC):
        v.tensor_tensor(b.conv[:, c, :], b.conv[:, c, :], k.bank(("b", "sum"))[:, 0:SEQ], ALU.subtract).then_inc(k.b_mean_gone, 1)
    v.wait_ge(k.b_mean_gone, KC)
    v.sem_inc(k.freed[k.banks.at[("b", "sum")][0]], 1)
    k.wait_filled(v, ("b", "squares"))
    k.release(v.tensor_scalar(b.var, k.bank(("b", "squares"))[:, 0:SEQ], EPS, None, ALU.add), ("b", "squares"))
    k.wait_released(v, ("b", "squares"))
    v.sem_inc(k.b_var_ready, 1)
    v.wait_ge(k.b_root_ready, 1)
    steps.link(v.reciprocal(b.rstd, b.root))
    for c in range(KC):
        v.tensor_tensor(b.conv[:, c, :], b.conv[:, c, :], b.rstd, ALU.mult).then_inc(k.b_normed, 1)
    for c in range(KC):
        v.wait_ge(k.b_silu_ready, c + 1)
        v.tensor_tensor(k.yT[:, c, :], b.squares[:, c, :], b.gate[:, c, :], ALU.mult).then_inc(k.b_mixed, 1)
    out_vector(k, v, "b")



def c_buffers(k):
    k.reset_arena()
    b = Buffers()
    b.qT = k.carve(C_HEADS, SEQ)
    b.kT = k.carve(C_HEADS, SEQ)
    b.qropeT = k.carve(C_HEADS // 2, SEQ)
    b.kropeT = k.carve(2, SEQ)
    b.v = k.carve(TILES, C_WIDTH)
    b.gate = k.carve(TILES, C_WIDTH)
    b.y = k.carve(2, 512)
    b.q_tables = k.carve(2 * TILES, C_ROPE)
    b.k_tables = k.carve(2 * TILES, C_ROPE)
    b.staged0 = STAGED["c"][0]
    b.lowT = k.yT
    a = k.h[:, :, :].rearrange("p t d -> p (t d)")
    b.low, b.q = a[:, 0:1024].rearrange("p (s n) -> p s n", s=2), a[:, 0:1024].rearrange("p (s n) -> p s n", s=2)
    b.raw, b.direct, b.swapped = a[:, 1024:1152], a[:, 1152:1280], a[:, 1280:1408]
    b.k = b.y[:, :, 0:256]
    b.junk = a[:, 1536:2048]
    return b


C_WIDTH = C_HEADS * C_V


def c_tensor(k, pe, u):
    b = c_buffers(k)
    staged0 = STAGED["c"][1]
    for kind, i in c_order():
        name = ("c", kind, i)
        bank = k.bank(name)
        if kind == "low":
            product(k, pe, name, u, k.hT, i, KC, C_HEAD_IN, 0, C_HEAD_IN)
        if kind == "gate":
            product(k, pe, name, u + 1 + i // 2, k.hT, i % 2, KC, 512)
        if kind == "lowturn":
            pe.wait_ge(k.c_low_staged, i + 1)
            k.take(pe, name)
            for c in range(4):
                last = pe.transpose(bank[:, P * c:P * (c + 1)], b.low[:, i, P * c:P * (c + 1)], k.ident)
            k.fill(last, name)
        if kind == "q":
            k.wait_released(pe, ("c", "lowturn", i % 2))
            product(k, pe, name, u + 3, b.lowT, i % 2, C_Q_LORA // P, 2 * C_QK, 2 * C_QK * (i // 2), C_HEADS * C_QK)
        if kind == "kv":
            product(k, pe, name, u + 4, b.lowT[:, 2:3, :], i % 2, 1, 512, 512 * (i // 2), C_HEADS * (C_NOPE + C_V))
        if kind == "qturn":
            pe.wait_ge(k.c_q_staged, i + 1)
            k.take(pe, name)
            for c in range(3):
                last = pe.transpose(bank[:, P * c:P * (c + 1)], b.q[:, i % 2, P * c:P * (c + 1)], k.ident)
            k.fill(last, name)
        if kind == "kturn":
            pe.wait_ge(k.c_k_staged, i + 1)
            k.take(pe, name)
            for c in range(2):
                last = pe.transpose(bank[:, P * c:P * (c + 1)], b.k[:, i % 2, P * c:P * (c + 1)], k.ident)
            k.fill(last, name)
    pe.wait_ge(k.cleared, 2)
    for kind, i in c_order():
        k.wait_released(pe, ("c", kind, i))
    attention_tensor(k, pe, "c", b, u + 5)


def c_scalar(k, act):
    b = c_buffers(k)
    act.wait_ge(k.cleared, 2)
    squares = GROUP_MS["c"]
    steps = k.engine_steps["act"]
    for kind, i in c_order():
        name = ("c", kind, i)
        bank = k.bank(name)
        k.wait_filled(act, name)
        tile = slice(P * (i % 2), P * (i % 2 + 1))
        if kind in ("low", "q", "kv"):
            parts = {
                "low": ((0, C_Q_LORA), (C_Q_LORA, C_KV_LORA), (C_Q_LORA + C_KV_LORA, C_ROPE)),
                "q": ((0, C_NOPE), (C_NOPE, C_ROPE), (C_QK, C_NOPE), (C_QK + C_NOPE, C_ROPE)),
                "kv": ((0, C_NOPE), (C_NOPE + C_V, C_NOPE)),
            }[kind]
            if squares - GROUP_MS["c"] >= 4:
                act.wait_ge(k.c_roots_used, squares - GROUP_MS["c"] - 3)
            col = 8 * (squares % 4)
            junk = 0
            for m, (first, n) in enumerate(parts):
                last = act.activation(b.junk[:, junk:junk + n], bank[:, first:first + n],
                                      ACT.Square, scale=float(n) ** -0.5, accum_out=k.group_ms[:, col + m:col + m + 1])
                junk += n
            last.then_inc(k.group_ms_ready, 1)
            squares += 1
            act.wait_ge(k.group_ms_ready, squares)
            if kind == "kv":
                heads = bank.rearrange("p (h n) -> p h n", h=2)
                dst = b.v[:, i % 2, 256 * (i // 2):256 * (i // 2 + 1)].rearrange("p (h n) -> p h n", h=2)
                act.activation(dst, heads[:, :, C_NOPE:], ACT.Copy).then_inc(k.c_v_ready, 1)
        if kind == "gate":
            u, t = i // 2, i % 2
            k.release(act.activation(b.gate[:, t, 512 * u:512 * (u + 1)], bank, ACT.Silu), name)
        if kind == "lowturn":
            for c in range(3):
                gain = k.column("c_cq_norm_g", c) if c < 2 else k.column("c_ckv_norm_g", 0)
                act.activation(b.lowT[:, c, tile], bank[:, P * c:P * (c + 1)], ACT.Copy, scale=gain)
            act.activation(b.kropeT[0:C_ROPE, 0, tile], bank[0:C_ROPE, 3 * P:4 * P], ACT.Copy)
            k.release(act.activation(b.kropeT[C_ROPE:P, 1, tile], bank[C_ROPE:P, 3 * P:4 * P], ACT.Copy), name)
        if kind == "qturn":
            pair = i // 2
            act.activation(b.qT[:, 2 * pair:2 * pair + 2, tile], bank[:, 0:2 * P].rearrange("p (h q) -> p h q", h=2), ACT.Copy)
            k.release(act.activation(b.qropeT[:, pair, tile], bank[:, 2 * P:3 * P], ACT.Copy), name)
        if kind == "kturn":
            pair = i // 2
            k.release(act.activation(b.kT[:, 2 * pair:2 * pair + 2, tile], bank[:, 0:2 * P].rearrange("p (h q) -> p h q", h=2),
                                     ACT.Copy), name)
    attention_scalar(k, act, "c", b)


def c_vector(k, v):
    b = c_buffers(k)
    steps = k.engine_steps["dve"]
    rope_tables(k, v, steps, b.q_tables, k.wide("c_q_norm_g", C_NOPE, C_ROPE))
    rope_tables(k, v, steps, b.k_tables, k.wide("c_k_norm_g", C_NOPE, C_ROPE))
    v.memset(b.kropeT[:, :, :], 0.0).then_inc(k.cleared, 1)
    v.wait_ge(k.tables_ready, TABLES["c"])
    n = 0
    for kind, i in c_order():
        if kind not in ("low", "q", "kv"):
            continue
        name = ("c", kind, i)
        bank = k.bank(name)
        col = 8 * ((GROUP_MS["c"] + n) % 4)
        v.wait_ge(k.group_rstd_ready, GROUP_MS["c"] + n + 1)
        n += 1

        def root(m):
            return k.group_rstd[:, col + m:col + m + 1]

        t = i % 2
        if kind == "low":
            low = b.low[:, i, :]
            v.tensor_scalar(low[:, 0:C_Q_LORA], bank[:, 0:C_Q_LORA], root(0), None, ALU.mult)
            v.tensor_scalar(low[:, C_Q_LORA:C_Q_LORA + C_KV_LORA], bank[:, C_Q_LORA:C_Q_LORA + C_KV_LORA], root(1), None, ALU.mult)
            rope_one(k, v, steps, bank[:, C_Q_LORA + C_KV_LORA:C_HEAD_IN], root(2), b.k_tables[:, 2 * t, :],
                     b.k_tables[:, 2 * t + 1, :], b, low[:, 3 * P:3 * P + C_ROPE])
            k.release(v.tensor_copy(low[:, 3 * P + C_ROPE:4 * P], low[:, 3 * P:3 * P + C_ROPE]), name)
            k.wait_released(v, name)
            v.sem_inc(k.c_low_staged, 1)
        if kind == "q":
            q = b.q[:, t, :]
            if i < 2:
                k.wait_filled(v, ("c", "lowturn", 1))
            else:
                k.wait_filled(v, ("c", "qturn", i - 2))
            for m in range(2):
                v.scalar_tensor_tensor(q[:, P * m:P * (m + 1)], bank[:, C_QK * m:C_QK * m + C_NOPE], root(2 * m),
                                       k.wide("c_q_norm_g", 0, C_NOPE), ALU.mult, ALU.mult)
                rope_one(k, v, steps, bank[:, C_QK * m + C_NOPE:C_QK * (m + 1)], root(2 * m + 1), b.q_tables[:, 2 * t, :],
                         b.q_tables[:, 2 * t + 1, :], b, q[:, 2 * P + C_ROPE * m:2 * P + C_ROPE * (m + 1)])
            v.sem_inc(k.freed[k.banks.at[name][0]], 1)
            v.sem_inc(k.c_q_staged, 1)
        if kind == "kv":
            kk = b.k[:, t, :]
            if i >= 2:
                k.wait_filled(v, ("c", "kturn", i - 2))
            v.wait_ge(k.c_v_ready, i + 1)
            for m in range(2):
                last = v.scalar_tensor_tensor(kk[:, P * m:P * (m + 1)], bank[:, 256 * m:256 * m + C_NOPE], root(m),
                                              k.wide("c_k_norm_g", 0, C_NOPE), ALU.mult, ALU.mult)
            k.release(last, name)
            k.wait_released(v, name)
            v.sem_inc(k.c_k_staged, 1)
        v.sem_inc(k.c_roots_used, 1)
    attention_vector(k, v, "c", b)


def rope_one(k, v, steps, bank, root, cos, sin, b, out):
    half = C_ROPE // 2
    d, s = b.direct[:, 0:C_ROPE], b.swapped[:, 0:C_ROPE]
    v.scalar_tensor_tensor(d, bank, root, cos, ALU.mult, ALU.mult).then_inc(steps.sem, 1)
    v.scalar_tensor_tensor(s[:, 0:half], bank[:, half:], root, sin[:, 0:half], ALU.mult, ALU.mult).then_inc(steps.sem, 1)
    v.scalar_tensor_tensor(s[:, half:], bank[:, 0:half], root, sin[:, half:], ALU.mult, ALU.mult).then_inc(steps.sem, 1)
    steps.done += 3
    v.wait_ge(steps.sem, steps.done)
    steps.link(v.tensor_tensor(out, d, s, ALU.add))


def c_pool(k, pool):
    n = GROUP_MS["c"]
    for kind, i in c_order():
        if kind in ("low", "q", "kv"):
            pool.wait_ge(k.group_ms_ready, n + 1)
            m = {"low": 3, "q": 4, "kv": 2}[kind]
            col = 8 * (n % 4)
            inverse_root(k, pool, k.group_ms[:, col:col + m], k.group_rstd[:, col:col + m], k.group_rstd_ready)
            n += 1



def h_buffers(k):
    k.reset_arena()
    b = Buffers()
    b.qT = k.carve(H_HEADS // 2, SEQ)
    b.kT = k.carve(H_KV_HEADS, SEQ)
    b.v = k.carve(TILES, H_KV_HEADS * H_DIM)
    b.q = k.carve(TILES, 512)
    b.k = k.carve(TILES, P)
    b.squares = k.carve(2, 512)
    b.y = k.carve(2, 512)
    b.s = k.carve(2, SEQ)
    b.shift = k.carve(2, 2 * SEQ)
    b.padded = k.carve(4, H_TAPS - 1 + SEQ)
    b.conv = k.carve(4, SEQ)
    b.raw = k.carve(512)
    b.staged0 = STAGED["h"][0]
    return b


def h_groups(kind):
    return (H_HEADS, "hy_q_gain_2") if kind == "q" else (H_KV_HEADS, "hy_k_gain_2")


def h_tensor(k, pe, u):
    b = h_buffers(k)
    for kind, i in h_order():
        name = ("h", kind, i)
        if kind == "q":
            product(k, pe, name, u, k.hT, i, KC, 512)
        if kind == "kv":
            product(k, pe, name, u + 1, k.hT, i, KC, 256, 0, 256)
        if kind in ("shift", "value", "gate"):
            channel_product(k, pe, name, u + 2 + ("shift", "value", "gate").index(kind), 2 * P * i)
        if kind == "qturn":
            pe.wait_ge(k.h_q_staged, i + 1)
            k.take(pe, name)
            for c in range(4):
                last = pe.transpose(k.bank(name)[:, P * c:P * (c + 1)], b.q[:, i, P * c:P * (c + 1)], k.ident)
            k.fill(last, name)
        if kind == "kturn":
            pe.wait_ge(k.h_k_staged, i + 1)
            k.take(pe, name)
            k.fill(pe.transpose(k.bank(name)[:, 0:P], b.k[:, i, :], k.ident), name)
    for kind, i in h_order():
        k.wait_released(pe, ("h", kind, i))
    attention_tensor(k, pe, "h", b, u + 5)


def h_scalar(k, act):
    b = h_buffers(k)
    act.wait_ge(k.cleared, 4)
    n = GROUP_MS["h"]
    for kind, i in h_order():
        name = ("h", kind, i)
        bank = k.bank(name)
        k.wait_filled(act, name)
        tile = slice(P * (i % 2), P * (i % 2 + 1))
        if kind in ("q", "kv"):
            groups, _ = h_groups(kind)
            if kind == "kv":
                act.wait_ge(k.group_ms_ready, n - 1)
                act.activation(b.v[:, i, :], bank[:, groups * H_DIM:2 * groups * H_DIM], ACT.Copy)
            act.activation(b.squares[:, i, 0:groups * H_DIM], bank[:, 0:groups * H_DIM], ACT.Square,
                           scale=float(H_DIM) ** -0.5).then_inc(k.group_squares, 1)
            n += 1
        if kind == "shift":
            k.release(act.activation(b.shift[:, i, :], bank, ACT.Copy), name)
        if kind == "qturn":
            k.release(act.activation(b.qT[:, :, tile], bank.rearrange("p (c q) -> p c q", c=4), ACT.Copy), name)
        if kind == "kturn":
            act.activation(b.kT[0:H_DIM, 0, tile], bank[0:H_DIM, 0:P], ACT.Copy)
            k.release(act.activation(b.kT[H_DIM:P, 1, tile], bank[H_DIM:P, 0:P], ACT.Copy), name)
    attention_scalar(k, act, "h", b)


def h_vector(k, v):
    b = h_buffers(k)
    steps = k.engine_steps["dve"]
    pad = H_TAPS - 1
    v.memset(b.kT[:, :, :], 0.0).then_inc(k.cleared, 1)
    steps.link(v.memset(b.padded[:, :, 0:pad], 0.0))
    n = 0
    for kind, i in h_order():
        name = ("h", kind, i)
        bank = k.bank(name)
        if kind in ("q", "kv"):
            groups, gain = h_groups(kind)
            count = GROUP_MS["h"] + n
            col = 8 * n
            v.wait_ge(k.group_squares, 16 + n + 1)
            v.tensor_reduce(k.group_ms[:, col:col + groups], b.squares[:, i, 0:groups * H_DIM].rearrange("p (g d) -> p g d", g=groups),
                            AX, ALU.add).then_inc(k.group_ms_ready, 1)
            v.wait_ge(k.group_rstd_ready, count + 1)
            rstd = over_columns(k.group_rstd[:, col:col + groups], H_DIM)
            raw = b.raw[:, 0:groups * H_DIM].rearrange("p (g d) -> p g d", g=groups)
            k.release(v.tensor_tensor(raw, bank[:, 0:groups * H_DIM].rearrange("p (g d) -> p g d", g=groups), rstd, ALU.mult), name)
            k.wait_released(v, name)
            gains = over_groups(k.wide(gain), groups)
            if kind == "q":
                for side in range(2):
                    out = b.q[:, i, :].rearrange("p (j s d) -> p j s d", s=2, d=H_DIM)[:, :, side, :]
                    heads = slice(4 * side, 4 * side + 4)
                    steps.link(v.tensor_tensor(out, raw[:, heads, :], over_groups(k.wide(gain), 4), ALU.mult))
                v.sem_inc(k.h_q_staged, 1)
            else:
                v.tensor_tensor(b.k[:, i, :].rearrange("p (g d) -> p g d", g=groups), raw, gains, ALU.mult).then_inc(k.h_k_staged, 1)
            n += 1
        if kind == "value":
            k.wait_released(v, ("h", "shift", i))
            k.wait_filled(v, name)
            k.release(v.tensor_tensor(b.padded[:, 2 * i:2 * i + 2, pad:], bank.rearrange("p (c t) -> p c t", c=2),
                                      b.shift[:, i, :].rearrange("p (c t) -> p c t", c=2), ALU.mult), name)
            k.wait_released(v, name)
            for tap in range(H_TAPS):
                for c in (2 * i, 2 * i + 1):
                    window, weight = b.padded[:, c, tap:tap + SEQ], k.column("hy_conv_w_2", c, tap)
                    if tap == 0:
                        steps.link(v.tensor_scalar(b.conv[:, c, :], window, weight, None, ALU.mult))
                    else:
                        steps.link(v.scalar_tensor_tensor(b.conv[:, c, :], window, weight, b.conv[:, c, :], ALU.mult, ALU.add))
        if kind == "gate":
            k.wait_filled(v, name)
            k.release(v.tensor_tensor(k.yT[:, 4 + 2 * i:6 + 2 * i, :], bank.rearrange("p (c t) -> p c t", c=2),
                                      b.conv[:, 2 * i:2 * i + 2, :], ALU.mult), name)
    attention_vector(k, v, "h", b)


def h_pool(k, pool):
    for n in range(4):
        groups = H_HEADS if n < 2 else H_KV_HEADS
        pool.wait_ge(k.group_ms_ready, GROUP_MS["h"] + n + 1)
        inverse_root(k, pool, k.group_ms[:, 8 * n:8 * n + groups], k.group_rstd[:, 8 * n:8 * n + groups], k.group_rstd_ready)



def ffn_buffers(k):
    k.reset_arena()
    b = Buffers()
    b.silu = k.carve(TILES, FF_STEP)
    b.hidden = k.carve(TILES, FF_STEP)
    b.hiddenT = k.carve(TILES, 4 * P)
    return b


def ffn_tensor(k, pe, u):
    b = ffn_buffers(k)
    for kind, j, t in ffn_order():
        name = ("ffn", kind, j, t)
        if kind in ("gate", "up"):
            product(k, pe, name, u + 3 * j + (kind == "up"), k.hT, t, KC, FF_STEP)
        if kind == "turn":
            k.wait_released(pe, ("ffn", "up", j, t))
            k.take(pe, name)
            for c in range(4):
                last = pe.transpose(k.bank(name)[:, P * c:P * (c + 1)], b.hidden[:, t, P * c:P * (c + 1)], k.ident)
            k.fill(last, name)
        if kind == "down":
            k.wait_unit(pe, u + 3 * j + 2)
            w = k.unit(u + 3 * j + 2, 4)
            for n in range(2):
                for t in range(TILES):
                    out = ("ffn", "out", 2 * n + t)
                    if j == 0:
                        k.take(pe, out)
                    k.wait_released(pe, ("ffn", "turn", j, t))
                    for c in range(4):
                        last = pe.matmul(k.bank(out), b.hiddenT[:, t, P * c:P * (c + 1)], w[:, c, 512 * n:512 * (n + 1)],
                                         start=(j == 0 and c == 0), stop=(j == FF_STEPS - 1 and c == 3))
                    if j == FF_STEPS - 1:
                        k.fill(last, out)
            if j < FF_STEPS - 1:
                last.then_inc(k.down_done, 1)


def ffn_scalar(k, act):
    b = ffn_buffers(k)
    for kind, j, t in ffn_order():
        name = ("ffn", kind, j, t)
        if kind == "gate":
            if j > 0:
                k.wait_released(act, ("ffn", "up", j - 1, t))
            k.wait_filled(act, name)
            k.release(act.activation(b.silu[:, t, :], k.bank(name), ACT.Silu), name)
        if kind == "turn":
            if j > 0:
                act.wait_ge(k.down_done, j)
            k.wait_filled(act, name)
            k.release(act.activation(b.hiddenT[:, t, :], k.bank(name), ACT.Copy), name)


def ffn_vector(k, v):
    b = ffn_buffers(k)
    for kind, j, t in ffn_order():
        if kind == "up":
            name = ("ffn", kind, j, t)
            k.wait_filled(v, name)
            k.wait_released(v, ("ffn", "gate", j, t))
            if j > 0:
                k.wait_filled(v, ("ffn", "turn", j - 1, t))
            k.release(v.tensor_tensor(b.hidden[:, t, :], k.bank(name), b.silu[:, t, :], ALU.mult), name)
    out_vector(k, v, "ffn")



def r_buffers(k):
    k.reset_arena()
    b = Buffers()
    b.padded = k.carve(KC, R_TAPS - 1 + SEQ)
    b.conv = k.carve(KC, SEQ)
    b.keep = k.carve(KC, SEQ)
    b.take = k.carve(KC, SEQ)
    b.tanh = k.carve(KC, SEQ)
    b.decay = k.carve(KC, SEQ)
    b.root = k.h[:, :, :].rearrange("p t d -> p (t d)").rearrange("p (c n) -> p c n", c=KC)
    return b


def r_unit(kind, i):
    return {"x": i // 2, "y": 2 + 2 * (i // 2), "gates": 3}[kind]


def r_tensor(k, pe, u):
    b = r_buffers(k)
    for kind, i in r_order():
        name = ("r", kind, i)
        if kind in ("x", "y"):
            channel_product(k, pe, name, u + r_unit(kind, i), 2 * P * (i % 2))
        else:
            k.wait_unit(pe, u + 3)
            pe.wait_ge(k.gates_ready, 16)
            pe.wait_ge(k.r_conv_ready, i + 1)
            k.take(pe, name)
            w = k.ring[:, (u + 3) % RING, 0:2 * R_HEADS * P].rearrange("p (g h n) -> p g h n", g=2, h=R_HEADS)
            for g in range(2):
                last = pe.matmul(k.bank(name)[:, SEQ * g:SEQ * (g + 1)], w[:, g, i, :], b.conv[:, i, :], start=True, stop=True)
            k.fill(last, name)
    pe.wait_ge(k.r_mixed, KC)
    out_tensor(k, pe, "r", u + 5)


def r_scalar(k, act):
    b = r_buffers(k)
    for kind, i in r_order():
        name = ("r", kind, i)
        bank = k.bank(name)
        if kind == "x":
            k.wait_filled(act, name)
            k.release(act.activation(b.padded[:, 2 * i:2 * i + 2, R_TAPS - 1:], bank.rearrange("p (c t) -> p c t", c=2), ACT.Copy), name)
        if kind == "gates":
            k.wait_filled(act, name)
            act.activation(b.keep[:, i, :], bank[:, 0:SEQ], ACT.Sigmoid, bias=k.column("rg_gate_a_b_2", i))
            k.release(act.activation(b.take[:, i, :], bank[:, SEQ:2 * SEQ], ACT.Sigmoid, bias=k.column("rg_gate_x_b_2", i)), name)
        if kind == "y":
            k.wait_filled(act, name)
            k.release(act.activation(k.yT[:, 2 * i:2 * i + 2, :], bank.rearrange("p (c t) -> p c t", c=2), ACT.Gelu_apprx_tanh), name)
    for h in range(R_HEADS):
        k.wait_released(act, ("r", "gates", h))
    act.wait_ge(k.r_decay_ready, 1)
    for c in range(KC):
        act.activation(b.tanh[:, c, :], b.keep[:, c, :], ACT.Tanh, scale=k.decay[:, c:c + 1])
        act.activation(b.decay[:, c, :], b.keep[:, c, :], ACT.Exp, scale=k.negdecay[:, c:c + 1]).then_inc(k.r_decays, 1)
    for c in range(KC):
        act.wait_ge(k.r_root_in, c + 1)
        act.activation(b.root[:, c, :], b.tanh[:, c, :], ACT.Sqrt).then_inc(k.r_root_ready, 1)


def r_vector(k, v):
    b = r_buffers(k)
    steps = k.engine_steps["dve"]
    pad = R_TAPS - 1
    v.tensor_scalar(k.negdecay, k.decay, -1.0, None, ALU.mult).then_inc(k.r_decay_ready, 1)
    steps.link(v.memset(b.padded[:, :, 0:pad], 0.0))
    for pair in range(4):
        k.wait_released(v, ("r", "x", pair))
        for tap in range(R_TAPS):
            for c in (2 * pair, 2 * pair + 1):
                window, weight = b.padded[:, c, tap:tap + SEQ], k.column("rg_conv_w_2", c, tap)
                if tap == 0:
                    last = v.tensor_scalar(b.conv[:, c, :], window, weight, k.column("rg_conv_b_2", c), ALU.mult, ALU.add)
                else:
                    last = v.scalar_tensor_tensor(b.conv[:, c, :], window, weight, b.conv[:, c, :], ALU.mult, ALU.add)
                if tap == R_TAPS - 1:
                    last.then_inc(k.r_conv_ready, 1)
                else:
                    steps.link(last)
    for c in range(KC):
        v.wait_ge(k.r_decays, c + 1)
        square = b.padded[:, c, 0:SEQ]
        steps.link(v.tensor_tensor(square, b.decay[:, c, :], b.decay[:, c, :], ALU.mult))
        v.scalar_tensor_tensor(b.tanh[:, c, :], square, 1.0, b.tanh[:, c, :], ALU.add, ALU.mult).then_inc(k.r_root_in, 1)
        v.tensor_tensor(b.conv[:, c, :], b.conv[:, c, :], b.take[:, c, :], ALU.mult).then_inc(steps.sem, 1)
        steps.done += 1
    v.wait_ge(steps.sem, steps.done)
    for h in range(4):
        k.wait_released(v, ("r", "y", h))
    for c in range(KC):
        v.wait_ge(k.r_root_ready, c + 1)
        steps.link(v.memset(b.root[:, c, 0:1], 1.0))
        steps.link(v.tensor_tensor(b.conv[:, c, :], b.conv[:, c, :], b.root[:, c, :], ALU.mult))
        steps.link(v.tensor_tensor_scan(b.padded[:, c, 0:SEQ], b.decay[:, c, :], b.conv[:, c, :], 0.0, ALU.mult, ALU.add))
        v.tensor_tensor(k.yT[:, c, :], k.yT[:, c, :], b.padded[:, c, 0:SEQ], ALU.mult).then_inc(k.r_mixed, 1)
    out_vector(k, v, "r")



SLOTS = P
CAP = float(SLOTS)
N_WORK = 1 + N_EXPERTS
DOWN_OF_FFN = FF_STEPS - 1


def moe_buffers(k):
    k.reset_arena()
    b = Buffers()
    b.tokens = k.carve(KC, SLOTS)
    b.placed = k.carve(TILES, SLOTS)
    b.unplaced = k.carve(TILES, P)
    b.silu = k.carve(2, FF_STEP)
    b.hidden = k.carve(2, FF_STEP)
    b.hiddenT = k.carve(2, 4 * P)
    b.out = k.carve(D)
    return b


def short_turns(t):
    return (MOE_SHORT // 4) * t


def rounds(k, eng, one_round):
    with eng.Fori(0, N_EXPERTS) as t:
        one_round(t, t, 0)
    more_rounds(k, eng, one_round)


def more_rounds(k, eng, one_round):
    eng.wait_ge(k.work_ready, 1)
    n = eng.value_load(k.work[0:1, 0:1], min_val=0, max_val=N_EXPERTS)
    with eng.If(n > 0):
        with eng.Fori(0, n) as r:
            expert = None
            if eng in (k.nc.sync, k.nc.vector):
                expert = eng.value_load(k.work[0:1, bass.ds(r + 1, 1)], min_val=0, max_val=N_EXPERTS - 1)
            one_round(r + N_EXPERTS, expert, 1)
    with eng.Else():
        pass
    return n


def moe_load(k, sp, t, expert, units):
    names = [(kind, j) for j in range(FF_STEPS) for kind in ("gate", "up", "down")]
    for i in units:
        kind, j = names[i]
        before, of = (names[i - RING], t) if i >= RING else (names[i + UNITS_PER_EXPERT - RING], t - 1)
        if before[0] == "down":
            if before[1] < FF_STEPS - 1:
                sp.wait_ge(k.down_done, of * (FF_STEPS - 1) + DOWN_OF_FFN + before[1] + 1)
            else:
                k.wait_filled(sp, ("moe", "expert", 1), of)
        else:
            k.wait_filled(sp, ("moe",) + before, short_turns(of))
        moe_unit(k, sp, i, kind, j, expert)


def moe_unit(k, sp, i, kind, j, expert):
    slot = i % RING
    experts = k.w[f"moe_w_{kind}_2"][0]
    if isinstance(expert, int):
        a = experts[expert]
    else:
        a = experts[bass.ds(expert, 1)].rearrange("e a b -> (e a) b")
    if kind == "down":
        src, kc = a[FF_STEP * j:FF_STEP * (j + 1), :], FF_STEP // P
    else:
        src, kc = a[:, FF_STEP * j:FF_STEP * (j + 1)], KC
    dst = k.ring[:, slot, :].rearrange("p (c n) -> p c n", c=kc)
    sp.dma_start(dst, src.rearrange("(c p) n -> p c n", p=P)).then_inc(k.landed[slot], 16)


def moe_sync(k, sp):
    units = weight_units(k)
    names = [(kind, j) for j in range(FF_STEPS) for kind in ("gate", "up", "down")]
    for i in range(RING):
        sync_unit_used(k, sp, units[len(units) - RING + i][2])
        moe_unit(k, sp, i, *names[i], 0)
    with sp.Fori(0, N_EXPERTS - 1) as t:
        moe_load(k, sp, t, t, range(RING, UNITS_PER_EXPERT))
        moe_load(k, sp, t + 1, t + 1, range(RING))
    moe_load(k, sp, N_EXPERTS - 1, N_EXPERTS - 1, range(RING, UNITS_PER_EXPERT))
    k.more = more_rounds(k, sp, lambda t, expert, _: moe_load(k, sp, t, expert, range(UNITS_PER_EXPERT)))


def moe_wait_all(k, sp):
    k.wait_released(sp, ("moe", "scatter", 3), short_turns(k.more + N_EXPERTS - 1))


def moe_tensor(k, pe, _):
    b = moe_buffers(k)
    pe.wait_ge(k.router_landed, 16)
    k.take(pe, "logits")
    for t in range(TILES):
        for c in range(KC):
            last = pe.matmul(k.bank("logits")[:, 8 * t:8 * t + 8], k.hT[:, c, P * t:P * (t + 1)], k.router[:, c, :],
                             start=(c == 0), stop=(c == KC - 1))
    k.fill(last, "logits")
    pe.wait_ge(k.routed, 1)
    k.take(pe, "places")
    bank, (chosen0, chosen1) = k.bank("places"), (k.chosen[:, 0, :], k.chosen[:, 1, :])
    pe.matmul(bank[:, 0:8], k.before, chosen0, start=True, stop=True)
    pe.matmul(bank[:, 8:16], k.ones, chosen0, start=True, stop=False)
    pe.matmul(bank[:, 8:16], k.before, chosen1, start=False, stop=True)
    pe.matmul(bank[:, 16:24], k.ones, chosen0, start=True, stop=False)
    k.fill(pe.matmul(bank[:, 16:24], k.ones, chosen1, start=False, stop=True), "places")
    rounds(k, pe, lambda t, _, __: moe_round_tensor(k, pe, b, t))


def moe_round_tensor(k, pe, b, t):
    more = short_turns(t)
    for kind, i in moe_order():
        name = ("moe", kind, i)
        if kind == "gather":
            if i == 0:
                pe.wait_ge(k.placed, 2 * t + 2)
            k.take(pe, name, more)
            for c in range(4 * i, 4 * i + 4):
                for tile in range(TILES):
                    last = pe.matmul(k.bank(name)[:, P * (c % 4):P * (c % 4 + 1)], k.h[:, tile, P * c:P * (c + 1)],
                                     b.placed[:, tile, :], start=(tile == 0), stop=(tile == TILES - 1))
            k.fill(last, name)
        if kind == "unplace":
            k.take(pe, name, more)
            for tile in range(TILES):
                last = pe.transpose(k.bank(name)[:, P * tile:P * (tile + 1)], b.placed[:, tile, :], k.ident)
            k.fill(last, name)
        if kind in ("gate", "up"):
            if kind == "gate" and i == 0:
                for g in range(2):
                    k.wait_released(pe, ("moe", "gather", g), more)
            u = 3 * i + (kind == "up")
            pe.wait_ge(k.landed[u % RING], moe_landed(t, u))
            k.take(pe, name, more)
            for c in range(KC):
                last = pe.matmul(k.bank(name), b.tokens[:, c, :], k.unit(u)[:, c, :], start=(c == 0), stop=(c == KC - 1))
            k.fill(last, name)
        if kind == "turn":
            k.wait_released(pe, ("moe", "up", i), more)
            k.take(pe, name, more)
            for c in range(4):
                last = pe.transpose(k.bank(name)[:, P * c:P * (c + 1)], b.hidden[:, i % 2, P * c:P * (c + 1)], k.ident)
            k.fill(last, name)
        if kind == "down":
            u = 3 * i + 2
            pe.wait_ge(k.landed[u % RING], moe_landed(t, u))
            k.wait_released(pe, ("moe", "turn", i), more)
            w = k.unit(u, 4)
            for half in range(2):
                out = ("moe", "expert", half)
                if i == 0:
                    k.take(pe, out, t)
                for c in range(4):
                    last = pe.matmul(k.bank(out), b.hiddenT[:, i % 2, P * c:P * (c + 1)], w[:, c, 512 * half:512 * (half + 1)],
                                     start=(i == 0 and c == 0), stop=(i == FF_STEPS - 1 and c == 3))
                if i == FF_STEPS - 1:
                    k.fill(last, out)
            if i < FF_STEPS - 1:
                last.then_inc(k.down_done, 1)
        if kind == "scatter":
            half, tile = i // 2, i % 2
            if i == 0:
                k.wait_released(pe, ("moe", "unplace", 0), more)
            k.wait_released(pe, ("moe", "expert", half), t)
            k.take(pe, name, more)
            k.fill(pe.matmul(k.bank(name), b.unplaced[:, tile, :], b.out[:, 512 * half:512 * (half + 1)], start=True, stop=True), name)


def moe_landed(t, u):
    uses = len(FIRST_UNITS_BEFORE_MOE) // RING + u // RING
    return t * (16 * UNITS_PER_EXPERT // RING) + 16 * (uses + 1)


FIRST_UNITS_BEFORE_MOE = range(70)


def moe_scalar(k, act):
    b = moe_buffers(k)
    act.wait_ge(k.gap_ready, 1)
    act.activation(k.both, k.gap, ACT.Exp).then_inc(k.share_ready, 1)

    def one_round(t, _, __):
        more = short_turns(t)
        for kind, i in moe_order():
            name = ("moe", kind, i)
            if kind == "gate":
                if i >= 2:
                    k.wait_released(act, ("moe", "up", i - 2), more)
                k.wait_filled(act, name, more)
                k.release(act.activation(b.silu[:, i % 2, :], k.bank(name), ACT.Silu), name)
            if kind == "turn":
                k.wait_filled(act, name, more)
                k.release(act.activation(b.hiddenT[:, i % 2, :], k.bank(name), ACT.Copy), name)
        k.wait_filled(act, ("moe", "expert", 0), t)
        k.release(act.activation(b.out[:, 0:512], k.bank(("moe", "expert", 0)), ACT.Copy), ("moe", "expert", 0))

    rounds(k, act, one_round)


def moe_vector(k, v):
    b = moe_buffers(k)
    steps = k.engine_steps["dve"]
    k.wait_filled(v, "logits")
    k.release(v.tensor_copy(k.logits, k.bank("logits")[:, 0:TILES * 8]), "logits")
    k.wait_released(v, "logits")
    for t in range(TILES):
        logits, ordered = k.logits[:, 8 * t:8 * t + 8], k.sorted[:, 8 * t:8 * t + 8]
        steps.link(v.max(ordered, logits))
        steps.link(v.max_index(k.best[:, t, :], ordered, logits))
        steps.link(v.tensor_copy(k.first[:, 2 * t:2 * t + 2], k.best[:, t, 0:2]))
        steps.link(v.tensor_tensor(k.gap[:, t:t + 1], ordered[:, 1:2], ordered[:, 0:1], ALU.subtract))
    v.sem_inc(k.gap_ready, 1)
    v.wait_ge(k.share_ready, 1)
    one_hot, other = k.over[:, 0:8], k.over[:, 8:16]
    for t in range(TILES):
        share = k.share[:, 2 * t:2 * t + 2]
        steps.link(v.tensor_scalar(share[:, 0:1], k.both[:, t:t + 1], 1.0, None, ALU.add))
        steps.link(v.reciprocal(share[:, 0:1], share[:, 0:1]))
        steps.link(v.tensor_tensor(share[:, 1:2], share[:, 0:1], k.both[:, t:t + 1], ALU.mult))
        experts = k.count[:, 0:8]
        steps.link(v.tensor_scalar(one_hot, experts, k.first[:, 2 * t:2 * t + 1], None, ALU.is_equal))
        steps.link(v.tensor_scalar(other, experts, k.first[:, 2 * t + 1:2 * t + 2], None, ALU.is_equal))
        steps.link(v.tensor_tensor(k.chosen[:, t, :], one_hot, other, ALU.add))
        steps.link(v.tensor_scalar(one_hot, one_hot, share[:, 0:1], None, ALU.mult))
        steps.link(v.scalar_tensor_tensor(k.weight[:, t, :], other, share[:, 1:2], one_hot, ALU.mult, ALU.add))
    v.sem_inc(k.routed, 1)
    k.wait_filled(v, "places")
    bank = k.bank("places")
    for t in range(TILES):
        steps.link(v.scalar_tensor_tensor(k.place[:, 0, t, :], bank[:, 8 * t:8 * t + 8], 1.0, k.chosen[:, t, :], ALU.add, ALU.mult))
        steps.link(v.tensor_scalar(k.place[:, 0, t, :], k.place[:, 0, t, :], -1.0, None, ALU.add))
        steps.link(v.tensor_scalar(k.place[:, 1, t, :], k.place[:, 0, t, :], -CAP, None, ALU.add))
    over, upto, match = k.over[:, 0:8], k.over[:, 8:16], k.over[:, 16:24]
    listed = k.over[:, 24:24 + N_WORK]
    steps.link(v.tensor_scalar(over, bank[:, 16:24], CAP, None, ALU.is_gt))
    v.sem_inc(k.freed[k.banks.at["places"][0]], 1)
    steps.link(v.tensor_tensor_scan(upto, k.ones[:, 0:8], over, 0.0, ALU.mult, ALU.add))
    steps.link(v.tensor_copy(listed[:, 0:1], upto[:, 7:8]))
    for r in range(N_EXPERTS):
        steps.link(v.scalar_tensor_tensor(match, upto, float(r + 1), over, ALU.is_equal, ALU.mult))
        steps.link(v.tensor_tensor_reduce(match, match, k.count[:, 0:8], 1.0, 0.0, ALU.mult, ALU.add, listed[:, r + 1:r + 2]))
    v.tensor_copy(k.work[:, 0:N_WORK], listed).then_inc(k.work_ready, 1)

    def one_round(t, expert, second):
        more = short_turns(t)
        for tile in range(TILES):
            v.tensor_scalar(b.placed[:, tile, :], k.count, k.place[:, second, tile, bass.ds(expert, 1)], None, ALU.is_equal)\
             .then_inc(k.placed, 1)
        for kind, i in moe_order():
            name = ("moe", kind, i)
            if kind == "gather":
                k.wait_filled(v, name, more)
                r = VECTOR_ROWS["norm_ffn_2"][0] + 1
                k.release(v.tensor_tensor(b.tokens[:, 4 * i:4 * i + 4, :], k.bank(name).rearrange("p (c s) -> p c s", c=4),
                                          over_columns(k.vecs[:, 4 * i:4 * i + 4, r], SLOTS), ALU.mult), name)
            if kind == "unplace":
                k.wait_filled(v, name, more)
                k.release(v.tensor_copy(b.unplaced[:, :, :], k.bank(name)[:, 0:TILES * P].rearrange("p (t q) -> p t q", t=TILES)), name)
            if kind == "up":
                k.wait_filled(v, name, more)
                k.wait_released(v, ("moe", "gate", i), more)
                if i >= 2:
                    k.wait_filled(v, ("moe", "turn", i - 2), more)
                k.release(v.tensor_tensor(b.hidden[:, i % 2, :], k.bank(name), b.silu[:, i % 2, :], ALU.mult), name)
            if kind == "scatter":
                if i == 0:
                    k.wait_filled(v, ("moe", "expert", 1), t)
                    k.release(v.tensor_copy(b.out[:, 512:1024], k.bank(("moe", "expert", 1))), ("moe", "expert", 1))
                half, tile = i // 2, i % 2
                k.wait_filled(v, name, more)
                part = k.x[:, tile, 512 * half:512 * (half + 1)]
                k.release(v.scalar_tensor_tensor(part, k.bank(name), k.weight[:, tile, bass.ds(expert, 1)], part,
                                                 ALU.mult, ALU.add), name)

    rounds(k, v, one_round)


LAYERS = ("a0", "b", "c", "a1", "h", "ffn", "r", "moe")


def build(nc, w, consts, const_at, out, layers=LAYERS):
    with ExitStack() as ctx:
        k = Core(nc, ctx, w, consts, const_at, out)
        block = ctx.enter_context(nc.Block())
        units = first_units()

        @block.sync
        def _(sp):
            sync_weights(k, sp)
            if "moe" in layers:
                moe_sync(k, sp)
            store(k, sp, layers)

        @block.tensor
        def _(pe):
            setup_tensor(k, pe)
            for n, layer in enumerate(layers):
                norm_tensor(k, pe, n)
                if layer[0] == "a":
                    a_tensor(k, pe, int(layer[1]), units[layer])
                else:
                    {"b": b_tensor, "c": c_tensor, "h": h_tensor, "ffn": ffn_tensor, "r": r_tensor, "moe": moe_tensor}[layer](k, pe, units.get(layer))

        @block.vector
        def _(v):
            k.engine_steps["dve"] = Steps(v, k.own["dve"])
            setup_vector(k, v)
            x_from = []
            for n, layer in enumerate(layers):
                norm_vector(k, v, n, x_from)
                if layer[0] == "a":
                    a_vector(k, v, int(layer[1]))
                else:
                    {"b": b_vector, "c": c_vector, "h": h_vector, "ffn": ffn_vector, "r": r_vector, "moe": moe_vector}[layer](k, v)
                x_from = out_names(layer)

        @block.scalar
        def _(act):
            k.engine_steps["act"] = Steps(act, k.own["act"])
            setup_loads(k, act)
            setup_scalar(k, act)
            x_from = []
            for n, layer in enumerate(layers):
                norm_scalar(k, act, n, x_from)
                if layer[0] == "a":
                    a_scalar(k, act, int(layer[1]))
                else:
                    {"b": b_scalar, "c": c_scalar, "h": h_scalar, "ffn": ffn_scalar, "r": r_scalar, "moe": moe_scalar}[layer](k, act)
                x_from = out_names(layer)

        @block.gpsimd
        def _(pool):
            k.engine_steps["pool"] = Steps(pool, k.own["pool"])
            for n, layer in enumerate(layers):
                if n == 0:
                    pool.wait_ge(k.const_landed, 16)
                norm_pool(k, pool, n)
                if layer[0] == "a":
                    a_pool(k, pool, int(layer[1]))
                elif layer in ("c", "h"):
                    {"c": c_pool, "h": h_pool}[layer](k, pool)


def store(k, sp, layers):
    if layers[-1] == "moe":
        moe_wait_all(k, sp)
    else:
        for name in out_names(layers[-1]):
            k.wait_released(sp, name)
    sp.dma_start(k.out[0].rearrange("(t p) d -> p t d", p=P), k.x[:, :, :]).then_inc(k.stored, 16)
    sp.wait_ge(k.stored, 16)


INPUTS = tuple(VECTOR_ROWS) + tuple(SPREAD) + (
    "x", "a_w_in", "a_w_out", "b_w_in", "b_w_out", "c_w_in", "c_w_uq", "c_w_ukv", "c_w_out", "hy_w_in_2", "hy_w_out_2",
    "rg_w_in_2", "rg_gate_a_w_2", "rg_gate_x_w_2", "rg_w_out_2", "ffn_w_gate_2", "ffn_w_up_2", "ffn_w_down_2",
    "moe_router_2", "moe_w_gate_2", "moe_w_up_2", "moe_w_down_2",
)


def kernel(**inputs):
    import concourse.bacc as bacc
    from concourse.bass_utils import run_bass_kernel_spmd

    nc = bacc.Bacc("TRN2", target_bir_lowering=False, num_devices=1)
    arrays, w = {}, {}
    for name in INPUTS:
        a = np.ascontiguousarray(inputs[name])
        arrays[f"in_{name}"] = a
        w[name] = nc.dram_tensor(f"in_{name}", a.shape, mybir.dt.from_np(a.dtype), kind="ExternalInput").ap()
    consts, const_at = constants()
    arrays["in_constants"] = consts
    const_ap = nc.dram_tensor("in_constants", consts.shape, F32, kind="ExternalInput").ap()
    out = nc.dram_tensor("out_x", (1, SEQ, D), F32, kind="ExternalOutput").ap()
    build(nc, w, const_ap, const_at, out)
    results = run_bass_kernel_spmd(nc, [arrays], core_ids=[0])
    return results.results[0]["out_x"]
```

```python
from contextlib import ExitStack

import numpy as np

import concourse.bass as bass
from concourse import mybir

ALU = mybir.AluOpType
ACT = mybir.ActivationFunctionType
F32 = mybir.dt.float32
F32R = mybir.dt.float32r
I32 = mybir.dt.int32
U32 = mybir.dt.uint32
AX = mybir.AxisListType.X

P = 128
SEQ = 256
TILES = SEQ // P
D = 1024
KC = D // P
EPS = 1e-6
MASKED = -1e30

A_HEADS, A_QK, A_V = 8, 64, 128
A_LAMBDA_INIT = (0.8 - 0.6 * float(np.exp(-0.3 * 0)), 0.8 - 0.6 * float(np.exp(-0.3 * 3)))
CHUNK = 64
CONV_TAPS = 31
C_HEADS, C_NOPE, C_ROPE, C_V = 8, 128, 64, 128
C_QK = C_NOPE + C_ROPE
C_Q_LORA, C_KV_LORA = 256, 128
C_HEAD_IN = C_Q_LORA + C_KV_LORA + C_ROPE
H_HEADS, H_KV_HEADS, H_DIM = 8, 2, 64
H_WINDOW = 128
H_CONV = 512
H_TAPS = 3
R_HEADS = 8
R_TAPS = 4
R_C = 8.0
D_FF = 3584
FF_STEP = 512
FF_STEPS = D_FF // FF_STEP
N_EXPERTS = 8

GRANULE = 2048
RAW = 6
SPLIT = 3
ITEMS = 16
GROUP = 4

VECTOR_ROWS = {}
_row = 0
for _name, _rows, _width in (
    ("a_norm_g", 2, D), ("b_norm_g", 1, D), ("c_norm_g", 1, D), ("norm_mix_2", 2, D), ("norm_ffn_2", 2, D),
    ("b_b_in", 3, D), ("b_conv_b", 1, D), ("b_ln_g", 1, D), ("b_ln_b", 1, D),
    ("c_cq_norm_g", 1, C_Q_LORA), ("c_ckv_norm_g", 1, C_KV_LORA),
    ("rg_conv_b_2", 1, D), ("rg_gate_a_b_2", 1, D), ("rg_gate_x_b_2", 1, D), ("rg_lambda_2", 1, D),
    ("rg_conv_w_2", R_TAPS, D), ("hy_conv_w_2", H_TAPS, H_CONV), ("b_conv_w", CONV_TAPS, D),
):
    VECTOR_ROWS[_name] = (_row, _rows, _width)
    _row += _rows
N_ROWS = 64
assert _row <= N_ROWS

SPREAD = {}
_col = 0
for _name, _cols in (
    ("a_q_norm_g", 2 * A_QK), ("a_k_norm_g", 2 * A_QK), ("a_sub_norm_g", 2 * A_V),
    ("c_q_norm_g", C_QK), ("c_k_norm_g", C_QK), ("hy_q_gain_2", H_DIM), ("hy_k_gain_2", H_DIM), ("hy_sinks_2", H_HEADS),
    ("a_lam_q1", 2 * A_QK), ("a_lam_k1", 2 * A_QK), ("a_lam_q2", 2 * A_QK), ("a_lam_k2", 2 * A_QK),
):
    SPREAD[_name] = (_col, _cols)
    _col += _cols
N_SPREAD = SPREAD["a_lam_q1"][0]


def constants():
    half = A_QK // 2
    inverse = (1.0 / (np.float32(10000.0) ** (np.arange(0, A_QK, 2, dtype=np.float32) / np.float32(A_QK)))).astype(np.float32)
    angle = np.arange(SEQ, dtype=np.float32)[:, None] * inverse[None, :]
    cos, sin = np.cos(angle).astype(np.float32), np.sin(angle).astype(np.float32)

    def by_tile(a):
        return a.reshape(TILES, P, 2 * half).transpose(1, 0, 2).reshape(P, TILES * 2 * half)

    q = np.arange(P, dtype=np.float32)[:, None]
    back = P + q - np.arange(2 * P, dtype=np.float32)[None, :]
    parts = {
        "ident": np.eye(P, dtype=np.float32),
        "cos": by_tile(np.concatenate([cos, cos], axis=1)),
        "sin": by_tile(np.concatenate([-sin, sin], axis=1)),
        "back": np.where((back >= 0) & (back < H_WINDOW), back, np.float32(1e33)),
        "before": np.triu(np.ones((P, P), np.float32), 1),
        "ones": np.ones((P, P), np.float32),
        "mean": np.full((P, P), 1.0 / D, np.float32),
        "count": np.broadcast_to(np.arange(P, dtype=np.float32), (P, P)),
        "neghalf": np.full((P, 16), -0.5, np.float32),
    }
    at, col = {}, 0
    for name, a in parts.items():
        at[name] = (col, a.shape[1])
        col += a.shape[1]
    return np.ascontiguousarray(np.concatenate(list(parts.values()), axis=1).astype(np.float32)), at


class Banks:

    SHORT, LONG = 0, 4

    def __init__(self):
        self.turns = {0: 0, 4: 0}
        self.at = {}
        self.order = {}
        self.in_parts = {}

    def plan(self, name, ring=0, parts=False):
        n = self.turns[ring]
        self.turns[ring] += 1
        self.at[name] = (ring + n % 4, n // 4)
        self.order[name] = len(self.order)
        if parts:
            self.in_parts[name] = len(self.in_parts)


class Steps:

    def __init__(self, eng, sem):
        self.eng, self.sem, self.done = eng, sem, 0

    def link(self, instruction):
        self.done = self.done + 1
        instruction.then_inc(self.sem, 1)
        self.eng.wait_ge(self.sem, self.done)


def attention_order(layer):
    order = []
    for s in range(ITEMS + 5):
        if s < ITEMS:
            order.append(("scores", s))
        if 0 <= s - 2 < ITEMS:
            order.append(("weights", s - 2))
        if 0 <= s - 3 < ITEMS:
            order.append(("values", s - 3))
        g = (s - 8) // GROUP
        if s >= 8 and (s - 8) % GROUP == 0:
            order.append(("output", g))
    return order


def a_order():
    order = []
    for u in range(8):
        order += [("product", 2 * u), ("product", 2 * u + 1)]
        if 1 <= u < 5:
            order += [("turn", 2 * u - 2), ("turn", 2 * u - 1)]
    return order


def c_order():
    order = [("low", 0), ("low", 1), ("gate", 0), ("gate", 1), ("lowturn", 0), ("lowturn", 1), ("gate", 2), ("gate", 3)]
    for pair in range(5):
        for kind in ("q", "kv"):
            if pair < 4:
                order += [(kind, 2 * pair), (kind, 2 * pair + 1)]
            if pair >= 1:
                order += [("qturn" if kind == "q" else "kturn", i) for i in (2 * pair - 2, 2 * pair - 1)]
    return order


def h_order():
    return [
        ("q", 0), ("q", 1), ("kv", 0), ("kv", 1), ("shift", 0), ("value", 0), ("qturn", 0), ("kturn", 0),
        ("gate", 0), ("shift", 1), ("qturn", 1), ("kturn", 1), ("value", 1), ("gate", 1),
    ]


def r_order():
    return (
        [("x", p) for p in range(4)] + [("y", 0), ("y", 1)] + [("gates", h) for h in range(R_HEADS)] + [("y", 2), ("y", 3)]
    )


def ffn_order():
    order = []
    for j in range(FF_STEPS + 1):
        if j < FF_STEPS:
            order += [("gate", j, 0), ("gate", j, 1)]
        if j >= 1:
            order += [("turn", j - 1, 0), ("turn", j - 1, 1)]
        if j < FF_STEPS:
            order += [("up", j, 0), ("up", j, 1)]
        if j >= 1:
            order += [("down", j - 1, None)]
    return order


def moe_order():
    order = []
    for j in range(FF_STEPS + 1):
        if j < FF_STEPS:
            order += [("gate", j)]
        if j >= 1:
            order += [("turn", j - 1)]
        if j < FF_STEPS:
            order += [("up", j)]
        if j == 0:
            order += [("unplace", 0)]
        if j == FF_STEPS:
            order += [("gather", 0), ("gather", 1)]
        if j >= 1:
            order += [("down", j - 1)]
    return order + [("scatter", i) for i in range(4)]


MOE_SHORT = sum(kind != "down" for kind, _ in moe_order())
assert MOE_SHORT % 4 == 0


def plan_banks():
    banks = Banks()

    def norm(n):
        for i in range(4):
            banks.plan(("norm", n, i), parts=n != 1)

    def attention(layer):
        for kind, i in attention_order(layer):
            if kind == "values":
                if i % GROUP == 0:
                    banks.plan((layer, "values", i // GROUP), Banks.LONG)
            else:
                banks.plan((layer, kind, i), parts=kind == "output")

    def out(layer):
        for i in range(4):
            banks.plan((layer, "out", i), Banks.LONG)

    def in_order(layer, order, parts=()):
        for kind, i in order:
            banks.plan((layer, kind, i), parts=kind in parts)

    banks.plan("vectors")
    norm(0)
    in_order("a0", a_order())
    attention("a0")
    out("a0")
    norm(1)
    for i in range(12):
        banks.plan(("b", "product", i))
    banks.plan(("b", "sum"), Banks.LONG)
    banks.plan(("b", "squares"), Banks.LONG)
    out("b")
    norm(2)
    in_order("c", c_order(), ("lowturn",))
    attention("c")
    out("c")
    norm(3)
    in_order("a1", a_order())
    attention("a1")
    out("a1")
    norm(4)
    in_order("h", h_order())
    attention("h")
    out("h")
    norm(5)
    for kind, j, t in ffn_order():
        if kind != "down":
            banks.plan(("ffn", kind, j, t), parts=kind == "turn")
    out("ffn")
    norm(6)
    in_order("r", r_order())
    out("r")
    norm(7)
    banks.plan("logits")
    banks.plan("places")
    for i in range(2):
        banks.plan(("moe", "first", i), parts=True)
    for kind, j in moe_order():
        if kind != "down":
            banks.plan(("moe", kind, j), parts=kind in ("gather", "turn"))
    for half in range(2):
        banks.plan(("moe", "expert", half), Banks.LONG)
    return banks


MOE_PARTS = 2 + FF_STEPS


class Granule:

    def __init__(self, src, shape, last, step, plain=False):
        self.src, self.shape, self.last, self.step, self.plain = src, shape, last, step, plain
        self.number = 0


def plan_granules(w, banks):
    granules, first = [], {}
    halves = 0

    def rows(a, c0, c1, col, n):
        return a[P * c0:P * c1, col:col + n].rearrange("(c p) n -> p c n", p=P)

    def halved(a, col, n, tickets):
        nonlocal halves
        halves += 1
        granules.append(Granule(rows(a, 0, 4, col, n), (4, n), halves, banks.order[tickets[0]] - 1))
        granules.append(Granule(rows(a, 4, 8, col, n), (4, n), tickets[1], banks.order[tickets[1]]))

    def whole(a, col, n, last, plain=False):
        granules.append(Granule(rows(a, 0, a.shape[0] // P, col, n), (a.shape[0] // P, n), last, banks.order[last], plain))

    def out(layer, a):
        for n in range(2):
            halved(a, 512 * n, 512, [(layer, "out", 2 * n), (layer, "out", 2 * n + 1)])

    for layer in ("a0", "b", "c", "a1", "h", "ffn", "r"):
        first[layer] = len(granules)
        if layer[0] == "a":
            for u in range(8):
                halved(w["a_w_in"][int(layer[1])], 512 * u, 512, [(layer, "product", 2 * u), (layer, "product", 2 * u + 1)])
            out(layer, w["a_w_out"][int(layer[1])])
        if layer == "b":
            for i in range(12):
                whole(w["b_w_in"][0], D * (i % 3) + 2 * P * (i // 3), 2 * P, (layer, "product", i), plain=True)
            out(layer, w["b_w_out"][0])
        if layer == "c":
            a = w["c_w_in"][0]
            halved(a, 0, C_HEAD_IN, [(layer, "low", 0), (layer, "low", 1)])
            for n in range(2):
                halved(a, C_HEAD_IN + 512 * n, 512, [(layer, "gate", 2 * n), (layer, "gate", 2 * n + 1)])
            whole(w["c_w_uq"][0], 0, 4 * C_QK, (layer, "q", 3))
            whole(w["c_w_ukv"][0], 0, C_HEADS * (C_NOPE + C_V), (layer, "kv", 7))
            whole(w["c_w_uq"][0], 4 * C_QK, 4 * C_QK, (layer, "q", 7))
            out(layer, w["c_w_out"][0])
        if layer == "h":
            a = w["hy_w_in_2"][0]
            halved(a, 0, 512, [(layer, "q", 0), (layer, "q", 1)])
            halved(a, 512, 256, [(layer, "kv", 0), (layer, "kv", 1)])
            col = {"gate": 768, "shift": 1280, "value": 1792}
            for kind, i in h_order():
                if kind in col:
                    whole(a, col[kind] + 2 * P * i, 2 * P, (layer, kind, i))
            out(layer, w["hy_w_out_2"][0])
        if layer == "ffn":
            for kind, j, t in ffn_order():
                if kind in ("gate", "up") and t == 0:
                    halved(w[f"ffn_w_{kind}_2"][0], FF_STEP * j, FF_STEP, [(layer, kind, j, 0), (layer, kind, j, 1)])
                if kind == "down":
                    for half in range(2):
                        row = FF_STEP * j + 2 * P * half
                        src = w["ffn_w_down_2"][0][row:row + 2 * P, :].rearrange("(c p) n -> p c n", p=P)
                        if j == FF_STEPS - 1 and half == 1:
                            granules.append(Granule(src, (2, D), (layer, "out", 3), banks.order[(layer, "out", 3)]))
                        else:
                            halves += 1
                            before = ("up", j + 1, 1) if j < FF_STEPS - 1 else ("turn", j, 1)
                            granules.append(Granule(src, (2, D), halves, banks.order[(layer,) + before]))
        if layer == "r":
            a = w["rg_w_in_2"][0]
            for kind, i in r_order():
                if kind == "gates" and i == 0:
                    granules.append(Granule(None, None, (layer, "gates", R_HEADS - 1), banks.order[(layer, "gates", R_HEADS - 1)], True))
                if kind in ("x", "y"):
                    whole(a, D * (kind == "x") + 2 * P * i, 2 * P, (layer, kind, i))
            out(layer, w["rg_w_out_2"][0])
    first["moe"] = len(granules)
    for before, granule in zip(granules, granules[1:]):
        granule.number = before.number + (not before.plain)
    return granules, first, halves


ARENA = 12320


class Parts:

    def __init__(self, high, low):
        self.high, self.low = high, low

    def __getitem__(self, index):
        return Parts(self.high[index], self.low[index])

    def rearrange(self, pattern, **sizes):
        return Parts(self.high.rearrange(pattern, **sizes), self.low.rearrange(pattern, **sizes))


class Buffers:
    pass


class Core:

    def __init__(self, nc, ctx, w, consts, const_at, out):
        self.nc, self.w, self.consts, self.out = nc, w, consts, out
        self.banks = plan_banks()
        self.granules, self.first_granule, self.halves = plan_granules(w, self.banks)
        self.engine_steps = {}
        self.split_so_far = {"act": 0, "dve": 0}

        def sb(name, shape, dtype=F32):
            return ctx.enter_context(nc.sbuf_tensor(name, shape, dtype))

        def sem(name):
            return ctx.enter_context(nc.semaphore(name))

        self.psum = ctx.enter_context(nc.psum_tensor("psum", [P, 8, 512], F32))
        self.raw = sb("raw", [P, RAW, GRANULE])
        self.high = sb("high", [P, SPLIT, GRANULE], F32R)
        self.low = sb("low", [P, SPLIT, GRANULE], F32R)
        self.x = sb("x", [P, TILES, D])
        self.h = sb("h", [P, TILES, D])
        self.hT = Parts(sb("hT_high", [P, KC, SEQ], F32R), sb("hT_low", [P, KC, SEQ], F32R))
        self.yT = Parts(sb("yT_high", [P, KC, SEQ], F32R), sb("yT_low", [P, KC, SEQ], F32R))
        self.const = sb("const", [P, consts.shape[1]])
        self.spread = sb("spread", [P, N_SPREAD])
        self.vecs = sb("vecs", [P, KC, N_ROWS])
        self.arena = sb("arena", [P, ARENA])
        self.small = sb("small", [P, 640])
        self.work = sb("work", [P, 16], I32)
        self.router = sb("router", [P, KC, N_EXPERTS])
        self.best = sb("best", [P, TILES, 8], U32)
        self.carved = 0

        def const(name):
            col, n = const_at[name]
            return self.const[:, col:col + n]

        self.ident, self.before, self.ones, self.mean = const("ident"), const("before"), const("ones"), const("mean")
        self.cos = const("cos").rearrange("p (t d) -> p t d", t=TILES)
        self.sin = const("sin").rearrange("p (t d) -> p t d", t=TILES)
        self.back, self.count, self.neghalf = const("back"), const("count"), const("neghalf")

        at = 0

        def small(n):
            nonlocal at
            at += n
            return self.small[:, at - n:at]

        self.ms, self.rstd = small(2), small(2)
        self.neglam = small(2)
        self.lam_sums, self.lam_exps = small(4), small(4)
        self.subgain = small(2 * A_V)
        self.decay, self.negdecay = small(KC), small(KC)
        self.soft = [small(KC) for _ in range(6)]
        self.group_ms, self.group_rstd = small(4 * 8), small(4 * 8)
        self.top, self.lowest, self.sums, self.inverse = small(4), small(4), small(4), small(4)
        self.pair_scale = small(4)
        self.sink_exp = small(4)
        self.out_ms, self.out_rstd = small(2 * GROUP), small(2 * GROUP)
        self.logits = small(TILES * 8)
        self.sorted = small(TILES * 8)
        self.first = small(TILES * 2)
        self.gap, self.both = small(TILES), small(TILES)
        self.share = small(TILES * 2)
        self.chosen = small(TILES * N_EXPERTS).rearrange("p (t e) -> p t e", t=TILES)
        self.weight = small(TILES * N_EXPERTS).rearrange("p (t e) -> p t e", t=TILES)
        self.place = small(2 * TILES * N_EXPERTS).rearrange("p (s t e) -> p s t e", s=2, t=TILES)
        self.over = small(5 * 8)
        assert at <= 640

        self.x_landed = sem("x_landed")
        self.const_landed = sem("const_landed")
        self.rows_landed = sem("rows_landed")
        self.spread_landed = sem("spread_landed")
        self.router_landed = sem("router_landed")
        self.stored = sem("stored")
        self.landed = [sem(f"granule_landed_{i}") for i in range(RAW)]
        self.high_ready = sem("high_ready")
        self.low_ready = sem("low_ready")
        self.half_done = sem("half_done")
        self.part_ready = sem("part_ready")
        self.filled = [sem(f"filled_{i}") for i in range(8)]
        self.freed = [sem(f"freed_{i}") for i in range(8)]
        self.own = {e: sem(f"{e}_own") for e in ("act", "dve", "pool")}
        self.rows_cleared = sem("rows_cleared")
        self.tables_ready = sem("tables_ready")
        self.lam_exps_ready = sem("lam_exps_ready")
        self.soft_ready = sem("soft_ready")
        self.softexp_ready = sem("softexp_ready")
        self.ms_ready = sem("ms_ready")
        self.rstd_ready = sem("rstd_ready")
        self.h_ready = sem("h_ready")
        self.group_squares = sem("group_squares")
        self.group_ms_ready = sem("group_ms_ready")
        self.group_rstd_ready = sem("group_rstd_ready")
        self.staged = sem("staged")
        self.cleared = sem("cleared")
        self.lowest_ready = sem("lowest_ready")
        self.weights_ready = sem("weights_ready")
        self.out_squares = sem("out_squares")
        self.out_ms_ready = sem("out_ms_ready")
        self.out_rstd_ready = sem("out_rstd_ready")
        self.gates_ready = sem("gates_ready")
        self.c_low_staged = sem("c_low_staged")
        self.c_q_staged = sem("c_q_staged")
        self.c_k_staged = sem("c_k_staged")
        self.c_v_ready = sem("c_v_ready")
        self.c_roots_used = sem("c_roots_used")
        self.b_gate_ready = sem("b_gate_ready")
        self.b_pair_done = sem("b_pair_done")
        self.conv_ready = sem("conv_ready")
        self.b_mean_gone = sem("b_mean_gone")
        self.b_squares_ready = sem("b_squares_ready")
        self.b_var_ready = sem("b_var_ready")
        self.b_root_ready = sem("b_root_ready")
        self.b_normed = sem("b_normed")
        self.b_silu_ready = sem("b_silu_ready")
        self.b_mixed = sem("b_mixed")
        self.h_q_staged = sem("h_q_staged")
        self.h_k_staged = sem("h_k_staged")
        self.r_conv_ready = sem("r_conv_ready")
        self.r_decay_ready = sem("r_decay_ready")
        self.r_decays = sem("r_decays")
        self.r_root_in = sem("r_root_in")
        self.r_root_ready = sem("r_root_ready")
        self.r_mixed = sem("r_mixed")
        self.routed = sem("routed")
        self.placed = sem("placed")
        self.gap_ready = sem("gap_ready")
        self.share_ready = sem("share_ready")
        self.work_ready = sem("work_ready")

    def reset_arena(self):
        self.carved = 0

    def carve(self, *shape):
        n = int(np.prod(shape))
        a = self.arena[:, self.carved:self.carved + n]
        self.carved += n
        assert self.carved <= ARENA
        if len(shape) == 2:
            return a.rearrange("p (a b) -> p a b", a=shape[0])
        if len(shape) == 3:
            return a.rearrange("p (a b c) -> p a b c", a=shape[0], b=shape[1])
        return a

    def bank(self, name):
        return self.psum[:, self.banks.at[name][0], :]

    def take(self, pe, name, more=0):
        b, use = self.banks.at[name]
        if use > 0:
            pe.wait_ge(self.freed[b], use + more)

    def fill(self, matmul, name):
        matmul.then_inc(self.filled[self.banks.at[name][0]], 1)

    def wait_filled(self, eng, name, more=0):
        b, use = self.banks.at[name]
        eng.wait_ge(self.filled[b], use + 1 + more)

    def release(self, instruction, name):
        instruction.then_inc(self.freed[self.banks.at[name][0]], 1)

    def wait_released(self, eng, name, more=0):
        b, use = self.banks.at[name]
        eng.wait_ge(self.freed[b], use + 1 + more)

    def wait_part(self, eng, name, more=0):
        eng.wait_ge(self.part_ready, self.banks.in_parts[name] + 1 + more)

    def wait_landed(self, eng, g):
        eng.wait_ge(self.landed[g % RAW], 16 * (g // RAW + 1))

    def wait_used(self, eng, last):
        if isinstance(last, int):
            eng.wait_ge(self.half_done, last)
        else:
            self.wait_filled(eng, last)

    def column(self, name, c, row=0):
        r = VECTOR_ROWS[name][0] + row
        return self.vecs[:, c, r:r + 1]

    def wide(self, name, start=0, n=None):
        col, m = SPREAD[name]
        if col >= N_SPREAD:
            first = ROWS_AT + D + col - N_SPREAD + start
            return self.arena[:, first:first + (m - start if n is None else n)]
        return self.spread[:, col + start:col + start + (m - start if n is None else n)]


def over_groups(a, groups):
    return a.unsqueeze(1).broadcast_to([P, groups, a.shape[1]])


def over_columns(a, n):
    return a.unsqueeze(2).broadcast_to([P, a.shape[1], n])



def sync_weights(k, sp):
    sp.wait_ge(k.x_landed, 16 * TILES)
    sp.wait_ge(k.rows_landed, 16 * len(VECTOR_ROWS))
    for g, granule in enumerate(k.granules):
        if g == 2:
            spread_loads(k, sp)
        if g >= RAW:
            before = k.granules[g - RAW]
            if before.plain:
                k.wait_used(sp, before.last)
            else:
                sp.wait_ge(k.low_ready, before.number + 1)
        if granule.src is None:
            dst = k.raw[:, g % RAW, :].rearrange("p (g h n) -> p g h n", g=2, h=R_HEADS)
            sp.dma_start(dst[:, 1], k.w["rg_gate_x_w_2"][0].rearrange("h p n -> p h n")).then_inc(k.gates_ready, 16)
            sp.dma_start(dst[:, 0], k.w["rg_gate_a_w_2"][0].rearrange("h p n -> p h n")).then_inc(k.landed[g % RAW], 16)
            continue
        c, n = granule.shape
        dst = k.raw[:, g % RAW, 0:c * n].rearrange("p (c n) -> p c n", c=c)
        sp.dma_start(dst, granule.src).then_inc(k.landed[g % RAW], 16)


def ahead(k, eng, name):
    engine = "act" if eng is k.nc.scalar else "dve"
    step = k.banks.order[name]
    while k.split_so_far[engine] < len(k.granules):
        g = k.split_so_far[engine]
        granule = k.granules[g]
        if not granule.plain:
            n = granule.number
            if n >= SPLIT and split_granules(k)[n - SPLIT].step >= step:
                return
            if g >= RAW and k.granules[g - RAW].plain and k.granules[g - RAW].step >= step:
                return
            if engine == "act":
                if n >= SPLIT:
                    k.wait_used(eng, split_granules(k)[n - SPLIT].last)
                k.wait_landed(eng, g)
            split(k, eng, n % SPLIT, g % RAW, granule.shape[0] * granule.shape[1], granule.number)
        k.split_so_far[engine] += 1


def split_granules(k):
    return [granule for granule in k.granules if not granule.plain]


def split(k, eng, slot, raw_slot, n, number):
    high, low, raw = k.high[:, slot, 0:n], k.low[:, slot, 0:n], k.raw[:, raw_slot, 0:n]
    if eng is k.nc.scalar:
        eng.activation(high, raw, ACT.Copy).then_inc(k.high_ready, 1)
    else:
        eng.wait_ge(k.high_ready, number + 1)
        eng.tensor_tensor(low, raw, high.bitcast(F32), ALU.subtract).then_inc(k.low_ready, 1)


def wait_split(k, pe, g):
    pe.wait_ge(k.low_ready, k.granules[g].number + 1)


def granule_parts(k, g, c):
    n, slot = k.granules[g].shape[1], k.granules[g].number % SPLIT
    parts = Parts(k.high[:, slot, 0:c * n], k.low[:, slot, 0:c * n])
    return parts.rearrange("p (c n) -> p c n", c=c)


def three_passes(pe, out, lhs, rhs, start, stop):
    pe.matmul(out, lhs.high, rhs.high, start=start, stop=False)
    pe.matmul(out, lhs.high, rhs.low, start=False, stop=False)
    return pe.matmul(out, lhs.low, rhs.high, start=False, stop=stop)



ROWS_AT = 8192


def setup_loads(k, act):
    for t in range(TILES):
        act.dma_start(k.x[:, t, :], k.w["x"][0].rearrange("(t p) d -> p t d", p=P)[:, t, :]).then_inc(k.x_landed, 16)
    act.dma_start(k.const[:, :], k.consts).then_inc(k.const_landed, 16)
    act.wait_ge(k.rows_cleared, 1)
    rows = k.arena[:, ROWS_AT:ROWS_AT + D]
    for name, (row, n, width) in VECTOR_ROWS.items():
        a = k.w[name]
        src = a[0] if name in ("rg_conv_w_2", "hy_conv_w_2", "b_conv_w") else a
        if name == "b_b_in":
            src = a[0].rearrange("(a d) -> a d", a=3)
        act.dma_start(rows[row:row + n, 0:width], src).then_inc(k.rows_landed, 16)


def spread_loads(k, sp):
    for name, (col, n) in SPREAD.items():
        a = k.w[name].rearrange("a n -> (a n)").unsqueeze(0)
        sp.dma_start(k.wide(name), a.broadcast_to([P, n])).then_inc(k.spread_landed, 16)
    sp.dma_start(k.router[:, :, :], k.w["moe_router_2"][0].rearrange("(c p) e -> p c e", p=P)).then_inc(k.router_landed, 16)


def setup_tensor(k, pe):
    pe.wait_ge(k.const_landed, 16)
    pe.wait_ge(k.rows_landed, 16 * len(VECTOR_ROWS))
    rows = k.arena[:, ROWS_AT:ROWS_AT + D]
    k.take(pe, "vectors")
    for c in range(KC):
        last = pe.transpose(k.bank("vectors")[:, N_ROWS * c:N_ROWS * (c + 1)], rows[0:N_ROWS, P * c:P * (c + 1)],
                            k.ident[0:N_ROWS, 0:N_ROWS])
    k.fill(last, "vectors")


def rope_tables(k, v, steps, tables, gain, tile_tables=True):
    half = A_QK // 2
    for t in range(TILES):
        cos, sin = tables[:, 2 * t, :], tables[:, 2 * t + 1, :]
        v.tensor_tensor(cos, k.cos[:, t, :], gain, ALU.mult).then_inc(k.tables_ready, 1)
        v.tensor_tensor(sin[:, 0:half], k.sin[:, t, 0:half], gain[:, half:], ALU.mult).then_inc(k.tables_ready, 1)
        v.tensor_tensor(sin[:, half:], k.sin[:, t, half:], gain[:, 0:half], ALU.mult).then_inc(k.tables_ready, 1)


def setup_vector(k, v):
    v.memset(k.arena[:, ROWS_AT:ROWS_AT + D], 0.0).then_inc(k.rows_cleared, 1)
    k.wait_filled(v, "vectors")
    k.release(v.tensor_copy(k.vecs[:, :, :].rearrange("p c r -> p (c r)"), k.bank("vectors")[:, 0:KC * N_ROWS]), "vectors")
    k.wait_released(v, "vectors")


def setup_lambdas(k, v):
    steps = k.engine_steps["dve"]
    v.wait_ge(k.const_landed, 16)
    v.wait_ge(k.spread_landed, 16 * len(SPREAD))
    junk = k.arena[:, 0:A_QK]
    for j in range(2):
        for m, (q, kk) in enumerate((("a_lam_q1", "a_lam_k1"), ("a_lam_q2", "a_lam_k2"))):
            steps.link(v.tensor_tensor_reduce(junk, k.wide(q, A_QK * j, A_QK), k.wide(kk, A_QK * j, A_QK), 1.0, 0.0,
                                              ALU.mult, ALU.add, k.lam_sums[:, 2 * j + m:2 * j + m + 1]))
    lam = k.vecs[:, :, VECTOR_ROWS["rg_lambda_2"][0]]
    neg, mag, s, s2, acc, pos = k.soft
    steps.link(v.tensor_scalar(neg, lam, -1.0, None, ALU.mult))
    steps.link(v.tensor_tensor(mag, neg, lam, ALU.min))
    v.tensor_scalar(pos, neg, 0.0, None, ALU.max).then_inc(k.soft_ready, 1)
    v.wait_ge(k.softexp_ready, 1)
    steps.link(v.tensor_scalar(s2, mag, 2.0, None, ALU.add))
    steps.link(v.reciprocal(s2, s2))
    steps.link(v.tensor_tensor(s, mag, s2, ALU.mult))
    steps.link(v.tensor_tensor(s2, s, s, ALU.mult))
    steps.link(v.tensor_scalar(acc, s2, 1.0 / 17, 1.0 / 15, ALU.mult, ALU.add))
    for n in (13, 11, 9, 7, 5, 3, 1):
        steps.link(v.tensor_tensor(acc, acc, s2, ALU.mult))
        steps.link(v.tensor_scalar(acc, acc, 1.0 / n, None, ALU.add))
    steps.link(v.tensor_tensor(acc, acc, s, ALU.mult))
    v.wait_ge(k.soft_ready, 1)
    steps.link(v.scalar_tensor_tensor(acc, acc, 2.0, pos, ALU.mult, ALU.add))
    steps.link(v.tensor_scalar(k.decay, acc, R_C, None, ALU.mult))
    v.wait_ge(k.lam_exps_ready, 1)
    for j in range(2):
        e = k.lam_exps[:, 2 * j:2 * j + 2]
        steps.link(v.tensor_tensor(k.neglam[:, j:j + 1], e[:, 1:2], e[:, 0:1], ALU.subtract))
        steps.link(v.tensor_scalar(k.neglam[:, j:j + 1], k.neglam[:, j:j + 1], -A_LAMBDA_INIT[j], None, ALU.add))
        steps.link(v.tensor_scalar(k.subgain[:, A_V * j:A_V * (j + 1)], k.wide("a_sub_norm_g", A_V * j, A_V),
                                   1.0 - A_LAMBDA_INIT[j], None, ALU.mult))


def setup_scalar(k, act):
    act.wait_ge(k.soft_ready, 1)
    act.activation(k.soft[1], k.soft[1], ACT.Exp).then_inc(k.softexp_ready, 1)
    act.activation(k.lam_exps, k.lam_sums, ACT.Exp).then_inc(k.lam_exps_ready, 1)



NORM_GAIN = [("a_norm_g", 0), ("b_norm_g", 0), ("c_norm_g", 0), ("a_norm_g", 1), ("norm_mix_2", 0), ("norm_ffn_2", 0),
             ("norm_mix_2", 1), ("norm_ffn_2", 1)]


def norm_scalar(k, act, n, x_from):
    for name in x_from:
        k.wait_released(act, name)
    if n == 0:
        act.wait_ge(k.x_landed, 16 * TILES)
    act.activation(k.h[:, 0, :], k.x[:, 0, :], ACT.Square, scale=float(D) ** -0.5, accum_out=k.ms[:, 0:1]).then_inc(k.ms_ready, 1)
    act.wait_ge(k.rstd_ready, n + 1)
    act.wait_ge(k.ms_ready, 2 * n + 2)
    act.activation(k.h[:, 0, :], k.x[:, 0, :], ACT.Copy, scale=k.rstd[:, 0:1]).then_inc(k.h_ready, 1)
    gain = NORM_GAIN[n]
    for i in range(4):
        name = ("norm", n, i)
        if n == 1 and i % 2 == 0:
            continue
        k.wait_filled(act, name)
        for c in (2 * i, 2 * i + 1):
            src = k.bank(name)[:, SEQ * (c % 2):SEQ * (c % 2 + 1)]
            dst = b_buffers(k).hT[:, c, :] if n == 1 else k.hT.high[:, c, :]
            last = act.activation(dst, src, ACT.Copy, scale=k.column(gain[0], c, gain[1]))
        if n == 1:
            k.release(last, name)
        else:
            last.then_inc(k.part_ready, 1)
    ahead(k, act, ("norm", n, 3))


def norm_vector(k, v, n, x_from):
    for name in x_from:
        k.wait_released(v, name)
    if n == 0:
        v.wait_ge(k.x_landed, 16 * TILES)
    v.tensor_tensor_reduce(k.h[:, 1, :], k.x[:, 1, :], k.x[:, 1, :], 1.0 / D, 0.0, ALU.mult, ALU.add, k.ms[:, 1:2])\
     .then_inc(k.ms_ready, 1)
    v.wait_ge(k.rstd_ready, n + 1)
    v.tensor_scalar(k.h[:, 1, :], k.x[:, 1, :], k.rstd[:, 1:2], None, ALU.mult).then_inc(k.h_ready, 1)
    gain = NORM_GAIN[n]
    for i in range(4):
        name = ("norm", n, i)
        if n == 1 and i % 2 == 1:
            continue
        k.wait_filled(v, name)
        if n != 1:
            k.wait_part(v, name)
        for c in (2 * i, 2 * i + 1):
            src = k.bank(name)[:, SEQ * (c % 2):SEQ * (c % 2 + 1)]
            if n == 1:
                last = v.tensor_scalar(b_buffers(k).hT[:, c, :], src, k.column(gain[0], c, gain[1]), None, ALU.mult)
            else:
                last = v.scalar_tensor_tensor(k.hT.low[:, c, :], src, k.column(gain[0], c, gain[1]),
                                              k.hT.high[:, c, :].bitcast(F32), ALU.mult, ALU.subtract)
        k.release(last, name)
    ahead(k, v, ("norm", n, 3))


def norm_pool(k, pool, n):
    pool.wait_ge(k.ms_ready, 2 * n + 2)
    inverse_root(k, pool, k.ms, k.rstd, k.rstd_ready)


def inverse_root(k, pool, ms, rstd, ready):
    n = ms.shape[1]
    k.engine_steps["pool"].link(pool.tensor_scalar(rstd, ms, EPS, None, ALU.add))
    pool.tensor_tensor(rstd, rstd, k.neghalf[:, 0:n], ALU.pow).then_inc(ready, 1)


def norm_tensor(k, pe, n):
    if n == 0:
        pe.wait_ge(k.const_landed, 16)
    pe.wait_ge(k.h_ready, 2 * n + 2)
    for i in range(4):
        k.take(pe, ("norm", n, i))
        for c in (2 * i, 2 * i + 1):
            for t in range(TILES):
                first = SEQ * (c % 2) + P * t
                last = pe.transpose(k.bank(("norm", n, i))[:, first:first + P], k.h[:, t, P * c:P * (c + 1)], k.ident)
        k.fill(last, ("norm", n, i))
    for i in range(4):
        k.wait_released(pe, ("norm", n, i))



def products(k, pe, names, g, lhs, kc, n, first=0, halves=2):
    for half in range(halves):
        wait_split(k, pe, g + half)
        chunks = kc // halves
        w = granule_parts(k, g + half, chunks)
        for t, name in enumerate(names):
            if half == 0:
                k.take(pe, name)
            for c in range(chunks):
                at = half * chunks + c
                last = three_passes(pe, k.bank(name)[:, 0:n], lhs[:, at, P * t:P * (t + 1)], w[:, c, first:first + n],
                                    at == 0, at == kc - 1)
            if half == halves - 1:
                k.fill(last, name)
        if half < halves - 1:
            last.then_inc(k.half_done, 1)


def channel_product(k, pe, name, g):
    wait_split(k, pe, g)
    k.take(pe, name)
    w = granule_parts(k, g, KC)
    for half in range(2):
        out = k.bank(name)[:, SEQ * half:SEQ * (half + 1)]
        for c in range(KC):
            last = three_passes(pe, out, w[:, c, P * half:P * (half + 1)], k.hT[:, c, :], c == 0, c == KC - 1)
    k.fill(last, name)


def out_tensor(k, pe, layer):
    g = k.first_granule[NEXT_LAYER[layer]] - 4
    for n in range(2):
        products(k, pe, [(layer, "out", 2 * n), (layer, "out", 2 * n + 1)], g + 2 * n, k.yT, KC, 512)


NEXT_LAYER = {"a0": "b", "b": "c", "c": "a1", "a1": "h", "h": "ffn", "ffn": "r", "r": "moe"}


def out_scalar(k, act, layer):
    for name in out_names(layer):
        ahead(k, act, name)


def out_vector(k, v, layer):
    for n in range(2):
        for t in range(TILES):
            add_to_x(k, v, (layer, "out", 2 * n + t), t, n)


def add_to_x(k, v, name, t, n):
    ahead(k, v, name)
    k.wait_filled(v, name)
    part = k.x[:, t, 512 * n:512 * (n + 1)]
    k.release(v.tensor_tensor(part, part, k.bank(name), ALU.add), name)


def out_names(layer):
    return [(layer, "out", i) for i in range(4)]



ATTENTIONS = {"a0": 0, "c": 1, "a1": 2, "h": 3}
SCORE_SCALE = {"a": A_QK ** -0.5, "c": C_QK ** -0.5, "h": H_DIM ** -0.5}
VALUE_DIM = {"a": A_V, "c": C_V, "h": H_DIM}


def item(i):
    return i // 8, i % 8


def keys_of(t):
    return P * (t + 1)


def attention_buffers(k):
    a = k.h[:, :, :].rearrange("p t d -> p (t d)")
    probs = a[:, 0:1024].rearrange("p (s n) -> p s n", s=2)
    weights = a[:, 1024:1536].rearrange("p (s n) -> p s n", s=2)
    turned = a[:, 1536:2048].rearrange("p (s n) -> p s n", s=2)
    return probs, weights, turned


def attention_tensor(k, pe, layer, b):
    probs, weights, turned = attention_buffers(k)
    base, kind = ITEMS * ATTENTIONS[layer], layer[0]
    dim = VALUE_DIM[kind]
    for step, i in attention_order(layer):
        t, head = item(i)
        tile = slice(P * t, P * (t + 1))
        e = keys_of(t)
        if step == "scores":
            name = (layer, step, i)
            k.take(pe, name)
            bank = k.bank(name)
            if kind == "a":
                for m in range(2):
                    last = pe.matmul(bank[:, SEQ * m:SEQ * m + e], b.qT[:, m, head, tile], b.kT[:, head, 0:e], start=True, stop=True)
            if kind == "c":
                pe.matmul(bank[:, 0:e], b.qT[:, head, tile], b.kT[:, head, 0:e], start=True, stop=False)
                last = pe.matmul(bank[:, 0:e], b.qropeT[:, head // 2, tile], b.kropeT[:, head % 2, 0:e], start=False, stop=True)
            if kind == "h":
                last = pe.matmul(bank[:, 0:e], b.qT[:, head % 4, tile], b.kT[:, head // 4, 0:e], start=True, stop=True)
            k.fill(last, name)
        if step == "weights":
            name = (layer, step, i)
            pe.wait_ge(k.weights_ready, base + i + 1)
            k.take(pe, name)
            for c in range(t + 1):
                last = pe.transpose(k.bank(name)[:, P * c:P * (c + 1)], weights[:, i % 2, P * c:P * (c + 1)], k.ident)
            k.fill(last, name)
        if step == "values":
            name = (layer, step, i // GROUP)
            if i % GROUP == 0:
                k.take(pe, name)
            k.wait_released(pe, (layer, "weights", i))
            if kind == "h":
                cols = slice(H_DIM * (head // 4), H_DIM * (head // 4 + 1))
            else:
                cols = slice(dim * head, dim * (head + 1))
            place = dim * (i % GROUP)
            for c in range(t + 1):
                last = pe.matmul(k.bank(name)[:, place:place + dim], turned[:, i % 2, P * c:P * (c + 1)], b.v[:, c, cols],
                                 start=(c == 0), stop=(c == t))
            if i % GROUP == GROUP - 1:
                k.fill(last, name)
        if step == "output":
            name = (layer, step, i)
            pe.wait_ge(k.staged, b.staged0 + i + 1)
            k.take(pe, name)
            for c in range(GROUP * dim // P):
                last = pe.transpose(k.bank(name)[:, P * c:P * (c + 1)], b.y[:, i % 2, P * c:P * (c + 1)], k.ident)
            k.fill(last, name)
    for g in range(ITEMS // GROUP):
        k.wait_released(pe, (layer, "output", g))
    out_tensor(k, pe, layer)


def attention_scalar(k, act, layer, b):
    probs, weights, turned = attention_buffers(k)
    base, kind = ITEMS * ATTENTIONS[layer], layer[0]
    scale = SCORE_SCALE[kind]
    for s in range(ITEMS + 5):
        if s < ITEMS:
            t, head = item(s)
            e = keys_of(t)
            act.wait_ge(k.lowest_ready, base + s + 1)
            low = k.lowest.rearrange("p (s m) -> p s m", s=2)[:, s % 2, :]
            sums = k.sums.rearrange("p (s m) -> p s m", s=2)[:, s % 2, :]
            name = (layer, "scores", s)
            if kind == "h":
                act.activation(k.sink_exp[:, s % 2:s % 2 + 1], k.wide("hy_sinks_2", head, 1), ACT.Exp, bias=low[:, 0:1])
                k.release(act.activation(probs[:, s % 2, 0:e], b.s[:, s % 2, 0:e], ACT.Exp, bias=low[:, 0:1],
                                         accum_out=sums[:, 0:1]), name)
            else:
                maps = 2 if kind == "a" else 1
                for m in range(maps):
                    last = act.activation(probs[:, s % 2, SEQ * m:SEQ * m + e], k.bank(name)[:, SEQ * m:SEQ * m + e], ACT.Exp,
                                          bias=low[:, m:m + 1], scale=scale, accum_out=sums[:, m:m + 1])
                k.release(last, name)
        if 0 <= s - 2 < ITEMS:
            i = s - 2
            e = keys_of(item(i)[0])
            k.wait_filled(act, (layer, "weights", i))
            k.release(act.activation(turned[:, i % 2, 0:e], k.bank((layer, "weights", i))[:, 0:e], ACT.Copy), (layer, "weights", i))
        g = (s - 6) // GROUP
        if kind == "a" and s >= 6 and (s - 6) % GROUP == 0 and g < 4:
            k.wait_filled(act, (layer, "values", g))
            act.activation(b.squares, k.bank((layer, "values", g)), ACT.Square, scale=float(A_V) ** -0.5).then_inc(k.out_squares, 1)
        g = (s - 8) // GROUP
        if s >= 8 and (s - 8) % GROUP == 0:
            t, half = g // 2, g % 2
            n = GROUP * VALUE_DIM[kind] // P
            k.wait_filled(act, (layer, "output", g))
            src = k.bank((layer, "output", g))[:, 0:P * n].rearrange("p (c q) -> p c q", c=n)
            act.activation(k.yT.high[:, n * half:n * (half + 1), P * t:P * (t + 1)], src, ACT.Copy).then_inc(k.part_ready, 1)
    out_scalar(k, act, layer)


def attention_vector(k, v, layer, b):
    steps = k.engine_steps["dve"]
    probs, weights, turned = attention_buffers(k)
    base, kind = ITEMS * ATTENTIONS[layer], layer[0]
    scale = SCORE_SCALE[kind]
    maps = 2 if kind == "a" else 1
    for s in range(ITEMS + 5):
        if s < ITEMS:
            t, head = item(s)
            e = keys_of(t)
            name = (layer, "scores", s)
            k.wait_filled(v, name)
            bank = k.bank(name)
            top = k.top.rearrange("p (s m) -> p s m", s=2)[:, s % 2, 0:maps]
            low = k.lowest.rearrange("p (s m) -> p s m", s=2)[:, s % 2, 0:maps]
            if kind == "h":
                slope = 2.0 ** -(head + 1)
                both = bank[:, 0:e]
                steps.link(v.tensor_scalar(b.s[:, s % 2, 0:e], both, scale, None, ALU.mult))
                steps.link(v.scalar_tensor_tensor(b.s[:, s % 2, 0:e], k.back[:, SEQ - e:SEQ], -slope, b.s[:, s % 2, 0:e],
                                                  ALU.mult, ALU.add))
                steps.link(v.tensor_reduce(top, b.s[:, s % 2, 0:e], AX, ALU.max))
                steps.link(v.tensor_tensor(top, top, k.wide("hy_sinks_2", head, 1), ALU.max))
                v.tensor_scalar(low, top, -1.0, None, ALU.mult).then_inc(k.lowest_ready, 1)
            else:
                bank3 = bank.rearrange("p (m n) -> p m n", m=2)
                steps.link(v.memset(bank3[0:CHUNK, 0:maps, e - CHUNK:e], MASKED))
                steps.link(v.tensor_reduce(top, bank3[:, 0:maps, 0:e], AX, ALU.max))
                v.tensor_scalar(low, top, -scale, None, ALU.mult).then_inc(k.lowest_ready, 1)
        i = s - 1
        if 0 <= i < ITEMS:
            t, head = item(i)
            e = keys_of(t)
            slot = i % 2
            sums = k.sums.rearrange("p (s m) -> p s m", s=2)[:, slot, 0:maps]
            inv = k.inverse.rearrange("p (s m) -> p s m", s=2)[:, slot, 0:maps]
            k.wait_released(v, (layer, "scores", i))
            if kind == "h":
                steps.link(v.tensor_tensor(sums, sums, k.sink_exp[:, slot:slot + 1], ALU.add))
            steps.link(v.reciprocal(inv, sums))
            if i >= 2:
                k.wait_filled(v, (layer, "weights", i - 2))
            if kind == "a":
                j = int(layer[1])
                steps.link(v.tensor_scalar(k.pair_scale[:, slot:slot + 1], inv[:, 1:2], k.neglam[:, j:j + 1], None, ALU.mult))
                steps.link(v.tensor_scalar(b.second[:, 0:e], probs[:, slot, SEQ:SEQ + e], k.pair_scale[:, slot:slot + 1], None, ALU.mult))
                v.scalar_tensor_tensor(weights[:, slot, 0:e], probs[:, slot, 0:e], inv[:, 0:1], b.second[:, 0:e],
                                       ALU.mult, ALU.add).then_inc(k.weights_ready, 1)
            else:
                v.tensor_scalar(weights[:, slot, 0:e], probs[:, slot, 0:e], inv[:, 0:1], None, ALU.mult).then_inc(k.weights_ready, 1)
        g = (s - 6) // GROUP
        if kind == "a" and s >= 6 and (s - 6) % GROUP == 0 and g < 4:
            n = 4 * int(layer[1]) + g
            v.wait_ge(k.out_squares, n + 1)
            v.tensor_reduce(k.out_ms[:, 0:GROUP], b.squares.rearrange("p (h d) -> p h d", h=GROUP), AX, ALU.add)\
             .then_inc(k.out_ms_ready, 1)
        g = (s - 7) // GROUP
        if s >= 7 and (s - 7) % GROUP == 0 and g < 4:
            t, half = g // 2, g % 2
            name = (layer, "values", g)
            k.wait_filled(v, name)
            dim = VALUE_DIM[kind]
            bank = k.bank(name)[:, 0:GROUP * dim]
            y = b.y[:, g % 2, 0:GROUP * dim]
            if g >= 2:
                k.wait_filled(v, (layer, "output", g - 2))
            if kind == "a":
                v.wait_ge(k.out_rstd_ready, 4 * int(layer[1]) + g + 1)
                y3 = y.rearrange("p (h d) -> p h d", h=GROUP)
                k.release(v.tensor_tensor(y3, bank.rearrange("p (h d) -> p h d", h=GROUP),
                                          over_columns(k.out_rstd[:, 0:GROUP], dim), ALU.mult), name)
                k.wait_released(v, name)
                j = int(layer[1])
                steps.link(v.tensor_tensor(y3, y3, over_groups(k.subgain[:, A_V * j:A_V * (j + 1)], GROUP), ALU.mult))
                v.tensor_tensor(y, y, b.gate[:, t, 512 * half:512 * (half + 1)], ALU.mult).then_inc(k.staged, 1)
            if kind == "c":
                k.release(v.tensor_tensor(y, bank, b.gate[:, t, 512 * half:512 * (half + 1)], ALU.mult), name)
                k.wait_released(v, name)
                v.sem_inc(k.staged, 1)
            if kind == "h":
                k.release(v.tensor_copy(y, bank), name)
                k.wait_released(v, name)
                v.sem_inc(k.staged, 1)
        g = (s - 8) // GROUP
        if s >= 8 and (s - 8) % GROUP == 0:
            t, half = g // 2, g % 2
            n = GROUP * VALUE_DIM[kind] // P
            name = (layer, "output", g)
            k.wait_part(v, name)
            chunks, tile = slice(n * half, n * (half + 1)), slice(P * t, P * (t + 1))
            k.release(v.tensor_tensor(k.yT.low[:, chunks, tile], k.bank(name)[:, 0:P * n].rearrange("p (c q) -> p c q", c=n),
                                      k.yT.high[:, chunks, tile].bitcast(F32), ALU.subtract), name)
    out_vector(k, v, layer)


def attention_pool(k, pool, layer):
    if layer[0] == "a":
        for g in range(4):
            pool.wait_ge(k.out_ms_ready, 4 * int(layer[1]) + g + 1)
            inverse_root(k, pool, k.out_ms[:, 0:GROUP], k.out_rstd[:, 0:GROUP], k.out_rstd_ready)



def a_buffers(k, j):
    k.reset_arena()
    b = Buffers()
    b.qT = k.carve(2 * A_HEADS, SEQ).rearrange("p (m h) t -> p m h t", m=2)
    b.kT = k.carve(A_HEADS, SEQ)
    b.v = k.carve(TILES, A_HEADS * A_V)
    b.gate = k.carve(TILES, A_HEADS * A_V)
    b.raw = k.h[:, 0, 0:512]
    b.direct = k.h[:, 0, 512:1024]
    b.swapped = k.h[:, 1, 0:512]
    b.q = k.carve(2, 512)
    b.squares2 = k.carve(2, 512)
    tables = k.h[:, 1, 512:1024].rearrange("p (a d) -> p a d", d=A_QK)
    b.q_tables, b.k_tables = tables[:, 0:2 * TILES, :], tables[:, 2 * TILES:, :]
    b.staged0 = STAGED[f"a{j}"][0]
    b.y, b.squares, b.second = b.q, b.squares2[:, 0, :], b.squares2[:, 1, 0:SEQ]
    return b


STAGED = {"a0": (8, 0), "c": (12, 12), "a1": (16 + 8, 16), "h": (28, 28)}

GROUP_MS = {"a0": 0, "c": 8, "a1": 26, "h": 34}


def a_tensor(k, pe, j):
    b, layer = a_buffers(k, j), f"a{j}"
    staged0 = STAGED[layer][1]
    for kind, i in a_order():
        name = (layer, kind, i)
        if kind == "product":
            if i % 2 == 0:
                products(k, pe, [name, (layer, kind, i + 1)], k.first_granule[layer] + i, k.hT, KC, 512)
        else:
            pe.wait_ge(k.staged, staged0 + i + 1)
            k.take(pe, name)
            for c in range(4):
                last = pe.transpose(k.bank(name)[:, P * c:P * (c + 1)], b.q[:, i % 2, P * c:P * (c + 1)], k.ident)
            k.fill(last, name)
    pe.wait_ge(k.cleared, 1 + 2 * j)
    for kind, i in a_order():
        k.wait_released(pe, (layer, kind, i))
    attention_tensor(k, pe, layer, b)


def a_scalar(k, act, j):
    b, layer = a_buffers(k, j), f"a{j}"
    act.wait_ge(k.cleared, 1 + 2 * j)
    for kind, i in a_order():
        name = (layer, kind, i)
        bank = k.bank(name)
        u, t = i // 2, i % 2
        ahead(k, act, name)
        if kind == "product":
            if i >= 2 and i < 8:
                act.wait_ge(k.group_ms_ready, GROUP_MS[layer] + i - 1)
            k.wait_filled(act, name)
            if u < 4:
                act.activation(b.squares2[:, i % 2, :], bank, ACT.Square, scale=float(A_QK) ** -0.5).then_inc(k.group_squares, 1)
            elif u < 6:
                k.release(act.activation(b.v[:, t, 512 * (u - 4):512 * (u - 3)], bank, ACT.Copy), name)
            else:
                k.release(act.activation(b.gate[:, t, 512 * (u - 6):512 * (u - 5)], bank, ACT.Silu), name)
        else:
            k.wait_filled(act, name)
            src = bank.rearrange("p (c q) -> p c q", c=4)
            heads, tile = slice(4 * (u % 2), 4 * (u % 2) + 4), slice(P * t, P * (t + 1))
            if u < 2:
                act.activation(b.qT[0:A_QK, 0, heads, tile], src[0:A_QK], ACT.Copy)
                k.release(act.activation(b.qT[A_QK:P, 1, heads, tile], src[A_QK:P], ACT.Copy), name)
            else:
                k.release(act.activation(b.kT[:, heads, tile], src, ACT.Copy), name)
    ahead(k, act, (layer, "scores", 0))
    attention_scalar(k, act, layer, b)


def a_vector(k, v, j):
    b, layer = a_buffers(k, j), f"a{j}"
    steps = k.engine_steps["dve"]
    k.wait_filled(v, ("norm", 3 * j, 3))
    rope_tables(k, v, steps, b.q_tables, k.wide("a_q_norm_g", A_QK * j, A_QK))
    rope_tables(k, v, steps, b.k_tables, k.wide("a_k_norm_g", A_QK * j, A_QK))
    v.memset(b.qT[:, :, :, :], 0.0).then_inc(k.cleared, 1)
    v.wait_ge(k.tables_ready, TABLES[layer])

    def reduce(i):
        ahead(k, v, (layer, "product", i))
        v.wait_ge(k.group_squares, 8 * j + i + 1)
        v.tensor_reduce(k.group_ms[:, 8 * (i % 4):8 * (i % 4 + 1)], b.squares2[:, i % 2, :].rearrange("p (g d) -> p g d", g=8),
                        AX, ALU.add).then_inc(k.group_ms_ready, 1)

    for i in range(8):
        if i % 2 == 0:
            reduce(i)
            reduce(i + 1)
        t = i % 2
        name = (layer, "product", i)
        tables = b.q_tables if i < 4 else b.k_tables
        v.wait_ge(k.group_rstd_ready, GROUP_MS[layer] + i + 1)
        if i >= 2:
            k.wait_filled(v, (layer, "turn", i - 2))
        rotate(k, v, steps, k.bank(name), over_columns(k.group_rstd[:, 8 * (i % 4):8 * (i % 4 + 1)], A_QK), 8,
               tables[:, 2 * t, :], tables[:, 2 * t + 1, :], b, b.q[:, i % 2, :], name)
    for i in range(8, 16):
        ahead(k, v, (layer, "product", i))
    ahead(k, v, (layer, "scores", 0))
    attention_vector(k, v, layer, b)


def rotate(k, v, steps, bank, rstd, groups, cos, sin, b, out, name):
    half = A_QK // 2
    n = groups * A_QK

    def grouped(a):
        return a[:, 0:n].rearrange("p (g d) -> p g d", g=groups)

    raw, direct, swapped = grouped(b.raw), grouped(b.direct), grouped(b.swapped)
    k.release(v.tensor_tensor(raw, grouped(bank), rstd, ALU.mult), name)
    k.wait_released(v, name)
    steps.link(v.tensor_tensor(direct, raw, over_groups(cos, groups), ALU.mult))
    steps.link(v.tensor_tensor(swapped[:, :, 0:half], raw[:, :, half:], over_groups(sin[:, 0:half], groups), ALU.mult))
    steps.link(v.tensor_tensor(swapped[:, :, half:], raw[:, :, 0:half], over_groups(sin[:, half:], groups), ALU.mult))
    v.tensor_tensor(grouped(out), direct, swapped, ALU.add).then_inc(k.staged, 1)


TABLES = {"a0": 12, "c": 24, "a1": 36}


def a_pool(k, pool, j):
    for i in range(8):
        n = GROUP_MS[f"a{j}"] + i
        pool.wait_ge(k.group_ms_ready, n + 1)
        inverse_root(k, pool, k.group_ms[:, 8 * (i % 4):8 * (i % 4 + 1)], k.group_rstd[:, 8 * (i % 4):8 * (i % 4 + 1)], k.group_rstd_ready)
    attention_pool(k, pool, f"a{j}")



def b_buffers(k):
    k.reset_arena()
    b = Buffers()
    b.padded = k.carve(KC, CONV_TAPS - 1 + SEQ)
    b.conv = k.carve(KC, SEQ)
    b.gate = k.carve(KC, SEQ)
    b.squares = k.carve(KC, SEQ)
    b.hT = b.squares
    b.gate_in = k.carve(2, 2 * SEQ)
    b.gate_sigmoid = k.carve(2, 2 * SEQ)
    b.root = k.carve(SEQ)
    b.var = k.carve(SEQ)
    b.rstd = k.h[:, 0, 0:SEQ]
    return b


def b_products():
    return [(6 * half + 3 * pair + kind, kind, 2 * half + pair) for half in range(2) for pair in range(2) for kind in range(3)]


def b_tensor(k, pe):
    b = b_buffers(k)
    for i, kind, pair in b_products():
        name, g = ("b", "product", i), k.first_granule["b"] + i
        k.wait_landed(pe, g)
        k.take(pe, name)
        w = k.raw[:, g % RAW, :].rearrange("p (c n) -> p c n", c=KC)
        for half in range(2):
            for c in range(KC):
                last = pe.matmul(k.bank(name)[:, SEQ * half:SEQ * (half + 1)], w[:, c, P * half:P * (half + 1)], b.hT[:, c, :],
                                 start=(c == 0), stop=(c == KC - 1))
        k.fill(last, name)
    for name, what, ready in (("sum", b.conv, k.conv_ready), ("squares", b.squares, k.b_squares_ready)):
        k.take(pe, ("b", name))
        for c in range(KC):
            pe.wait_ge(ready, c + 1)
            last = pe.matmul(k.bank(("b", name))[:, 0:SEQ], k.mean, what[:, c, :], start=(c == 0), stop=(c == KC - 1))
        k.fill(last, ("b", name))
    pe.wait_ge(k.b_mixed, KC)
    out_tensor(k, pe, "b")


def b_scalar(k, act):
    b = b_buffers(k)
    for i, kind, pair in b_products():
        if kind == 0:
            continue
        name = ("b", "product", i)
        ahead(k, act, name)
        k.wait_filled(act, name)
        if pair >= 2:
            act.wait_ge(k.b_pair_done, pair - 1)
        dst = (b.gate_in if kind == 1 else b.gate_sigmoid)[:, pair % 2, :]
        for half in range(2):
            c = 2 * pair + half
            last = act.activation(dst[:, SEQ * half:SEQ * (half + 1)], k.bank(name)[:, SEQ * half:SEQ * (half + 1)], ACT.Sigmoid,
                                  bias=k.column("b_b_in", c, kind))
        if kind == 1:
            k.release(last, name)
        else:
            last.then_inc(k.b_gate_ready, 1)
    ahead(k, act, ("b", "squares"))
    for c in range(KC):
        act.wait_ge(k.b_mean_gone, c + 1)
        act.activation(b.squares[:, c, :], b.conv[:, c, :], ACT.Square).then_inc(k.b_squares_ready, 1)
    act.wait_ge(k.b_var_ready, 1)
    act.activation(b.root, b.var, ACT.Sqrt).then_inc(k.b_root_ready, 1)
    for c in range(KC):
        act.wait_ge(k.b_normed, c + 1)
        act.activation(b.squares[:, c, :], b.conv[:, c, :], ACT.Silu, scale=k.column("b_ln_g", c), bias=k.column("b_ln_b", c))\
           .then_inc(k.b_silu_ready, 1)
    out_scalar(k, act, "b")


def b_vector(k, v):
    b = b_buffers(k)
    steps = k.engine_steps["dve"]
    pad = CONV_TAPS - 1
    steps.link(v.memset(b.padded[:, :, 0:pad], 0.0))
    for pair in range(4):
        a_name, _, g_name = (("b", "product", 6 * (pair // 2) + 3 * (pair % 2) + kind) for kind in range(3))
        k.wait_filled(v, a_name)
        k.wait_released(v, ("b", "product", 6 * (pair // 2) + 3 * (pair % 2) + 1))
        for half in range(2):
            c = 2 * pair + half
            cols = slice(SEQ * half, SEQ * (half + 1))
            last = v.scalar_tensor_tensor(b.padded[:, c, pad:], k.bank(a_name)[:, cols], k.column("b_b_in", c, 0),
                                          b.gate_in[:, pair % 2, cols], ALU.add, ALU.mult)
        k.release(last, a_name)
        v.wait_ge(k.b_gate_ready, pair + 1)
        for half in range(2):
            c = 2 * pair + half
            cols = slice(SEQ * half, SEQ * (half + 1))
            last = v.scalar_tensor_tensor(b.gate[:, c, :], k.bank(g_name)[:, cols], k.column("b_b_in", c, 2),
                                          b.gate_sigmoid[:, pair % 2, cols], ALU.add, ALU.mult)
        k.release(last, g_name)
        k.wait_released(v, g_name)
        v.sem_inc(k.b_pair_done, 1)
        ahead(k, v, ("b", "product", 3 * pair + 3) if pair < 3 else ("b", "squares"))
        for tap in range(CONV_TAPS):
            for half in range(2):
                c = 2 * pair + half
                window, weight = b.padded[:, c, tap:tap + SEQ], k.column("b_conv_w", c, tap)
                if tap > 0:
                    v.wait_ge(steps.sem, steps.done - 1)
                if tap == 0:
                    last = v.tensor_scalar(b.conv[:, c, :], window, weight, k.column("b_conv_b", c), ALU.mult, ALU.add)
                else:
                    last = v.scalar_tensor_tensor(b.conv[:, c, :], window, weight, b.conv[:, c, :], ALU.mult, ALU.add)
                if tap == CONV_TAPS - 1:
                    last.then_inc(k.conv_ready, 1)
                else:
                    last.then_inc(steps.sem, 1)
                    steps.done += 1
            if tap == CONV_TAPS - 2:
                v.wait_ge(steps.sem, steps.done)
    v.wait_ge(k.conv_ready, KC)
    k.wait_filled(v, ("b", "sum"))
    for c in range(KC):
        v.tensor_tensor(b.conv[:, c, :], b.conv[:, c, :], k.bank(("b", "sum"))[:, 0:SEQ], ALU.subtract).then_inc(k.b_mean_gone, 1)
    v.wait_ge(k.b_mean_gone, KC)
    v.sem_inc(k.freed[k.banks.at[("b", "sum")][0]], 1)
    k.wait_filled(v, ("b", "squares"))
    k.release(v.tensor_scalar(b.var, k.bank(("b", "squares"))[:, 0:SEQ], EPS, None, ALU.add), ("b", "squares"))
    k.wait_released(v, ("b", "squares"))
    v.sem_inc(k.b_var_ready, 1)
    v.wait_ge(k.b_root_ready, 1)
    steps.link(v.reciprocal(b.rstd, b.root))
    for c in range(KC):
        v.tensor_tensor(b.conv[:, c, :], b.conv[:, c, :], b.rstd, ALU.mult).then_inc(k.b_normed, 1)
    for c in range(KC):
        v.wait_ge(k.b_silu_ready, c + 1)
        to_parts(k, v, b.squares[:, c, :], b.gate[:, c, :], c, k.b_mixed)
    out_vector(k, v, "b")


def to_parts(k, v, a, gate, c, ready):
    steps = k.engine_steps["dve"]
    steps.link(v.tensor_tensor(a, a, gate, ALU.mult))
    steps.link(v.tensor_copy(k.yT.high[:, c, :], a))
    v.tensor_tensor(k.yT.low[:, c, :], a, k.yT.high[:, c, :].bitcast(F32), ALU.subtract).then_inc(ready, 1)



def c_buffers(k):
    k.reset_arena()
    b = Buffers()
    b.qT = k.carve(C_HEADS, SEQ)
    b.kT = k.carve(C_HEADS, SEQ)
    b.qropeT = k.carve(C_HEADS // 2, SEQ)
    b.kropeT = k.carve(2, SEQ)
    b.v = k.carve(TILES, C_WIDTH)
    b.gate = k.carve(TILES, C_WIDTH)
    b.y = k.carve(2, 512)
    b.q_tables = k.carve(2 * TILES, C_ROPE)
    b.k_tables = k.carve(2 * TILES, C_ROPE)
    b.staged0 = STAGED["c"][0]
    b.lowT = k.yT
    a = k.h[:, :, :].rearrange("p t d -> p (t d)")
    b.low, b.q = a[:, 0:1024].rearrange("p (s n) -> p s n", s=2), a[:, 0:1024].rearrange("p (s n) -> p s n", s=2)
    b.raw, b.direct, b.swapped = a[:, 1024:1152], a[:, 1152:1280], a[:, 1280:1408]
    b.k = b.y[:, :, 0:256]
    b.junk = a[:, 1536:2048]
    return b


C_WIDTH = C_HEADS * C_V


def c_tensor(k, pe):
    b = c_buffers(k)
    g = k.first_granule["c"]
    for kind, i in c_order():
        name = ("c", kind, i)
        bank = k.bank(name)
        if kind == "low":
            if i == 0:
                products(k, pe, [name, ("c", kind, 1)], g, k.hT, KC, C_HEAD_IN)
        if kind == "gate" and i % 2 == 0:
            products(k, pe, [name, ("c", kind, i + 1)], g + 2 + i, k.hT, KC, 512)
        if kind == "lowturn":
            pe.wait_ge(k.c_low_staged, i + 1)
            k.take(pe, name)
            for c in range(4):
                last = pe.transpose(bank[:, P * c:P * (c + 1)], b.low[:, i, P * c:P * (c + 1)], k.ident)
            k.fill(last, name)
        if kind == "q" and i % 2 == 0:
            for t in range(TILES):
                k.wait_released(pe, ("c", "lowturn", t))
            products(k, pe, [name, ("c", kind, i + 1)], g + 6 + 2 * (i // 4), b.lowT, C_Q_LORA // P, 2 * C_QK,
                     2 * C_QK * (i // 2 % 2), 1)
        if kind == "kv" and i % 2 == 0:
            products(k, pe, [name, ("c", kind, i + 1)], g + 7, b.lowT[:, 2:3, :], 1, 512, 512 * (i // 2), 1)
        if kind == "qturn":
            pe.wait_ge(k.c_q_staged, i + 1)
            k.take(pe, name)
            for c in range(3):
                last = pe.transpose(bank[:, P * c:P * (c + 1)], b.q[:, i % 2, P * c:P * (c + 1)], k.ident)
            k.fill(last, name)
        if kind == "kturn":
            pe.wait_ge(k.c_k_staged, i + 1)
            k.take(pe, name)
            for c in range(2):
                last = pe.transpose(bank[:, P * c:P * (c + 1)], b.k[:, i % 2, P * c:P * (c + 1)], k.ident)
            k.fill(last, name)
    pe.wait_ge(k.cleared, 2)
    for kind, i in c_order():
        k.wait_released(pe, ("c", kind, i))
    attention_tensor(k, pe, "c", b)


def c_scalar(k, act):
    b = c_buffers(k)
    act.wait_ge(k.cleared, 2)
    squares = GROUP_MS["c"]
    steps = k.engine_steps["act"]
    for kind, i in c_order():
        name = ("c", kind, i)
        bank = k.bank(name)
        ahead(k, act, name)
        k.wait_filled(act, name)
        tile = slice(P * (i % 2), P * (i % 2 + 1))
        if kind in ("low", "q", "kv"):
            parts = {
                "low": ((0, C_Q_LORA), (C_Q_LORA, C_KV_LORA), (C_Q_LORA + C_KV_LORA, C_ROPE)),
                "q": ((0, C_NOPE), (C_NOPE, C_ROPE), (C_QK, C_NOPE), (C_QK + C_NOPE, C_ROPE)),
                "kv": ((0, C_NOPE), (C_NOPE + C_V, C_NOPE)),
            }[kind]
            if squares - GROUP_MS["c"] >= 4:
                act.wait_ge(k.c_roots_used, squares - GROUP_MS["c"] - 3)
            col = 8 * (squares % 4)
            junk = 0
            for m, (first, n) in enumerate(parts):
                last = act.activation(b.junk[:, junk:junk + n], bank[:, first:first + n],
                                      ACT.Square, scale=float(n) ** -0.5, accum_out=k.group_ms[:, col + m:col + m + 1])
                junk += n
            last.then_inc(k.group_ms_ready, 1)
            squares += 1
            act.wait_ge(k.group_ms_ready, squares)
            if kind == "kv":
                heads = bank.rearrange("p (h n) -> p h n", h=2)
                dst = b.v[:, i % 2, 256 * (i // 2):256 * (i // 2 + 1)].rearrange("p (h n) -> p h n", h=2)
                act.activation(dst, heads[:, :, C_NOPE:], ACT.Copy).then_inc(k.c_v_ready, 1)
        if kind == "gate":
            u, t = i // 2, i % 2
            k.release(act.activation(b.gate[:, t, 512 * u:512 * (u + 1)], bank, ACT.Silu), name)
        if kind == "lowturn":
            for c in range(3):
                gain = k.column("c_cq_norm_g", c) if c < 2 else k.column("c_ckv_norm_g", 0)
                act.activation(b.lowT.high[:, c, tile], bank[:, P * c:P * (c + 1)], ACT.Copy, scale=gain)
            act.activation(b.kropeT[0:C_ROPE, 0, tile], bank[0:C_ROPE, 3 * P:4 * P], ACT.Copy)
            act.activation(b.kropeT[C_ROPE:P, 1, tile], bank[C_ROPE:P, 3 * P:4 * P], ACT.Copy).then_inc(k.part_ready, 1)
        if kind == "qturn":
            pair = i // 2
            act.activation(b.qT[:, 2 * pair:2 * pair + 2, tile], bank[:, 0:2 * P].rearrange("p (h q) -> p h q", h=2), ACT.Copy)
            k.release(act.activation(b.qropeT[:, pair, tile], bank[:, 2 * P:3 * P], ACT.Copy), name)
        if kind == "kturn":
            pair = i // 2
            k.release(act.activation(b.kT[:, 2 * pair:2 * pair + 2, tile], bank[:, 0:2 * P].rearrange("p (h q) -> p h q", h=2),
                                     ACT.Copy), name)
    ahead(k, act, ("c", "scores", 0))
    attention_scalar(k, act, "c", b)


def c_vector(k, v):
    b = c_buffers(k)
    steps = k.engine_steps["dve"]
    rope_tables(k, v, steps, b.q_tables, k.wide("c_q_norm_g", C_NOPE, C_ROPE))
    rope_tables(k, v, steps, b.k_tables, k.wide("c_k_norm_g", C_NOPE, C_ROPE))
    v.memset(b.kropeT[:, :, :], 0.0).then_inc(k.cleared, 1)
    v.wait_ge(k.tables_ready, TABLES["c"])
    n = 0
    for kind, i in c_order():
        name = ("c", kind, i)
        bank = k.bank(name)
        ahead(k, v, name)
        if kind == "lowturn":
            tile = slice(P * i, P * (i + 1))
            k.wait_part(v, name)
            for c in range(3):
                gain = k.column("c_cq_norm_g", c) if c < 2 else k.column("c_ckv_norm_g", 0)
                last = v.scalar_tensor_tensor(b.lowT.low[:, c, tile], bank[:, P * c:P * (c + 1)], gain,
                                              b.lowT.high[:, c, tile].bitcast(F32), ALU.mult, ALU.subtract)
            k.release(last, name)
        if kind not in ("low", "q", "kv"):
            continue
        col = 8 * ((GROUP_MS["c"] + n) % 4)
        v.wait_ge(k.group_rstd_ready, GROUP_MS["c"] + n + 1)
        n += 1

        def root(m):
            return k.group_rstd[:, col + m:col + m + 1]

        t = i % 2
        if kind == "low":
            low = b.low[:, i, :]
            v.tensor_scalar(low[:, 0:C_Q_LORA], bank[:, 0:C_Q_LORA], root(0), None, ALU.mult)
            v.tensor_scalar(low[:, C_Q_LORA:C_Q_LORA + C_KV_LORA], bank[:, C_Q_LORA:C_Q_LORA + C_KV_LORA], root(1), None, ALU.mult)
            rope_one(k, v, steps, bank[:, C_Q_LORA + C_KV_LORA:C_HEAD_IN], root(2), b.k_tables[:, 2 * t, :],
                     b.k_tables[:, 2 * t + 1, :], b, low[:, 3 * P:3 * P + C_ROPE])
            k.release(v.tensor_copy(low[:, 3 * P + C_ROPE:4 * P], low[:, 3 * P:3 * P + C_ROPE]), name)
            k.wait_released(v, name)
            v.sem_inc(k.c_low_staged, 1)
        if kind == "q":
            q = b.q[:, t, :]
            if i < 2:
                k.wait_filled(v, ("c", "lowturn", 1))
            else:
                k.wait_filled(v, ("c", "qturn", i - 2))
            for m in range(2):
                v.scalar_tensor_tensor(q[:, P * m:P * (m + 1)], bank[:, C_QK * m:C_QK * m + C_NOPE], root(2 * m),
                                       k.wide("c_q_norm_g", 0, C_NOPE), ALU.mult, ALU.mult)
                rope_one(k, v, steps, bank[:, C_QK * m + C_NOPE:C_QK * (m + 1)], root(2 * m + 1), b.q_tables[:, 2 * t, :],
                         b.q_tables[:, 2 * t + 1, :], b, q[:, 2 * P + C_ROPE * m:2 * P + C_ROPE * (m + 1)])
            v.sem_inc(k.freed[k.banks.at[name][0]], 1)
            v.sem_inc(k.c_q_staged, 1)
        if kind == "kv":
            kk = b.k[:, t, :]
            if i >= 2:
                k.wait_filled(v, ("c", "kturn", i - 2))
            v.wait_ge(k.c_v_ready, i + 1)
            for m in range(2):
                last = v.scalar_tensor_tensor(kk[:, P * m:P * (m + 1)], bank[:, 256 * m:256 * m + C_NOPE], root(m),
                                              k.wide("c_k_norm_g", 0, C_NOPE), ALU.mult, ALU.mult)
            k.release(last, name)
            k.wait_released(v, name)
            v.sem_inc(k.c_k_staged, 1)
        v.sem_inc(k.c_roots_used, 1)
    ahead(k, v, ("c", "scores", 0))
    attention_vector(k, v, "c", b)


def rope_one(k, v, steps, bank, root, cos, sin, b, out):
    half = C_ROPE // 2
    d, s = b.direct[:, 0:C_ROPE], b.swapped[:, 0:C_ROPE]
    v.scalar_tensor_tensor(d, bank, root, cos, ALU.mult, ALU.mult).then_inc(steps.sem, 1)
    v.scalar_tensor_tensor(s[:, 0:half], bank[:, half:], root, sin[:, 0:half], ALU.mult, ALU.mult).then_inc(steps.sem, 1)
    v.scalar_tensor_tensor(s[:, half:], bank[:, 0:half], root, sin[:, half:], ALU.mult, ALU.mult).then_inc(steps.sem, 1)
    steps.done += 3
    v.wait_ge(steps.sem, steps.done)
    steps.link(v.tensor_tensor(out, d, s, ALU.add))


def c_pool(k, pool):
    n = GROUP_MS["c"]
    for kind, i in c_order():
        if kind in ("low", "q", "kv"):
            pool.wait_ge(k.group_ms_ready, n + 1)
            m = {"low": 3, "q": 4, "kv": 2}[kind]
            col = 8 * (n % 4)
            inverse_root(k, pool, k.group_ms[:, col:col + m], k.group_rstd[:, col:col + m], k.group_rstd_ready)
            n += 1



def h_buffers(k):
    k.reset_arena()
    b = Buffers()
    b.qT = k.carve(H_HEADS // 2, SEQ)
    b.kT = k.carve(H_KV_HEADS, SEQ)
    b.v = k.carve(TILES, H_KV_HEADS * H_DIM)
    b.q = k.carve(TILES, 512)
    b.k = k.carve(TILES, P)
    b.squares = k.carve(2, 512)
    b.y = k.carve(2, 512)
    b.s = k.carve(2, SEQ)
    b.shift = k.carve(2, 2 * SEQ)
    b.padded = k.carve(4, H_TAPS - 1 + SEQ)
    b.conv = k.carve(4, SEQ)
    b.raw = k.carve(512)
    b.staged0 = STAGED["h"][0]
    return b


def h_groups(kind):
    return (H_HEADS, "hy_q_gain_2") if kind == "q" else (H_KV_HEADS, "hy_k_gain_2")


def h_tensor(k, pe):
    b = h_buffers(k)
    g = k.first_granule["h"]
    for kind, i in h_order():
        name = ("h", kind, i)
        if kind in ("q", "kv"):
            if i == 0:
                products(k, pe, [name, ("h", kind, 1)], g, k.hT, KC, 512 if kind == "q" else 256)
                g += 2
        if kind in ("shift", "value", "gate"):
            channel_product(k, pe, name, g)
            g += 1
        if kind == "qturn":
            pe.wait_ge(k.h_q_staged, i + 1)
            k.take(pe, name)
            for c in range(4):
                last = pe.transpose(k.bank(name)[:, P * c:P * (c + 1)], b.q[:, i, P * c:P * (c + 1)], k.ident)
            k.fill(last, name)
        if kind == "kturn":
            pe.wait_ge(k.h_k_staged, i + 1)
            k.take(pe, name)
            k.fill(pe.transpose(k.bank(name)[:, 0:P], b.k[:, i, :], k.ident), name)
    for kind, i in h_order():
        k.wait_released(pe, ("h", kind, i))
    attention_tensor(k, pe, "h", b)


def h_scalar(k, act):
    b = h_buffers(k)
    act.wait_ge(k.cleared, 4)
    n = GROUP_MS["h"]
    for kind, i in h_order():
        name = ("h", kind, i)
        bank = k.bank(name)
        ahead(k, act, name)
        k.wait_filled(act, name)
        tile = slice(P * (i % 2), P * (i % 2 + 1))
        if kind in ("q", "kv"):
            groups, _ = h_groups(kind)
            if kind == "kv":
                act.wait_ge(k.group_ms_ready, n - 1)
                act.activation(b.v[:, i, :], bank[:, groups * H_DIM:2 * groups * H_DIM], ACT.Copy)
            act.activation(b.squares[:, i, 0:groups * H_DIM], bank[:, 0:groups * H_DIM], ACT.Square,
                           scale=float(H_DIM) ** -0.5).then_inc(k.group_squares, 1)
            n += 1
        if kind == "shift":
            k.release(act.activation(b.shift[:, i, :], bank, ACT.Copy), name)
        if kind == "qturn":
            k.release(act.activation(b.qT[:, :, tile], bank.rearrange("p (c q) -> p c q", c=4), ACT.Copy), name)
        if kind == "kturn":
            act.activation(b.kT[0:H_DIM, 0, tile], bank[0:H_DIM, 0:P], ACT.Copy)
            k.release(act.activation(b.kT[H_DIM:P, 1, tile], bank[H_DIM:P, 0:P], ACT.Copy), name)
    ahead(k, act, ("h", "scores", 0))
    attention_scalar(k, act, "h", b)


def h_vector(k, v):
    b = h_buffers(k)
    steps = k.engine_steps["dve"]
    pad = H_TAPS - 1
    v.memset(b.kT[:, :, :], 0.0).then_inc(k.cleared, 1)
    steps.link(v.memset(b.padded[:, :, 0:pad], 0.0))
    n = 0
    for kind, i in h_order():
        name = ("h", kind, i)
        bank = k.bank(name)
        ahead(k, v, name)
        if kind in ("q", "kv"):
            groups, gain = h_groups(kind)
            count = GROUP_MS["h"] + n
            col = 8 * n
            v.wait_ge(k.group_squares, 16 + n + 1)
            v.tensor_reduce(k.group_ms[:, col:col + groups], b.squares[:, i, 0:groups * H_DIM].rearrange("p (g d) -> p g d", g=groups),
                            AX, ALU.add).then_inc(k.group_ms_ready, 1)
            v.wait_ge(k.group_rstd_ready, count + 1)
            rstd = over_columns(k.group_rstd[:, col:col + groups], H_DIM)
            raw = b.raw[:, 0:groups * H_DIM].rearrange("p (g d) -> p g d", g=groups)
            k.release(v.tensor_tensor(raw, bank[:, 0:groups * H_DIM].rearrange("p (g d) -> p g d", g=groups), rstd, ALU.mult), name)
            k.wait_released(v, name)
            gains = over_groups(k.wide(gain), groups)
            if kind == "q":
                for side in range(2):
                    out = b.q[:, i, :].rearrange("p (j s d) -> p j s d", s=2, d=H_DIM)[:, :, side, :]
                    heads = slice(4 * side, 4 * side + 4)
                    steps.link(v.tensor_tensor(out, raw[:, heads, :], over_groups(k.wide(gain), 4), ALU.mult))
                v.sem_inc(k.h_q_staged, 1)
            else:
                v.tensor_tensor(b.k[:, i, :].rearrange("p (g d) -> p g d", g=groups), raw, gains, ALU.mult).then_inc(k.h_k_staged, 1)
            n += 1
        if kind == "value":
            k.wait_released(v, ("h", "shift", i))
            k.wait_filled(v, name)
            k.release(v.tensor_tensor(b.padded[:, 2 * i:2 * i + 2, pad:], bank.rearrange("p (c t) -> p c t", c=2),
                                      b.shift[:, i, :].rearrange("p (c t) -> p c t", c=2), ALU.mult), name)
            k.wait_released(v, name)
            for tap in range(H_TAPS):
                for c in (2 * i, 2 * i + 1):
                    window, weight = b.padded[:, c, tap:tap + SEQ], k.column("hy_conv_w_2", c, tap)
                    if tap == 0:
                        steps.link(v.tensor_scalar(b.conv[:, c, :], window, weight, None, ALU.mult))
                    else:
                        steps.link(v.scalar_tensor_tensor(b.conv[:, c, :], window, weight, b.conv[:, c, :], ALU.mult, ALU.add))
        if kind == "gate":
            k.wait_filled(v, name)
            mixed, chunks = b.conv[:, 2 * i:2 * i + 2, :], slice(4 + 2 * i, 6 + 2 * i)
            steps.link(v.tensor_tensor(mixed, bank.rearrange("p (c t) -> p c t", c=2), mixed, ALU.mult))
            steps.link(v.tensor_copy(k.yT.high[:, chunks, :], mixed))
            k.release(v.tensor_tensor(k.yT.low[:, chunks, :], mixed, k.yT.high[:, chunks, :].bitcast(F32), ALU.subtract), name)
    ahead(k, v, ("h", "scores", 0))
    attention_vector(k, v, "h", b)


def h_pool(k, pool):
    for n in range(4):
        groups = H_HEADS if n < 2 else H_KV_HEADS
        pool.wait_ge(k.group_ms_ready, GROUP_MS["h"] + n + 1)
        inverse_root(k, pool, k.group_ms[:, 8 * n:8 * n + groups], k.group_rstd[:, 8 * n:8 * n + groups], k.group_rstd_ready)



def ffn_buffers(k):
    k.reset_arena()
    b = Buffers()
    b.silu = k.carve(TILES, FF_STEP)
    b.hidden = k.carve(TILES, FF_STEP)
    b.hiddenT = hidden_parts(k)
    return b


def hidden_parts(k):
    return k.yT.rearrange("p c n -> p (c n)")[:, 0:2 * FF_STEP].rearrange("p (t n) -> p t n", t=2)


def ffn_tensor(k, pe):
    b = ffn_buffers(k)
    g = k.first_granule["ffn"]
    for kind, j, t in ffn_order():
        name = ("ffn", kind, j, t)
        if kind in ("gate", "up") and t == 0:
            products(k, pe, [name, ("ffn", kind, j, 1)], g, k.hT, KC, FF_STEP)
            g += 2
        if kind == "turn":
            k.wait_released(pe, ("ffn", "up", j, t))
            k.take(pe, name)
            for c in range(4):
                last = pe.transpose(k.bank(name)[:, P * c:P * (c + 1)], b.hidden[:, t, P * c:P * (c + 1)], k.ident)
            k.fill(last, name)
        if kind == "down":
            for t in range(TILES):
                k.wait_released(pe, ("ffn", "turn", j, t))
            for half in range(2):
                first, final = j == 0 and half == 0, j == FF_STEPS - 1 and half == 1
                wait_split(k, pe, g)
                w = granule_parts(k, g, 2)
                for n in range(2):
                    for t in range(TILES):
                        out = ("ffn", "out", 2 * n + t)
                        if first:
                            k.take(pe, out)
                        for c in range(2):
                            at = P * (2 * half + c)
                            last = three_passes(pe, k.bank(out), b.hiddenT[:, t, at:at + P], w[:, c, 512 * n:512 * (n + 1)],
                                                first and c == 0, final and c == 1)
                        if final:
                            k.fill(last, out)
                if not final:
                    last.then_inc(k.half_done, 1)
                g += 1


def ffn_scalar(k, act):
    b = ffn_buffers(k)
    for kind, j, t in ffn_order():
        name = ("ffn", kind, j, t)
        if kind == "down":
            continue
        ahead(k, act, name)
        if kind == "gate":
            if j > 0:
                k.wait_released(act, ("ffn", "up", j - 1, t))
            k.wait_filled(act, name)
            k.release(act.activation(b.silu[:, t, :], k.bank(name), ACT.Silu), name)
        if kind == "turn":
            k.wait_filled(act, name)
            act.activation(b.hiddenT.high[:, t, :], k.bank(name), ACT.Copy).then_inc(k.part_ready, 1)
    out_scalar(k, act, "ffn")


def ffn_vector(k, v):
    b = ffn_buffers(k)
    for kind, j, t in ffn_order():
        name = ("ffn", kind, j, t)
        if kind == "down":
            continue
        ahead(k, v, name)
        if kind == "up":
            k.wait_filled(v, name)
            k.wait_released(v, ("ffn", "gate", j, t))
            if j > 0:
                k.wait_filled(v, ("ffn", "turn", j - 1, t))
            k.release(v.tensor_tensor(b.hidden[:, t, :], k.bank(name), b.silu[:, t, :], ALU.mult), name)
        if kind == "turn":
            k.wait_part(v, name)
            k.release(v.tensor_tensor(b.hiddenT.low[:, t, :], k.bank(name), b.hiddenT.high[:, t, :].bitcast(F32), ALU.subtract), name)
    out_vector(k, v, "ffn")



def r_buffers(k):
    k.reset_arena()
    b = Buffers()
    b.padded = k.carve(KC, R_TAPS - 1 + SEQ)
    b.conv = k.carve(KC, SEQ)
    b.keep = k.carve(KC, SEQ)
    b.take = k.carve(KC, SEQ)
    b.gelu = k.carve(KC, SEQ)
    b.decay = k.carve(KC, SEQ)
    b.root = k.h[:, :, :].rearrange("p t d -> p (t d)").rearrange("p (c n) -> p c n", c=KC)
    return b


def r_tensor(k, pe):
    b = r_buffers(k)
    g = k.first_granule["r"]
    for kind, i in r_order():
        name = ("r", kind, i)
        if kind in ("x", "y"):
            channel_product(k, pe, name, g)
            g += 1
        else:
            if i == 0:
                k.wait_landed(pe, g)
                pe.wait_ge(k.gates_ready, 16)
            pe.wait_ge(k.r_conv_ready, i + 1)
            k.take(pe, name)
            w = k.raw[:, g % RAW, :].rearrange("p (g h n) -> p g h n", g=2, h=R_HEADS)
            for gate in range(2):
                last = pe.matmul(k.bank(name)[:, SEQ * gate:SEQ * (gate + 1)], w[:, gate, i, :], b.conv[:, i, :], start=True, stop=True)
            k.fill(last, name)
            if i == R_HEADS - 1:
                g += 1
    pe.wait_ge(k.r_mixed, KC)
    out_tensor(k, pe, "r")


def r_scalar(k, act):
    b = r_buffers(k)
    for kind, i in r_order():
        name = ("r", kind, i)
        bank = k.bank(name)
        ahead(k, act, name)
        k.wait_filled(act, name)
        if kind == "x":
            k.release(act.activation(b.padded[:, 2 * i:2 * i + 2, R_TAPS - 1:], bank.rearrange("p (c t) -> p c t", c=2), ACT.Copy), name)
        if kind == "gates":
            act.activation(b.keep[:, i, :], bank[:, 0:SEQ], ACT.Sigmoid, bias=k.column("rg_gate_a_b_2", i))
            k.release(act.activation(b.take[:, i, :], bank[:, SEQ:2 * SEQ], ACT.Sigmoid, bias=k.column("rg_gate_x_b_2", i)), name)
        if kind == "y":
            k.release(act.activation(b.gelu[:, 2 * i:2 * i + 2, :], bank.rearrange("p (c t) -> p c t", c=2), ACT.Gelu_apprx_tanh), name)
    for h in range(R_HEADS):
        k.wait_released(act, ("r", "gates", h))
    act.wait_ge(k.r_decay_ready, 1)
    for c in range(KC):
        act.activation(b.decay[:, c, :], b.keep[:, c, :], ACT.Exp, scale=k.negdecay[:, c:c + 1])
        act.activation(b.keep[:, c, :], b.keep[:, c, :], ACT.Tanh, scale=k.decay[:, c:c + 1]).then_inc(k.r_decays, 1)
    for c in range(KC):
        act.wait_ge(k.r_root_in, c + 1)
        act.activation(b.root[:, c, :], b.keep[:, c, :], ACT.Sqrt).then_inc(k.r_root_ready, 1)
    out_scalar(k, act, "r")


def r_vector(k, v):
    b = r_buffers(k)
    steps = k.engine_steps["dve"]
    pad = R_TAPS - 1
    v.tensor_scalar(k.negdecay, k.decay, -1.0, None, ALU.mult).then_inc(k.r_decay_ready, 1)
    steps.link(v.memset(b.padded[:, :, 0:pad], 0.0))
    for pair in range(4):
        ahead(k, v, ("r", "x", pair))
        k.wait_released(v, ("r", "x", pair))
        for tap in range(R_TAPS):
            for c in (2 * pair, 2 * pair + 1):
                window, weight = b.padded[:, c, tap:tap + SEQ], k.column("rg_conv_w_2", c, tap)
                if tap == 0:
                    last = v.tensor_scalar(b.conv[:, c, :], window, weight, k.column("rg_conv_b_2", c), ALU.mult, ALU.add)
                else:
                    last = v.scalar_tensor_tensor(b.conv[:, c, :], window, weight, b.conv[:, c, :], ALU.mult, ALU.add)
                if tap == R_TAPS - 1:
                    last.then_inc(k.r_conv_ready, 1)
                else:
                    steps.link(last)
    for kind, i in r_order()[4:]:
        ahead(k, v, ("r", kind, i))
    for c in range(KC):
        v.wait_ge(k.r_decays, c + 1)
        square = b.padded[:, c, 0:SEQ]
        steps.link(v.tensor_tensor(square, b.decay[:, c, :], b.decay[:, c, :], ALU.mult))
        v.scalar_tensor_tensor(b.keep[:, c, :], square, 1.0, b.keep[:, c, :], ALU.add, ALU.mult).then_inc(k.r_root_in, 1)
        v.tensor_tensor(b.conv[:, c, :], b.conv[:, c, :], b.take[:, c, :], ALU.mult).then_inc(steps.sem, 1)
        steps.done += 1
    v.wait_ge(steps.sem, steps.done)
    for h in range(4):
        k.wait_released(v, ("r", "y", h))
    for c in range(KC):
        v.wait_ge(k.r_root_ready, c + 1)
        steps.link(v.memset(b.root[:, c, 0:1], 1.0))
        steps.link(v.tensor_tensor(b.conv[:, c, :], b.conv[:, c, :], b.root[:, c, :], ALU.mult))
        steps.link(v.tensor_tensor_scan(b.padded[:, c, 0:SEQ], b.decay[:, c, :], b.conv[:, c, :], 0.0, ALU.mult, ALU.add))
        to_parts(k, v, b.padded[:, c, 0:SEQ], b.gelu[:, c, :], c, k.r_mixed)
    out_vector(k, v, "r")



SLOTS = P
CAP = float(SLOTS)
N_WORK = 2 + N_EXPERTS


def moe_buffers(k):
    k.reset_arena()
    b = Buffers()
    b.placed = k.carve(TILES, SLOTS)
    b.unplaced = k.carve(TILES, P)
    b.silu = k.carve(2, FF_STEP)
    b.hidden = k.carve(2, FF_STEP)
    b.out = k.carve(D)
    b.hiddenT = hidden_parts(k)
    b.tokens = k.yT.rearrange("p c n -> p (c n)")[:, 2 * FF_STEP:].rearrange("p (c n) -> p c n", c=KC)
    return b


def short_turns(t):
    return (MOE_SHORT // 4) * t


def rounds(k, eng, one_round):
    with eng.Fori(0, N_EXPERTS) as t:
        one_round(t, t)
    return more_rounds(k, eng, lambda t, r: one_round(t, table_entry(k, eng, r + 1) if eng is k.nc.sync else None))


def more_rounds(k, eng, one_round):
    eng.wait_ge(k.work_ready, 1)
    n = eng.value_load(k.work[0:1, 0:1], min_val=0, max_val=N_EXPERTS)
    with eng.If(n > 0):
        with eng.Fori(0, n) as r:
            one_round(r + N_EXPERTS, r)
    with eng.Else():
        pass
    return n


def table_entry(k, eng, i):
    at = k.work[0:1, i:i + 1] if isinstance(i, int) else k.work[0:1, bass.ds(i, 1)]
    return eng.value_load(at, min_val=0, max_val=N_EXPERTS - 1)



def round_granules():
    order, granules, halves = moe_order(), [], 0
    for index, (kind, j) in enumerate(order):
        if kind in ("gate", "up"):
            halves += 1
            granules.append((kind, j, 0, halves, index - 1))
            granules.append((kind, j, 1, (kind, j), index))
        if kind == "down":
            for half in range(2):
                if j == FF_STEPS - 1 and half == 1:
                    granules.append((kind, j, half, ("expert", 1), index - 1))
                else:
                    halves += 1
                    granules.append((kind, j, half, halves, index - 1))
    return granules, halves


ROUND_GRANULES, ROUND_HALVES = round_granules()
ROUND = len(ROUND_GRANULES)
assert ROUND % RAW == 0 and ROUND % SPLIT == 0


def round_number(k, i, t):
    before = k.granules[-1]
    return before.number + 1 + i + ROUND * t


def load_round(k, sp, t, expert):
    for i, (kind, j, half, _, _) in enumerate(ROUND_GRANULES):
        slot = (k.first_granule["moe"] + i) % RAW
        sp.wait_ge(k.low_ready, round_number(k, i - RAW, t) + 1)
        a = k.w[f"moe_w_{kind}_2"][0][bass.ds(expert, 1)].rearrange("e a b -> (e a) b")
        if kind == "down":
            row = FF_STEP * j + 2 * P * half
            src, c = a[row:row + 2 * P, :], 2
        else:
            src, c = a[4 * P * half:4 * P * (half + 1), FF_STEP * j:FF_STEP * (j + 1)], 4
        dst = k.raw[:, slot, :].rearrange("p (c n) -> p c n", c=c)
        sp.dma_start(dst, src.rearrange("(c p) n -> p c n", p=P)).then_inc(k.landed[slot], 16)


def split_round(k, eng, done, index, t):
    first = k.first_granule["moe"]
    while done < ROUND and (done < SPLIT or ROUND_GRANULES[done - SPLIT][4] < index):
        i = done
        if eng is k.nc.scalar:
            if i >= SPLIT:
                last = ROUND_GRANULES[i - SPLIT][3]
                if isinstance(last, int):
                    eng.wait_ge(k.half_done, k.halves + last + ROUND_HALVES * t)
                else:
                    k.wait_filled(eng, ("moe",) + last, short_turns(t))
            eng.wait_ge(k.landed[(first + i) % RAW], 16 * ((first + i) // RAW + 1) + 16 * (ROUND // RAW) * t)
        split(k, eng, round_number(k, i, 0) % SPLIT, (first + i) % RAW, GRANULE, round_number(k, i, t))
        done += 1
    return done


def moe_sync(k, sp):
    k.more = rounds(k, sp, lambda t, expert: load_round(k, sp, t, expert))


def moe_wait_all(k, sp):
    k.wait_released(sp, ("moe", "scatter", 3), short_turns(k.more + N_EXPERTS - 1))


def moe_tensor(k, pe):
    b = moe_buffers(k)
    pe.wait_ge(k.router_landed, 16)
    k.take(pe, "logits")
    for t in range(TILES):
        for c in range(KC):
            for part in (k.hT.high, k.hT.low):
                last = pe.matmul(k.bank("logits")[:, 8 * t:8 * t + 8], part[:, c, P * t:P * (t + 1)].bitcast(F32), k.router[:, c, :],
                                 start=(c == 0 and part is k.hT.high), stop=(c == KC - 1 and part is k.hT.low))
    k.fill(last, "logits")
    pe.wait_ge(k.routed, 1)
    k.take(pe, "places")
    bank, (chosen0, chosen1) = k.bank("places"), (k.chosen[:, 0, :], k.chosen[:, 1, :])
    pe.matmul(bank[:, 0:8], k.before, chosen0, start=True, stop=True)
    pe.matmul(bank[:, 8:16], k.ones, chosen0, start=True, stop=False)
    pe.matmul(bank[:, 8:16], k.before, chosen1, start=False, stop=True)
    pe.matmul(bank[:, 16:24], k.ones, chosen0, start=True, stop=False)
    k.fill(pe.matmul(bank[:, 16:24], k.ones, chosen1, start=False, stop=True), "places")
    pe.wait_ge(k.placed, 2)
    for i in range(2):
        gather_tensor(k, pe, b, ("moe", "first", i), i, 0)
    for i in range(2):
        k.wait_released(pe, ("moe", "first", i))
    rounds(k, pe, lambda t, _: moe_round_tensor(k, pe, b, t))


def gather_tensor(k, pe, b, name, i, more):
    k.take(pe, name, more)
    for c in range(4 * i, 4 * i + 4):
        for tile in range(TILES):
            last = pe.matmul(k.bank(name)[:, P * (c % 4):P * (c % 4 + 1)], k.h[:, tile, P * c:P * (c + 1)],
                             b.placed[:, tile, :], start=(tile == 0), stop=(tile == TILES - 1))
    k.fill(last, name)


def gather_scalar(k, act, b, name, i, more):
    k.wait_filled(act, name, more)
    for c in range(4 * i, 4 * i + 4):
        last = act.activation(b.tokens.high[:, c, :], k.bank(name)[:, P * (c % 4):P * (c % 4 + 1)], ACT.Copy,
                              scale=k.column("norm_ffn_2", c, 1))
    last.then_inc(k.part_ready, 1)


def gather_vector(k, v, b, name, i, more, more_parts):
    k.wait_filled(v, name, more)
    k.wait_part(v, name, more_parts)
    for c in range(4 * i, 4 * i + 4):
        last = v.scalar_tensor_tensor(b.tokens.low[:, c, :], k.bank(name)[:, P * (c % 4):P * (c % 4 + 1)],
                                      k.column("norm_ffn_2", c, 1), b.tokens.high[:, c, :].bitcast(F32), ALU.mult, ALU.subtract)
    k.release(last, name)


def moe_round_tensor(k, pe, b, t):
    more = short_turns(t)
    i_granule = 0
    for kind, i in moe_order():
        name = ("moe", kind, i)
        if kind in ("gate", "up"):
            for half in range(2):
                pe.wait_ge(k.low_ready, round_number(k, i_granule, t) + 1)
                if half == 0:
                    k.take(pe, name, more)
                w = round_parts(k, i_granule, 4)
                for c in range(4):
                    at = 4 * half + c
                    last = three_passes(pe, k.bank(name), b.tokens[:, at, :], w[:, c, :], at == 0, at == KC - 1)
                if half == 0:
                    last.then_inc(k.half_done, 1)
                i_granule += 1
            k.fill(last, name)
        if kind == "unplace":
            k.take(pe, name, more)
            for tile in range(TILES):
                last = pe.transpose(k.bank(name)[:, P * tile:P * (tile + 1)], b.placed[:, tile, :], k.ident)
            k.fill(last, name)
        if kind == "turn":
            k.wait_released(pe, ("moe", "up", i), more)
            k.take(pe, name, more)
            for c in range(4):
                last = pe.transpose(k.bank(name)[:, P * c:P * (c + 1)], b.hidden[:, i % 2, P * c:P * (c + 1)], k.ident)
            k.fill(last, name)
        if kind == "gather":
            if i == 0:
                pe.wait_ge(k.placed, 2 * t + 4)
            gather_tensor(k, pe, b, name, i, more)
        if kind == "down":
            k.wait_released(pe, ("moe", "turn", i), more)
            for half in range(2):
                start, stop = i == 0 and half == 0, i == FF_STEPS - 1 and half == 1
                pe.wait_ge(k.low_ready, round_number(k, i_granule, t) + 1)
                w = round_parts(k, i_granule, 2)
                for n in range(2):
                    out = ("moe", "expert", n)
                    if start:
                        k.take(pe, out, t)
                    for c in range(2):
                        at = P * (2 * half + c)
                        last = three_passes(pe, k.bank(out), b.hiddenT[:, i % 2, at:at + P], w[:, c, 512 * n:512 * (n + 1)],
                                            start and c == 0, stop and c == 1)
                    if stop:
                        k.fill(last, out)
                if not stop:
                    last.then_inc(k.half_done, 1)
                i_granule += 1
        if kind == "scatter":
            half, tile = i // 2, i % 2
            if i == 0:
                k.wait_released(pe, ("moe", "unplace", 0), more)
                for g in range(2):
                    k.wait_released(pe, ("moe", "gather", g), more)
            k.wait_released(pe, ("moe", "expert", half), t)
            k.take(pe, name, more)
            k.fill(pe.matmul(k.bank(name), b.unplaced[:, tile, :], b.out[:, 512 * half:512 * (half + 1)], start=True, stop=True), name)


def round_parts(k, i, c):
    slot = round_number(k, i, 0) % SPLIT
    parts = Parts(k.high[:, slot, :], k.low[:, slot, :])
    return parts.rearrange("p (c n) -> p c n", c=c)


def moe_scalar(k, act):
    b = moe_buffers(k)
    act.wait_ge(k.gap_ready, 1)
    act.activation(k.both, k.gap, ACT.Exp).then_inc(k.share_ready, 1)
    for i in range(2):
        gather_scalar(k, act, b, ("moe", "first", i), i, 0)

    def one_round(t, _):
        more = short_turns(t)
        done = 0
        for index, (kind, i) in enumerate(moe_order()):
            name = ("moe", kind, i)
            done = split_round(k, act, done, index, t)
            if kind == "gate":
                if i >= 2:
                    k.wait_released(act, ("moe", "up", i - 2), more)
                k.wait_filled(act, name, more)
                k.release(act.activation(b.silu[:, i % 2, :], k.bank(name), ACT.Silu), name)
            if kind == "turn":
                k.wait_filled(act, name, more)
                act.activation(b.hiddenT.high[:, i % 2, :], k.bank(name), ACT.Copy).then_inc(k.part_ready, 1)
            if kind == "gather":
                gather_scalar(k, act, b, name, i, more)
        k.wait_filled(act, ("moe", "expert", 0), t)
        k.release(act.activation(b.out[:, 0:512], k.bank(("moe", "expert", 0)), ACT.Copy), ("moe", "expert", 0))
        k.wait_filled(act, ("moe", "expert", 1), t)

    rounds(k, act, one_round)


def moe_vector(k, v):
    b = moe_buffers(k)
    steps = k.engine_steps["dve"]
    k.wait_filled(v, "logits")
    k.release(v.tensor_copy(k.logits, k.bank("logits")[:, 0:TILES * 8]), "logits")
    k.wait_released(v, "logits")
    for t in range(TILES):
        logits, ordered = k.logits[:, 8 * t:8 * t + 8], k.sorted[:, 8 * t:8 * t + 8]
        steps.link(v.max(ordered, logits))
        steps.link(v.max_index(k.best[:, t, :], ordered, logits))
        steps.link(v.tensor_copy(k.first[:, 2 * t:2 * t + 2], k.best[:, t, 0:2]))
        steps.link(v.tensor_tensor(k.gap[:, t:t + 1], ordered[:, 1:2], ordered[:, 0:1], ALU.subtract))
    v.sem_inc(k.gap_ready, 1)
    v.wait_ge(k.share_ready, 1)
    one_hot, other = k.over[:, 0:8], k.over[:, 8:16]
    for t in range(TILES):
        share = k.share[:, 2 * t:2 * t + 2]
        steps.link(v.tensor_scalar(share[:, 0:1], k.both[:, t:t + 1], 1.0, None, ALU.add))
        steps.link(v.reciprocal(share[:, 0:1], share[:, 0:1]))
        steps.link(v.tensor_tensor(share[:, 1:2], share[:, 0:1], k.both[:, t:t + 1], ALU.mult))
        experts = k.count[:, 0:8]
        steps.link(v.tensor_scalar(one_hot, experts, k.first[:, 2 * t:2 * t + 1], None, ALU.is_equal))
        steps.link(v.tensor_scalar(other, experts, k.first[:, 2 * t + 1:2 * t + 2], None, ALU.is_equal))
        steps.link(v.tensor_tensor(k.chosen[:, t, :], one_hot, other, ALU.add))
        steps.link(v.tensor_scalar(one_hot, one_hot, share[:, 0:1], None, ALU.mult))
        steps.link(v.scalar_tensor_tensor(k.weight[:, t, :], other, share[:, 1:2], one_hot, ALU.mult, ALU.add))
    v.sem_inc(k.routed, 1)
    k.wait_filled(v, "places")
    bank = k.bank("places")
    for t in range(TILES):
        steps.link(v.scalar_tensor_tensor(k.place[:, 0, t, :], bank[:, 8 * t:8 * t + 8], 1.0, k.chosen[:, t, :], ALU.add, ALU.mult))
        steps.link(v.tensor_scalar(k.place[:, 0, t, :], k.place[:, 0, t, :], -1.0, None, ALU.add))
        steps.link(v.tensor_scalar(k.place[:, 1, t, :], k.place[:, 0, t, :], -CAP, None, ALU.add))

    def put(expert, second):
        for tile in range(TILES):
            column = k.place[:, second, tile, expert:expert + 1] if isinstance(expert, int) else \
                k.place[:, second, tile, bass.ds(expert, 1)]
            v.tensor_scalar(b.placed[:, tile, :], k.count, column, None, ALU.is_equal).then_inc(k.placed, 1)

    put(0, 0)
    over, upto, match = k.over[:, 0:8], k.over[:, 8:16], k.over[:, 16:24]
    listed = k.over[:, 24:24 + N_WORK]
    steps.link(v.tensor_scalar(over, bank[:, 16:24], CAP, None, ALU.is_gt))
    v.sem_inc(k.freed[k.banks.at["places"][0]], 1)
    steps.link(v.memset(listed[:, N_WORK - 1:N_WORK], 0.0))
    steps.link(v.tensor_tensor_scan(upto, k.ones[:, 0:8], over, 0.0, ALU.mult, ALU.add))
    steps.link(v.tensor_copy(listed[:, 0:1], upto[:, 7:8]))
    for r in range(N_EXPERTS):
        steps.link(v.scalar_tensor_tensor(match, upto, float(r + 1), over, ALU.is_equal, ALU.mult))
        steps.link(v.tensor_tensor_reduce(match, match, k.count[:, 0:8], 1.0, 0.0, ALU.mult, ALU.add, listed[:, r + 1:r + 2]))
    v.tensor_copy(k.work[:, 0:N_WORK], listed).then_inc(k.work_ready, 1)
    for i in range(2):
        gather_vector(k, v, b, ("moe", "first", i), i, 0, 0)

    def one_round(t, expert, next_expert, next_second):
        more, more_parts = short_turns(t), MOE_PARTS * t
        done = 0
        for index, (kind, i) in enumerate(moe_order()):
            name = ("moe", kind, i)
            done = split_round(k, v, done, index, t)
            if kind == "up":
                k.wait_filled(v, name, more)
                k.wait_released(v, ("moe", "gate", i), more)
                if i >= 2:
                    k.wait_filled(v, ("moe", "turn", i - 2), more)
                k.release(v.tensor_tensor(b.hidden[:, i % 2, :], k.bank(name), b.silu[:, i % 2, :], ALU.mult), name)
            if kind == "unplace":
                k.wait_filled(v, name, more)
                k.release(v.tensor_copy(b.unplaced[:, :, :], k.bank(name)[:, 0:TILES * P].rearrange("p (t q) -> p t q", t=TILES)), name)
                put(next_expert, next_second)
            if kind == "turn":
                k.wait_part(v, name, more_parts)
                k.release(v.tensor_tensor(b.hiddenT.low[:, i % 2, :], k.bank(name), b.hiddenT.high[:, i % 2, :].bitcast(F32),
                                          ALU.subtract), name)
            if kind == "gather":
                gather_vector(k, v, b, name, i, more, more_parts)
            if kind == "scatter":
                if i == 0:
                    k.wait_filled(v, ("moe", "expert", 1), t)
                    k.release(v.tensor_copy(b.out[:, 512:1024], k.bank(("moe", "expert", 1))), ("moe", "expert", 1))
                half, tile = i // 2, i % 2
                k.wait_filled(v, name, more)
                part = k.x[:, tile, 512 * half:512 * (half + 1)]
                weight = k.weight[:, tile, expert:expert + 1] if isinstance(expert, int) else k.weight[:, tile, bass.ds(expert, 1)]
                k.release(v.scalar_tensor_tensor(part, k.bank(name), weight, part, ALU.mult, ALU.add), name)

    with v.Fori(0, N_EXPERTS - 1) as t:
        one_round(t, t, t + 1, 0)
    v.wait_ge(k.work_ready, 1)
    one_round(N_EXPERTS - 1, N_EXPERTS - 1, table_entry(k, v, 1), 1)
    more_rounds(k, v, lambda t, r: one_round(t, table_entry(k, v, r + 1), table_entry(k, v, r + 2), 1))


LAYERS = ("a0", "b", "c", "a1", "h", "ffn", "r", "moe")


def build(nc, w, consts, const_at, out, layers=LAYERS):
    with ExitStack() as ctx:
        k = Core(nc, ctx, w, consts, const_at, out)
        block = ctx.enter_context(nc.Block())

        @block.sync
        def _(sp):
            sync_weights(k, sp)
            if "moe" in layers:
                moe_sync(k, sp)
            store(k, sp, layers)

        @block.tensor
        def _(pe):
            setup_tensor(k, pe)
            for n, layer in enumerate(layers):
                norm_tensor(k, pe, n)
                if layer[0] == "a":
                    a_tensor(k, pe, int(layer[1]))
                else:
                    {"b": b_tensor, "c": c_tensor, "h": h_tensor, "ffn": ffn_tensor, "r": r_tensor, "moe": moe_tensor}[layer](k, pe)

        @block.vector
        def _(v):
            k.engine_steps["dve"] = Steps(v, k.own["dve"])
            setup_vector(k, v)
            x_from = []
            for n, layer in enumerate(layers):
                norm_vector(k, v, n, x_from)
                if n == 0:
                    setup_lambdas(k, v)
                if layer[0] == "a":
                    a_vector(k, v, int(layer[1]))
                else:
                    {"b": b_vector, "c": c_vector, "h": h_vector, "ffn": ffn_vector, "r": r_vector, "moe": moe_vector}[layer](k, v)
                x_from = out_names(layer)

        @block.scalar
        def _(act):
            k.engine_steps["act"] = Steps(act, k.own["act"])
            setup_loads(k, act)
            x_from = []
            for n, layer in enumerate(layers):
                norm_scalar(k, act, n, x_from)
                if n == 0:
                    setup_scalar(k, act)
                if layer[0] == "a":
                    a_scalar(k, act, int(layer[1]))
                else:
                    {"b": b_scalar, "c": c_scalar, "h": h_scalar, "ffn": ffn_scalar, "r": r_scalar, "moe": moe_scalar}[layer](k, act)
                x_from = out_names(layer)

        @block.gpsimd
        def _(pool):
            k.engine_steps["pool"] = Steps(pool, k.own["pool"])
            for n, layer in enumerate(layers):
                if n == 0:
                    pool.wait_ge(k.const_landed, 16)
                norm_pool(k, pool, n)
                if layer[0] == "a":
                    a_pool(k, pool, int(layer[1]))
                elif layer in ("c", "h"):
                    {"c": c_pool, "h": h_pool}[layer](k, pool)


def store(k, sp, layers):
    if layers[-1] == "moe":
        moe_wait_all(k, sp)
    else:
        for name in out_names(layers[-1]):
            k.wait_released(sp, name)
    sp.dma_start(k.out[0].rearrange("(t p) d -> p t d", p=P), k.x[:, :, :]).then_inc(k.stored, 16)
    sp.wait_ge(k.stored, 16)


INPUTS = tuple(VECTOR_ROWS) + tuple(SPREAD) + (
    "x", "a_w_in", "a_w_out", "b_w_in", "b_w_out", "c_w_in", "c_w_uq", "c_w_ukv", "c_w_out", "hy_w_in_2", "hy_w_out_2",
    "rg_w_in_2", "rg_gate_a_w_2", "rg_gate_x_w_2", "rg_w_out_2", "ffn_w_gate_2", "ffn_w_up_2", "ffn_w_down_2",
    "moe_router_2", "moe_w_gate_2", "moe_w_up_2", "moe_w_down_2",
)


def kernel(**inputs):
    import concourse.bacc as bacc
    from concourse.bass_utils import run_bass_kernel_spmd

    nc = bacc.Bacc("TRN2", target_bir_lowering=False, num_devices=1)
    arrays, w = {}, {}
    for name in INPUTS:
        a = np.ascontiguousarray(inputs[name])
        arrays[f"in_{name}"] = a
        w[name] = nc.dram_tensor(f"in_{name}", a.shape, mybir.dt.from_np(a.dtype), kind="ExternalInput").ap()
    consts, const_at = constants()
    arrays["in_constants"] = consts
    const_ap = nc.dram_tensor("in_constants", consts.shape, F32, kind="ExternalInput").ap()
    out = nc.dram_tensor("out_x", (1, SEQ, D), F32, kind="ExternalOutput").ap()
    build(nc, w, const_ap, const_at, out)
    results = run_bass_kernel_spmd(nc, [arrays], core_ids=[0])
    return results.results[0]["out_x"]
```
